# Optimizing a Trainium2 kernel written in Bass

```python
import math
import jax, jax.numpy as jnp
from jax import lax
import numpy as np

D_MODEL = 1024
BATCH = 1
SEQ = 1024
DEPTH = 1

MIX_WIDTH = D_MODEL
ATT_WIDTH = MIX_WIDTH // 2
SGU_WIDTH = MIX_WIDTH - ATT_WIDTH
DIFF_HEADS = 4
DIFF_HEAD_DIM = ATT_WIDTH // DIFF_HEADS // 2
DIFF_VALUE_DIM = 2 * DIFF_HEAD_DIM
ROPE_DIM = DIFF_HEAD_DIM // 4
ROPE_THETA = 500000.0
QBLOCK = 128
SGU_GROUPS = 4
SGU_GROUP_WIDTH = SGU_WIDTH // SGU_GROUPS
CHUNK = 128
Q_COLS = DIFF_HEADS * 2 * DIFF_HEAD_DIM
K_COLS = DIFF_HEADS * 2 * DIFF_HEAD_DIM
V_COLS = DIFF_HEADS * DIFF_VALUE_DIM
IN_COLS = Q_COLS + K_COLS + V_COLS + 2 * SGU_WIDTH
N_GROUPS = 4
EXPERTS_PER_GROUP = 8
N_EXPERTS = N_GROUPS * EXPERTS_PER_GROUP
TOP_K_IN_GROUP = 2
D_FF_EXPERT = D_MODEL // 2
RMS_EPS = 1e-6
NEG_INF = -1e30

kernel_name = "hymba_diffattn_sgu_hmoe_layer"

def rms_norm(x, g):
    xf = x.astype(jnp.float32)
    y = xf * lax.rsqrt(jnp.mean(xf * xf, axis=-1, keepdims=True) + RMS_EPS)
    return (y * g.astype(jnp.float32)).astype(x.dtype)

def layer_norm(x, g, b):
    xf = x.astype(jnp.float32)
    mu = jnp.mean(xf, axis=-1, keepdims=True)
    xc = xf - mu
    y = xc * lax.rsqrt(jnp.mean(xc * xc, axis=-1, keepdims=True) + RMS_EPS)
    return (y * g.astype(jnp.float32) + b.astype(jnp.float32)).astype(x.dtype)

def rope_tables(positions):
    inv_freq = ROPE_THETA ** (-jnp.arange(0, ROPE_DIM, 2, dtype=jnp.float32) / ROPE_DIM)
    ang = positions.astype(jnp.float32)[..., None] * inv_freq
    return jnp.cos(ang), jnp.sin(ang)

def apply_partial_rope(x, cos, sin):
    half = ROPE_DIM // 2
    c = cos[:, :, None, None, :]
    s = sin[:, :, None, None, :]
    x1 = x[..., :half].astype(jnp.float32)
    x2 = x[..., half:ROPE_DIM].astype(jnp.float32)
    r1 = (x1 * c - x2 * s).astype(x.dtype)
    r2 = (x1 * s + x2 * c).astype(x.dtype)
    return jnp.concatenate([r1, r2, x[..., ROPE_DIM:]], axis=-1)

def diff_attention(q, k, v, lam):
    B, S, H, _, d = q.shape
    nb = S // QBLOCK
    kt = k.transpose(0, 2, 3, 1, 4)
    vt = v.transpose(0, 2, 1, 3)
    qb = q.transpose(0, 2, 3, 1, 4).reshape(B, H, 2, nb, QBLOCK, d).transpose(3, 0, 1, 2, 4, 5)
    key_pos = jnp.arange(S)

    def block(args):
        q_blk, i = args
        s = jnp.einsum('bhmqd,bhmkd->bhmqk', q_blk, kt, preferred_element_type=jnp.float32)
        q_pos = i * QBLOCK + jnp.arange(QBLOCK)
        mask = key_pos[None, :] <= q_pos[:, None]
        s = jnp.where(mask, s, NEG_INF)
        p = jax.nn.softmax(s, axis=-1)
        a = p[:, :, 0] - lam * p[:, :, 1]
        return jnp.einsum('bhqk,bhkv->bhqv', a.astype(vt.dtype), vt)

    out = lax.map(block, (qb, jnp.arange(nb)))
    return out.transpose(1, 0, 3, 2, 4).reshape(B, S, H, DIFF_VALUE_DIM)

def spatial_gating(u, v, ln_g, ln_b, w_s, b_s):
    B, S, _ = v.shape
    nc = S // CHUNK
    vn = layer_norm(v, ln_g, ln_b)
    vc = vn.reshape(B, nc, CHUNK, SGU_GROUPS, SGU_GROUP_WIDTH)
    w = w_s * jnp.tril(jnp.ones((CHUNK, CHUNK), dtype=w_s.dtype))
    s = jnp.einsum('gts,bcsgd->bctgd', w, vc) + b_s.T[None, None, :, :, None]
    return u * s.reshape(B, S, SGU_WIDTH)

def hier_moe(h, wg, bg, we, be, w_gate, w_up, w_down):
    B, S, D = h.shape
    T = B * S
    xt = h.reshape(T, D)
    g_logits = (xt @ wg).astype(jnp.float32) + bg.astype(jnp.float32)
    g_probs = jax.nn.softmax(g_logits, axis=-1)
    p_grp, grp = lax.top_k(g_probs, 1)
    e_logits = ((xt @ we).astype(jnp.float32) + be.astype(jnp.float32)).reshape(T, N_GROUPS, EXPERTS_PER_GROUP)
    e_logits = jnp.take_along_axis(e_logits, grp[:, :, None], axis=1)[:, 0]
    top_logit, top_e = lax.top_k(e_logits, TOP_K_IN_GROUP)
    gates = p_grp * jax.nn.softmax(top_logit, axis=-1)
    flat_id = (grp * EXPERTS_PER_GROUP + top_e).reshape(-1)
    order = jnp.argsort(flat_id)
    tok = order // TOP_K_IN_GROUP
    xs = xt[tok]
    sizes = jnp.bincount(flat_id, length=N_EXPERTS).astype(jnp.int32)
    hg = lax.ragged_dot(xs, w_gate, sizes)
    hu = lax.ragged_dot(xs, w_up, sizes)
    ys = lax.ragged_dot(jax.nn.silu(hg) * hu, w_down, sizes)
    ys = ys * gates.reshape(-1)[order][:, None].astype(ys.dtype)
    out = jnp.zeros((T, D), dtype=ys.dtype).at[tok].add(ys)
    return out.reshape(B, S, D)

def setup_inputs(seed: int = 0) -> dict:
    key = jax.random.key(seed)
    ks = jax.random.split(key, 24)
    f32 = jnp.float32
    L = DEPTH

    def nrm(k, shape, scale):
        return jax.random.normal(k, shape, f32) * scale

    x = jax.random.normal(ks[0], (BATCH, SEQ, D_MODEL), f32)
    offset = jax.random.randint(ks[1], (BATCH, 1), 0, 4096, dtype=jnp.int32)
    positions = (offset + jnp.arange(SEQ, dtype=jnp.int32)[None, :]).astype(jnp.int32)
    return {
        "x": x,
        "positions": positions,
        "norm_mix_g": 1.0 + nrm(ks[2], (L, D_MODEL), 0.02),
        "w_in": nrm(ks[3], (L, D_MODEL, IN_COLS), D_MODEL ** -0.5),
        "q_norm_g": 1.0 + nrm(ks[4], (L, DIFF_HEAD_DIM), 0.02),
        "k_norm_g": 1.0 + nrm(ks[5], (L, DIFF_HEAD_DIM), 0.02),
        "lambda_q1": nrm(ks[6], (L, DIFF_HEAD_DIM), 0.1),
        "lambda_k1": nrm(ks[7], (L, DIFF_HEAD_DIM), 0.1),
        "lambda_q2": nrm(ks[8], (L, DIFF_HEAD_DIM), 0.1),
        "lambda_k2": nrm(ks[9], (L, DIFF_HEAD_DIM), 0.1),
        "diff_out_norm_g": 1.0 + nrm(ks[10], (L, DIFF_VALUE_DIM), 0.02),
        "sgu_ln_g": 1.0 + nrm(ks[11], (L, SGU_WIDTH), 0.02),
        "sgu_ln_b": nrm(ks[12], (L, SGU_WIDTH), 0.02),
        "sgu_w": nrm(ks[13], (L, SGU_GROUPS, CHUNK, CHUNK), 0.5 * CHUNK ** -0.5),
        "sgu_b": 1.0 + nrm(ks[14], (L, SGU_GROUPS, CHUNK), 0.01),
        "sgu_out_norm_g": 1.0 + nrm(ks[15], (L, SGU_GROUPS, SGU_GROUP_WIDTH), 0.02),
        "w_out": nrm(ks[16], (L, MIX_WIDTH, D_MODEL), MIX_WIDTH ** -0.5),
        "norm_ffn_g": 1.0 + nrm(ks[17], (L, D_MODEL), 0.02),
        "router_group_w": nrm(ks[18], (L, D_MODEL, N_GROUPS), D_MODEL ** -0.5),
        "router_group_b": nrm(ks[19], (L, N_GROUPS), 0.01),
        "router_expert_w": nrm(ks[20], (L, D_MODEL, N_EXPERTS), D_MODEL ** -0.5),
        "router_expert_b": nrm(ks[21], (L, N_EXPERTS), 0.01),
        "expert_w_gate": nrm(ks[22], (L, N_EXPERTS, D_MODEL, D_FF_EXPERT), D_MODEL ** -0.5),
        "expert_w_up": nrm(jax.random.fold_in(ks[22], 1), (L, N_EXPERTS, D_MODEL, D_FF_EXPERT), D_MODEL ** -0.5),
        "expert_w_down": nrm(ks[23], (L, N_EXPERTS, D_FF_EXPERT, D_MODEL), D_FF_EXPERT ** -0.5),
    }

def reference(x, positions, norm_mix_g, w_in, q_norm_g, k_norm_g, lambda_q1, lambda_k1,
              lambda_q2, lambda_k2, diff_out_norm_g, sgu_ln_g, sgu_ln_b, sgu_w, sgu_b,
              sgu_out_norm_g, w_out, norm_ffn_g, router_group_w, router_group_b,
              router_expert_w, router_expert_b, expert_w_gate, expert_w_up, expert_w_down):
    B, S, _ = x.shape
    cos, sin = rope_tables(positions)
    scale = DIFF_HEAD_DIM ** -0.5
    h = x
    for l in range(DEPTH):
        lambda_init = 0.8 - 0.6 * math.exp(-0.3 * l)
        hn = rms_norm(h, norm_mix_g[l])
        proj = hn @ w_in[l]
        q, k, v, su, sv = jnp.split(
            proj, [Q_COLS, Q_COLS + K_COLS, Q_COLS + K_COLS + V_COLS, Q_COLS + K_COLS + V_COLS + SGU_WIDTH], axis=-1)
        q = q.reshape(B, S, DIFF_HEADS, 2, DIFF_HEAD_DIM)
        k = k.reshape(B, S, DIFF_HEADS, 2, DIFF_HEAD_DIM)
        v = v.reshape(B, S, DIFF_HEADS, DIFF_VALUE_DIM)
        q = apply_partial_rope(rms_norm(q, q_norm_g[l]), cos, sin) * scale
        k = apply_partial_rope(rms_norm(k, k_norm_g[l]), cos, sin)
        lam = (jnp.exp(jnp.sum(lambda_q1[l].astype(jnp.float32) * lambda_k1[l].astype(jnp.float32)))
               - jnp.exp(jnp.sum(lambda_q2[l].astype(jnp.float32) * lambda_k2[l].astype(jnp.float32)))
               + lambda_init)
        att = diff_attention(q, k, v, lam)
        att = rms_norm(att, diff_out_norm_g[l]) * (1.0 - lambda_init)
        att = att.reshape(B, S, ATT_WIDTH)
        su = jax.nn.gelu(su, approximate=False)
        sv = jax.nn.gelu(sv, approximate=False)
        sg = spatial_gating(su, sv, sgu_ln_g[l], sgu_ln_b[l], sgu_w[l], sgu_b[l])
        sg = rms_norm(sg.reshape(B, S, SGU_GROUPS, SGU_GROUP_WIDTH), sgu_out_norm_g[l]).reshape(B, S, SGU_WIDTH)
        mix = jnp.concatenate([att, sg], axis=-1)
        h = h + mix @ w_out[l]
        hn = rms_norm(h, norm_ffn_g[l])
        h = h + hier_moe(hn, router_group_w[l], router_group_b[l], router_expert_w[l], router_expert_b[l],
                         expert_w_gate[l], expert_w_up[l], expert_w_down[l])
    return h


_drawn_inputs = setup_inputs


def setup_inputs(seed=0):
    import zlib

    import numpy as np

    out = dict(_drawn_inputs(seed))
    spreads = {}
    factors = {'q_norm_g': 3.97,
     'k_norm_g': 3.273,
     'lambda_q1': 3.238,
     'lambda_k2': 6.891,
     'diff_out_norm_g': 10.377,
     'sgu_ln_g': 113.301,
     'sgu_ln_b': 145.698,
     'sgu_b': 200.0,
     'sgu_out_norm_g': 9.292,
     'router_group_b': 25.046,
     'router_expert_b': 24.66,
     'norm_ffn_g': 5.072}
    for name, (base, spread) in spreads.items():
        noise = np.random.default_rng([zlib.crc32(name.encode()), seed]).standard_normal(out[name].shape)
        drawn = base * np.exp(spread * noise) if base else spread * noise
        out[name] = __import__('jax').numpy.asarray(drawn.astype(out[name].dtype))
    for name, factor in factors.items():
        out[name] = (out[name] * factor).astype(out[name].dtype)
    return out
```

```python
from contextlib import ExitStack

import numpy as np

import concourse.bass as bass
from concourse import mybir

ALU = mybir.AluOpType
ACT = mybir.ActivationFunctionType
AX = mybir.AxisListType
F32 = mybir.dt.float32
F32R = mybir.dt.float32r
BF16 = mybir.dt.bfloat16
I32 = mybir.dt.int32

P = 128
BANK = 512
KB = 1024

D = 1024
SEQ = 1024
T = SEQ // P
KD = D // P
H = 4
DH = 64
QK = 2 * H
ROPE = DH // 4
HALF = ROPE // 2
THETA = 500000.0
G = 4
WB = 512
NB_IN, NB_OUT = 5, 2
EPS = 1e-6
LAMBDA_INIT = 0.2
NEG = -1e30

NG, EG = 4, 8
NE = NG * EG
F = 512
OVER = 2 * SEQ // P - 1
NT = NE + OVER + 1
NTHR = SEQ // P - 1
EMPTY = 1 << 20

SV, SU, Q, K, V = range(5)
COLUMN = {Q: 0, K: 1, V: 2, SU: 3, SV: 4}
STEPS_IN = NB_IN * KD
STEPS = STEPS_IN + NB_OUT * KD
RAW, RING = 8, 4


def build(nc, x, positions, norm_mix_g, w_in, q_norm_g, k_norm_g, lambda_q1, lambda_k1, lambda_q2,
          lambda_k2, diff_out_norm_g, sgu_ln_g, sgu_ln_b, sgu_w, sgu_b, sgu_out_norm_g, w_out,
          norm_ffn_g, router_group_w, router_group_b, router_expert_w, router_expert_b,
          expert_w_gate, expert_w_up, expert_w_down, out):
    ctx = ExitStack()
    with ctx:
        hn2_dram = nc.dram_tensor("hn2_rows", [SEQ, D], F32).ap()
        y_dram = nc.dram_tensor("expert_rows", [2 * SEQ, D], F32).ap()
        table_dram = nc.dram_tensor("slot_table", [P * NT, 2], I32).ap()

        base = -(-nc.sbuf_base // 64) * 64
        A = base + 31 * KB
        B = A + 64 * KB
        C = B + 80 * KB
        at_const = [base]

        def place(name, shape, dt, offset):
            return nc.alloc_sbuf_tensor_at(name, shape, dt, offset=offset)

        def const(name, shape, dt):
            size = int(np.prod(shape[1:])) * (2 if dt == BF16 else 4)
            t = place(name, shape, dt, at_const[0])
            at_const[0] += -(-size // 32) * 32
            assert at_const[0] <= A, name
            return t

        ident = const("ident", [P, P], F32)
        identb = const("identb", [P, P], BF16)
        causal = const("causal", [P, P], BF16)
        earlier = const("earlier", [P, P], BF16)
        onesb = const("onesb", [P, P], BF16)
        gmix = const("gmix", [P, D], F32)
        gffn = const("gffn", [P, D], F32)
        lng = const("lng", [P, WB], F32)
        lnb = const("lnb", [P, WB], F32)
        gsgu = const("gsgu", [P, WB], F32)
        gatt = const("gatt", [P, P], F32)
        gq = const("gq", [P, DH], F32)
        gk = const("gk", [P, DH], F32)
        lam4 = const("lam4", [P, 4, DH], F32)
        lam = const("lam", [P, 8], F32)
        wsT = const("wsT", [P, G, P], F32)
        bs = const("bs", [P, G], F32)
        router = const("router", [P, KD, NG + NE], F32)
        rbias = const("rbias", [P, NG + NE], F32)
        posi = const("posi", [P, T], I32)
        posf = const("posf", [P, T], F32)
        ang = const("ang", [P, 4, T, HALF], F32)
        cs = const("cs", [P, T, HALF], F32)
        sn = const("sn", [P, T, HALF], F32)
        ss = const("ss", [P, T], F32)
        rs = const("rs", [P, T], F32)
        ss2 = const("ss2", [P, T], F32)
        rs2 = const("rs2", [P, T], F32)
        stat = const("stat", [P, 6], F32)
        mv = const("mv", [P, T, 2], F32)
        lnr = const("lnr", [P, 2], F32)
        half = const("half", [P, QK], F32)
        sums = const("sums", [P, 2, QK], F32)
        inv = const("inv", [P, 2, QK], F32)
        sq = const("sq", [P, 2, WB], F32)
        rp = const("rp", [P, 4, QK, HALF], F32)
        nmax = const("nmax", [P, 2 * H * T], F32)
        lsum = const("lsum", [P, H * T, 2], F32)
        linv = const("linv", [P, H * T, 2], F32)
        mixc = const("mixc", [P, H * T], F32)

        hn_hi = place("hn_hi", [P, KD, SEQ], F32R, A)
        hn_lo = place("hn_lo", [P, KD, SEQ], F32R, A + 32 * KB)
        qT = place("qT", [P, H, SEQ], F32, A)
        kT = place("kT", [P, H, SEQ], F32, A + 16 * KB)
        att = place("att", [P, T, WB], F32, A + 32 * KB)
        prob = place("prob", [P, 2, 2, SEQ], F32, A + 48 * KB)
        h = place("h", [P, T, D], F32, A)
        hn2 = place("hn2", [P, 2, D], F32, A + 48 * KB)
        sq2 = place("sq2", [P, D], F32, A + 56 * KB)
        hnT2 = place("hnT2", [P, KD, P], F32, A + 32 * KB)
        actT = place("actT", [P, F // P, P], F32, A + 36 * KB)

        q = place("q", [P, T, WB], F32, B)
        k = place("k", [P, T, WB], F32, B + 16 * KB)
        v = place("v", [P, T, WB], F32, B + 32 * KB)
        sv = place("sv", [P, T, WB], F32, B + 48 * KB)
        su = place("su", [P, T, WB], F32, B + 64 * KB)
        xin = place("xin", [P, 4, D], F32, B)
        xs = place("xs", [P, 2, D], F32, B + 16 * KB)
        sq1 = place("sq1", [P, D], F32, B + 24 * KB)
        wsm = place("wsm", [P, G, P], F32, B + 32 * KB)
        probT = place("probT", [P, 2, T, P], F32, B + 48 * KB)
        mix_hi = place("mix_hi", [P, KD, SEQ], F32R, B)
        mix_lo = place("mix_lo", [P, KD, SEQ], F32R, B + 32 * KB)

        w_raw = place("w_raw", [P, RAW, WB], F32, C)
        w_hi = place("w_hi", [P, RING, WB], F32R, C + 16 * KB)
        w_lo = place("w_lo", [P, RING, WB], F32R, C + 24 * KB)

        ew = place("ew", [P, 2, 6, 2048], F32, B)
        xg = place("xg", [P, D], F32, C + 16 * KB)
        xT = place("xT", [P, KD, P], F32, C + 20 * KB)
        y = place("y", [P, D], F32, C + 24 * KB)
        gact = place("gact", [P, F], F32, C + 28 * KB)
        hid = place("hid", [P, F], F32, C + 30 * KB)
        yin = place("yin", [P, T, 2, D], F32, B)

        R = A + 38 * KB
        at_r = [R]

        def scratch(name, shape, dt=F32):
            size = int(np.prod(shape[1:])) * (2 if dt == BF16 else 4)
            t = place(name, shape, dt, at_r[0])
            at_r[0] += -(-size // 32) * 32
            assert at_r[0] <= A + 48 * KB, name
            return t

        lg = scratch("lg", [P, T, NG + NE])
        r8 = {n: scratch(n, [P, T]) for n in ("gmax", "gsum", "pgrp", "grank", "m1", "r1", "m2", "r2", "dm", "e2",
                                                "den", "gate1", "gate2", "slot1", "slot2")}
        gd = scratch("gd", [P, T, NG])
        grk = scratch("grk", [P, T, NG])
        gexp = scratch("gexp", [P, T, NG])
        pen = scratch("pen", [P, T, NG])
        revg = scratch("revg", [P, NG])
        reve = scratch("reve", [P, NE])
        ecol = scratch("ecol", [P, NE])
        thr = scratch("thr", [P, NTHR])
        ocol = scratch("ocol", [P, OVER + 1])
        eid = scratch("eid", [P, OVER + 1])
        total = scratch("total", [P, T + 1, NE])
        nover = scratch("nover", [P, NE])
        cum = scratch("cum", [P, NE])
        offs = scratch("offs", [P, NE])
        sloti = scratch("sloti", [P, 2, T], I32)
        pairs = scratch("pairs", [P, 2, T, 2], I32)
        idx1 = scratch("idx1", [P, 1], I32)
        idx2 = scratch("idx2", [P, 1], I32)
        oh1 = scratch("oh1", [P, T, NE])
        oh2 = scratch("oh2", [P, T, NE])
        W0 = C + 16 * KB
        ev = place("ev", [P, T, NE], F32, W0 + 4 * KB)
        rk = place("rk", [P, T, NE], F32, W0 + 5 * KB)
        pos = place("pos", [P, T, NE], F32, W0 + 6 * KB)
        posn = place("posn", [P, T, NE], I32, W0 + 7 * KB)
        qti = place("qti", [P, T, NE], I32, W0 + 8 * KB)
        qt = place("qt", [P, T, NE], F32, W0 + 9 * KB)
        tri = place("tri", [P, NE, NE], F32, W0 + 10 * KB)
        cnt = place("cnt", [P, T, NE], BF16, W0 + 14 * KB)
        cmpt = place("cmpt", [P, NE, NE], F32, A + 60 * KB)
        init = place("init", [P, 2 * NT], I32, W0 + 15 * KB)
        slots = place("slots", [P, NT, 2], I32, A + 56 * KB)
        eidi = place("eidi", [P, 2, OVER + 1], I32, A + 57 * KB)

        PS = [ctx.enter_context(nc.psum_tensor(f"ps{i}", [P, 2 * BANK], F32)) for i in range(4)]

        def bank(i):
            return PS[i // 2][:, BANK * (i % 2):BANK * (i % 2) + BANK]

        def sem(name):
            return ctx.enter_context(nc.semaphore(name))

        gmix_in, small_in, hx_in = sem("gmix_in"), sem("small_in"), sem("hx_in")
        x_in = [sem(f"x_in{i}") for i in range(4)]
        w_in_sem = [sem(f"w_in{i}") for i in range(RAW)]
        dve_step, pool_step = sem("dve_step"), sem("pool_step")
        ws_out = sem("ws_out")
        made, sin_done, lam_exp, ws_masked, ws_turned, rope_arg, lam_dot = (
            sem(n) for n in ("made", "sin_done", "lam_exp", "ws_masked", "ws_turned", "rope_arg", "lam_dot"))
        ss_ready, xs_ready, x_turned, hn_hi_done, hn_lo_done = (
            sem(n) for n in ("ss_ready", "xs_ready", "x_turned", "hn_hi_done", "hn_lo_done"))
        w_hi_done, w_lo_done, w_used, acc_ready, acc_out = (
            sem(n) for n in ("w_hi_done", "w_lo_done", "w_used", "acc_ready", "acc_out"))
        mv_ready, sv_done, sq_done, sums_done, qk_done, consts_done, rs_ready, rs2_ready = (
            sem(n) for n in ("mv_ready", "sv_done", "sq_done", "sums_done", "qk_done", "consts_done", "rs_ready",
                             "rs2_ready"))
        qk_turned, qT_done, kT_done, sg_ready, sg_gated, sg_done = (
            sem(n) for n in ("qk_turned", "qT_done", "kT_done", "sg_ready", "sg_gated", "sg_done"))
        s_ready, max_done, exp_done, a_ready, a_turned, aT_done, o_ready, o_done = (
            sem(n) for n in ("s_ready", "max_done", "exp_done", "a_ready", "a_turned", "aT_done", "o_ready", "o_done"))
        att_done = sem("att_done")
        mix_turned, mix_hi_done, mix_lo_done = sem("mix_turned"), sem("mix_hi_done"), sem("mix_lo_done")
        h_ready, ss2_ready, hn2_ready = sem("h_ready"), sem("ss2_ready"), sem("hn2_ready")
        hn2_out = [sem("hn2_out0"), sem("hn2_out1")]
        h_turned, hT_done, logits, lg_done = sem("h_turned"), sem("hT_done"), sem("logits"), sem("lg_done")
        gd_ready, gexp_done, dm_ready, e2_done, cnt_ready, counted, slots_ready = (
            sem(n) for n in ("gd_ready", "gexp_done", "dm_ready", "e2_done", "cnt_ready", "counted", "slots_ready"))
        table_init, table_out, slots_in = sem("table_init"), sem("table_out"), sem("slots_in")
        eid_ready, rtab, init_ready, zeroed = sem("eid_ready"), sem("rtab"), sem("init_ready"), sem("zeroed")
        ew_in = [[sem(f"ew_in{b}_{c}") for c in range(6)] for b in range(2)]
        rows_in, rows_turned, xTa_done, xTb_done = sem("rows_in"), sem("rows_turned"), sem("xTa_done"), sem("xTb_done")
        chunk_used, silu_done, hid_done, hid_turned, hidT_done = (
            sem(n) for n in ("chunk_used", "silu_done", "hid_done", "hid_turned", "hidT_done"))
        ya_done, yb_done, y_out, idx_first, idx1_set, idx2_set, moe_done = (
            sem(n) for n in ("ya_done", "yb_done", "y_out", "idx_first", "idx1_set", "idx2_set", "moe_done"))
        yin_sem = [sem(f"yin{t}") for t in range(T)]
        h1_done, h2_done, out_done = sem("h1_done"), sem("h2_done"), sem("out_done")

        x_t = x[0].rearrange("(t p) d -> t p d", p=P)
        out_t = out[0].rearrange("(t p) d -> t p d", p=P)
        y_t = y_dram.rearrange("(c t p) d -> t p c d", p=P, t=T)
        w_cols = [COLUMN[j] for j in range(NB_IN)]

        def w_slice(s):
            if s < STEPS_IN:
                c = w_cols[s // KD]
                return w_in[0, (s % KD) * P:(s % KD + 1) * P, c * WB:(c + 1) * WB]
            s -= STEPS_IN
            return w_out[0, (s % KD) * P:(s % KD + 1) * P, s // KD * WB:(s // KD + 1) * WB]

        def expert_chunk(e, c):
            w = (expert_w_gate, expert_w_up, expert_w_down)[c // 2]
            rows = w.shape[2] // 2
            return w[0, bass.ds(e, 1), (c % 2) * rows:(c % 2 + 1) * rows, :].rearrange("o (k p) n -> p (o k) n", p=P)

        def ew_chunk(half, c):
            return ew[:, half, c, :].rearrange("p (k n) -> p k n", n=F if c < 4 else D)

        SMALL = [(lng[:, :], sgu_ln_g.broadcast_to([P, WB])), (lnb[:, :], sgu_ln_b.broadcast_to([P, WB])),
                 (gsgu[:, :], sgu_out_norm_g.rearrange("l g d -> l (g d)").broadcast_to([P, WB])),
                 (gatt[:, :], diff_out_norm_g.broadcast_to([P, P])),
                 (gq[:, :], q_norm_g.broadcast_to([P, DH])), (gk[:, :], k_norm_g.broadcast_to([P, DH])),
                 (lam4[:, 0, :], lambda_q1.broadcast_to([P, DH])), (lam4[:, 1, :], lambda_q2.broadcast_to([P, DH])),
                 (lam4[:, 2, :], lambda_k1.broadcast_to([P, DH])), (lam4[:, 3, :], lambda_k2.broadcast_to([P, DH])),
                 (gffn[:, :], norm_ffn_g.broadcast_to([P, D])),
                 (rbias[:, 0:NG], router_group_b.broadcast_to([P, NG])),
                 (rbias[:, NG:], router_expert_b.broadcast_to([P, NE])),
                 (router[:, :, 0:NG], router_group_w[0].rearrange("(k p) n -> p k n", p=P)),
                 (router[:, :, NG:], router_expert_w[0].rearrange("(k p) n -> p k n", p=P)),
                 (wsm[:, :, :], sgu_w[0].rearrange("g t s -> t g s")),
                 (bs[:, :], sgu_b[0].rearrange("g t -> t g")),
                 (posi[:, :], positions[0].rearrange("(t p) -> p t", p=P))]

        def done_groups(u):
            return sum(-(-(w // H + 1) // 4) for w in range(u + 1))

        block = ctx.enter_context(nc.Block())

        @block.sync
        def _(sp):
            sp.dma_start(gmix[:, :], norm_mix_g.broadcast_to([P, D])).then_inc(gmix_in, 16)
            for t in range(T):
                if t >= 4:
                    sp.wait_ge(xs_ready, t - 3)
                sp.dma_start(xin[:, t % 4, :], x_t[t]).then_inc(x_in[t % 4], 16)
            for s in range(STEPS):
                if s == RAW:
                    for dst, src in SMALL:
                        sp.dma_start(dst, src, allow_slow_non_contiguous=True).then_inc(small_in, 16)
                if s >= RAW:
                    sp.wait_ge(w_lo_done, s - RAW + 1)
                sp.dma_start(w_raw[:, s % RAW, :], w_slice(s)).then_inc(w_in_sem[s % RAW], 16)
                if s == STEPS - 1 - RING:
                    sp.wait_ge(mix_turned, 1)
                    sp.dma_start(h[:, :, :], x[0].rearrange("(t p) d -> p t d", p=P)).then_inc(hx_in, 16)
            sp.wait_ge(w_used, STEPS)
            for e in range(2):
                for c in range(6):
                    sp.dma_start(ew_chunk(e, c), expert_chunk(e, c)).then_inc(ew_in[e][c], 16)
            with sp.Fori(0, NE // 2 - 1) as e2:
                for half in range(2):
                    for c in range(6):
                        sp.wait_ge(chunk_used, 12 * e2 + 6 * half + c + 1)
                        sp.dma_start(ew_chunk(half, c), expert_chunk(2 * e2 + 2 + half, c)).then_inc(ew_in[half][c], 16)
            sp.wait_ge(eid_ready, 2)
            with sp.Fori(0, OVER) as o:
                e = sp.value_load(eidi[0:1, 0, bass.ds(o, 1)], min_val=0, max_val=NE)
                with sp.If(e < NE):
                    weights = sp.value_load(eidi[0:1, 1, bass.ds(o, 1)], min_val=0, max_val=NE - 1)
                    sp.wait_ge(chunk_used, 6 * NE + 6 * o)
                    for c in range(6):
                        sp.dma_start(ew_chunk(0, c), expert_chunk(weights, c)).then_inc(ew_in[0][c], 16)
            sp.wait_ge(moe_done, 1)
            for t in range(T):
                sp.dma_start(yin[:, t, :, :], y_t[t]).then_inc(yin_sem[t], 16)
            for t in range(T):
                sp.wait_ge(h2_done, t + 1)
                sp.dma_start(out_t[t], h[:, t, :]).then_inc(out_done, 16)
            sp.wait_ge(out_done, 16 * T)

        @block.gpsimd
        def _(pool):
            steps = [0]

            def link(ins):
                steps[0] += 1
                ins.then_inc(pool_step, 1)
                pool.wait_ge(pool_step, steps[0])

            pool.memset(onesb[:, :], 1.0).then_inc(made, 1)
            link(pool.memset(ident[:, :], 0.0))
            pool.affine_select(out=ident[:, :], in_=ident[:, :], compare_op=ALU.not_equal, fill=1.0, base=0,
                               pattern=[[-1, P]], channel_multiplier=1).then_inc(made, 1)
            link(pool.memset(identb[:, :], 0.0))
            pool.affine_select(out=identb[:, :], in_=identb[:, :], compare_op=ALU.not_equal, fill=1.0, base=0,
                               pattern=[[-1, P]], channel_multiplier=1).then_inc(made, 1)
            link(pool.memset(causal[:, :], 0.0))
            pool.affine_select(out=causal[:, :], in_=causal[:, :], compare_op=ALU.is_ge, fill=NEG, base=0,
                               pattern=[[-1, P]], channel_multiplier=1).then_inc(made, 1)
            link(pool.memset(earlier[:, :], 1.0))
            pool.affine_select(out=earlier[:, :], in_=earlier[:, :], compare_op=ALU.is_gt, fill=0.0, base=0,
                               pattern=[[1, P]], channel_multiplier=-1).then_inc(made, 1)
            link(pool.memset(half[:, :], -0.5))

            def rstd(dst, src, n):
                link(pool.tensor_scalar(dst, src, 1.0 / n, EPS, ALU.mult, ALU.add))
                return pool.tensor_tensor(dst, dst, half[:, 0:dst.shape[1]], ALU.pow)

            for t in range(T):
                pool.wait_ge(ss_ready, t + 1)
                rstd(rs[:, t:t + 1], ss[:, t:t + 1], D).then_inc(rs_ready, 1)
            pool.wait_ge(small_in, 16 * len(SMALL))
            pool.affine_select(out=wsm[:, :, :], in_=wsm[:, :, :], compare_op=ALU.is_ge, fill=0.0, base=0,
                               pattern=[[0, G], [-1, P]], channel_multiplier=1).then_inc(ws_masked, 1)
            pool.tensor_scalar(gq[:, :], gq[:, :], DH ** -0.5, None, ALU.mult).then_inc(consts_done, 1)
            pool.tensor_scalar(gatt[:, :], gatt[:, :], 1.0 - LAMBDA_INIT, None, ALU.mult).then_inc(consts_done, 1)
            pool.wait_ge(consts_done, 2)

            for t in range(T):
                pool.wait_ge(mv_ready, t + 1)
                link(rstd(lnr[:, 0:1], mv[:, t, 1:2], 1))
                link(pool.tensor_tensor(lnr[:, 1:2], mv[:, t, 0:1], lnr[:, 0:1], ALU.mult))
                link(pool.tensor_scalar(lnr[:, 1:2], lnr[:, 1:2], -1.0, None, ALU.mult))
                link(pool.tensor_scalar(sv[:, t, :], sv[:, t, :], lnr[:, 0:1], lnr[:, 1:2], ALU.mult, ALU.add))
                link(pool.tensor_tensor(sv[:, t, :], sv[:, t, :], lng[:, :], ALU.mult))
                pool.tensor_tensor(sv[:, t, :], sv[:, t, :], lnb[:, :], ALU.add).then_inc(sv_done, 1)

            pool.wait_ge(sin_done, 2)
            normed = [(m, t) for m in (q, k, su, att) for t in range(T)]

            def squares(n):
                m, t = normed[n]
                if m is q or m is k:
                    pool.wait_ge(acc_out, T * (Q + n // T) + t + 1)
                elif m is su:
                    pool.wait_ge(sg_gated, 2 * G if t >= T // 2 else G)
                else:
                    pool.wait_ge(o_done, H * (t + 1))
                pool.tensor_tensor(sq[:, n % 2, :], m[:, t, :], m[:, t, :], ALU.mult).then_inc(sq_done, 1)

            rotated = [0]

            def rotate(mt, t):
                x1, x2 = mt[:, :, 0:HALF], mt[:, :, HALF:ROPE]
                c = cs[:, t, :].unsqueeze(1).broadcast_to([P, QK, HALF])
                s = sn[:, t, :].unsqueeze(1).broadcast_to([P, QK, HALF])
                if rotated[0]:
                    pool.wait_ge(qk_done, 2 * rotated[0])
                rotated[0] += 1
                for i, (a, b) in enumerate(((x1, c), (x2, s), (x1, s), (x2, c))):
                    steps[0] += 1
                    pool.tensor_tensor(rp[:, i], a, b, ALU.mult).then_inc(pool_step, 1)
                pool.wait_ge(pool_step, steps[0])
                pool.tensor_tensor(x1, rp[:, 0], rp[:, 1], ALU.subtract).then_inc(qk_done, 1)
                pool.tensor_tensor(x2, rp[:, 2], rp[:, 3], ALU.add).then_inc(qk_done, 1)

            for n, (m, t) in enumerate(normed):
                if t == 0 or m is att:
                    squares(n)
                if t + 1 < T and m is not att:
                    squares(n + 1)
                width = DH if m is q or m is k else P
                vectors = WB // width
                mt = m[:, t, :].rearrange("p (g d) -> p g d", d=width)
                r = inv[:, n % 2, 0:vectors]
                pool.wait_ge(sums_done, n + 1)
                link(rstd(r, sums[:, n % 2, 0:vectors], width))
                link(pool.tensor_tensor(mt, mt, r.unsqueeze(2).broadcast_to([P, vectors, width]), ALU.mult))
                if m is su:
                    pool.tensor_tensor(su[:, t, :], su[:, t, :], gsgu[:, :], ALU.mult).then_inc(sg_done, 1)
                    continue
                gain = (gq if m is q else gk if m is k else gatt)[:, :].unsqueeze(1).broadcast_to([P, vectors, width])
                ins = pool.tensor_tensor(mt, mt, gain, ALU.mult)
                if m is att:
                    ins.then_inc(att_done, 1)
                else:
                    link(ins)
                    rotate(mt, t)

            for t in range(T):
                pool.wait_ge(ss2_ready, t + 1)
                rstd(rs2[:, t:t + 1], ss2[:, t:t + 1], D).then_inc(rs2_ready, 1)
            pool.wait_ge(w_used, STEPS)
            pool.memset(init[:, :], EMPTY).then_inc(init_ready, 1)
            pool.wait_ge(init_ready, 1)
            pool.dma_start(table_dram.rearrange("(p a) c -> p (a c)", p=P), init[:, :]).then_inc(table_init, 16)
            pool.iota(revg[:, :], pattern=[[-1, NG]], base=NG, channel_multiplier=0,
                      allow_small_or_imprecise_dtypes=True).then_inc(rtab, 1)
            pool.iota(reve[:, :], pattern=[[-1, NE]], base=NE, channel_multiplier=0,
                      allow_small_or_imprecise_dtypes=True).then_inc(rtab, 1)
            pool.iota(ecol[:, :], pattern=[[1, NE]], base=0, channel_multiplier=0,
                      allow_small_or_imprecise_dtypes=True).then_inc(rtab, 1)
            pool.iota(thr[:, :], pattern=[[P, NTHR]], base=P, channel_multiplier=0,
                      allow_small_or_imprecise_dtypes=True).then_inc(rtab, 1)
            pool.iota(ocol[:, :], pattern=[[1, OVER + 1]], base=0, channel_multiplier=0,
                      allow_small_or_imprecise_dtypes=True).then_inc(rtab, 1)
            pool.iota(pairs[:, :, :, 0], pattern=[[0, 2], [P, T]], base=0, channel_multiplier=1).then_inc(rtab, 1)
            pool.iota(pairs[:, :, :, 1], pattern=[[SEQ, 2], [P, T]], base=0, channel_multiplier=1).then_inc(rtab, 1)
            link(pool.memset(tri[:, :, :], 1.0))
            pool.affine_select(out=tri[:, :, :], in_=tri[:, :, :], compare_op=ALU.is_ge, fill=0.0, base=0,
                               pattern=[[1, NE], [-1, NE]], channel_multiplier=0).then_inc(rtab, 1)
            pool.memset(xg[:, :], 0.0).then_inc(zeroed, 1)
            pool.wait_ge(zeroed, 1)
            pool.wait_ge(table_init, 16)
            pool.wait_ge(slots_ready, 1)
            pool.wait_ge(rtab, 8)
            for c in range(2):
                for t in range(T):
                    pool.indirect_dma_start(
                        out=table_dram, out_offset=bass.IndirectOffsetOnAxis(ap=sloti[:, c, t:t + 1], axis=0),
                        in_=pairs[:, c, t, :], in_offset=None).then_inc(table_out, 16)
            pool.wait_ge(table_out, 16 * 2 * T)
            pool.dma_start(slots[:, :, :], table_dram.rearrange("(p a) c -> p a c", p=P)).then_inc(slots_in, 16)
            pool.wait_ge(slots_in, 16)
            last_token, last_row = pool.to_reg(SEQ - 1), pool.to_reg(2 * SEQ - 1)

            def fetch_rows(i, is_set, times):
                pool.tensor_copy(idx1[:, :], slots[:, bass.ds(i, 1), 0]).then_inc(is_set, 1)
                for b in range(2):
                    pool.wait_ge(hn2_out[b], 16 * T // 2)
                pool.wait_ge(is_set, times)
                pool.indirect_dma_start(
                    out=xg[:, :], out_offset=None, in_=hn2_dram,
                    in_offset=bass.IndirectOffsetOnAxis(ap=idx1[:, 0:1], axis=0),
                    bounds_check=last_token, oob_is_err=False).then_inc(rows_in, 16)

            def tile(i):
                tiles, loads = pool.snap(i + 1), pool.snap(16 * i + 16)
                pool.wait_ge(rows_turned, tiles)
                pool.wait_ge(rows_in, loads)
                pool.tensor_copy(idx2[:, :], slots[:, bass.ds(i, 1), 1]).then_inc(idx2_set, 1)
                fetch_rows(tiles, idx1_set, tiles)
                pool.wait_ge(slots_in, 16)
                pool.wait_ge(ya_done, tiles)
                pool.wait_ge(yb_done, tiles)
                pool.wait_ge(idx2_set, tiles)
                pool.indirect_dma_start(
                    out=y_dram, out_offset=bass.IndirectOffsetOnAxis(ap=idx2[:, 0:1], axis=0),
                    in_=y[:, :], in_offset=None,
                    bounds_check=last_row, oob_is_err=False).then_inc(y_out, 16)
                pool.wait_ge(y_out, loads)

            fetch_rows(0, idx_first, 1)
            with pool.Fori(0, NE) as i:
                tile(i)
            pool.wait_ge(eid_ready, 2)
            with pool.Fori(0, OVER) as o:
                e = pool.value_load(eidi[0:1, 0, bass.ds(o, 1)], min_val=0, max_val=NE)
                with pool.If(e < NE):
                    tile(o + NE)
            pool.memset(idx2[:, :], 0).then_inc(moe_done, 1)

        @block.scalar
        def _(act):
            def copy(dst, src):
                return nc.scalar.activation(dst, src, ACT.Copy)

            def square_x(t):
                act.wait_ge(x_in[t % 4], 16 * (t // 4 + 1))
                if t:
                    act.wait_ge(ss_ready, t)
                nc.scalar.activation(sq1[:, :], xin[:, t % 4, :], ACT.Square,
                                     accum_out=ss[:, t:t + 1]).then_inc(ss_ready, 1)

            def split_w(s):
                act.wait_ge(w_in_sem[s % RAW], 16 * (s // RAW + 1))
                if s >= RING:
                    act.wait_ge(w_used, s - RING + 1)
                copy(w_hi[:, s % RING, :], w_raw[:, s % RAW, :]).then_inc(w_hi_done, 1)

            square_x(0)
            for t in range(T):
                if t + 1 < T:
                    square_x(t + 1)
                act.wait_ge(x_turned, t + 1)
                copy(hn_hi[:, :, P * t:P * t + P], PS[t % 2][:, :].rearrange("p (k n) -> p k n", n=P))\
                    .then_inc(hn_hi_done, 1)
            for s in range(RING):
                split_w(s)
            act.wait_ge(rope_arg, 2)
            nc.scalar.activation(sn[:, :, :], ang[:, 2], ACT.Sin).then_inc(sin_done, 1)
            nc.scalar.activation(cs[:, :, :], ang[:, 3], ACT.Sin).then_inc(sin_done, 1)
            act.wait_ge(lam_dot, 1)
            nc.scalar.activation(lam[:, 2:4], lam[:, 0:2], ACT.Exp).then_inc(lam_exp, 1)

            def evacuate(j):
                for t in range(T):
                    if t < T - 1:
                        act.wait_ge(acc_ready, (T - 1) * j + t + 1)
                    else:
                        act.wait_ge(w_used, KD * (j + 1))
                    dst = {SV: sv, SU: su, Q: q, K: k, V: v}[j]
                    nc.scalar.activation(dst[:, t, :], bank(t), ACT.Gelu if j in (SV, SU) else ACT.Copy)\
                        .then_inc(acc_out, 1)

            for s in range(STEPS_IN):
                if s % KD == KD - 1:
                    evacuate(s // KD)
                split_w(s + RING)
            for t in range(T):
                act.wait_ge(qk_turned, 2 * t + 1)
                copy(qT[:, :, P * t:P * t + P], bank(6).rearrange("p (h n) -> p h n", n=P)).then_inc(qT_done, 1)

            def turned_out(u, groups):
                n = u // H + 1
                for g0 in range(0, n, 4):
                    w = min(4, n - g0)
                    act.wait_ge(a_turned, groups + 1)
                    if u >= 2:
                        act.wait_ge(o_ready, u - 1)
                    copy(probT[:, u % 2, g0:g0 + w, :], bank(6)[:, 0:P * w].rearrange("p (k n) -> p k n", n=P))\
                        .then_inc(aT_done, 1)
                    groups += 1
                return groups

            groups = 0
            for u in range(H * T):
                n = u // H + 1
                for m in range(2):
                    act.wait_ge(max_done, 2 * u + m + 1)
                    if u >= 2:
                        act.wait_ge(a_turned, done_groups(u - 2))
                    nc.scalar.activation(prob[:, u % 2, m, 0:P * n], PS[(2 * u + m) % 3][:, 0:P * n], ACT.Exp,
                                         bias=nmax[:, 2 * u + m:2 * u + m + 1],
                                         accum_out=lsum[:, u, m:m + 1]).then_inc(exp_done, 1)
                if u >= 1:
                    groups = turned_out(u - 1, groups)
            groups = turned_out(H * T - 1, groups)

            for t in range(T):
                act.wait_ge(mix_turned, t + 1)
                copy(mix_hi[:, :, P * t:P * t + P], PS[t % 2][:, :].rearrange("p (k n) -> p k n", n=P))\
                    .then_inc(mix_hi_done, 1)
            for s in range(STEPS_IN + RING, STEPS):
                split_w(s)

            for t in range(T):
                act.wait_ge(h_ready, T + t + 1)
                if t:
                    act.wait_ge(ss2_ready, t)
                nc.scalar.activation(sq2[:, :], h[:, t, :], ACT.Square,
                                     accum_out=ss2[:, t:t + 1]).then_inc(ss2_ready, 1)
            for t in range(T):
                act.wait_ge(hn2_ready, t + 1)
                act.dma_start(hn2_dram[P * t:P * t + P, :], hn2[:, t % 2, :]).then_inc(hn2_out[t % 2], 16)
                act.wait_ge(h_turned, t + 1)
                if t:
                    act.wait_ge(logits, t)
                copy(hnT2[:, :, :], PS[t % 2][:, :].rearrange("p (k n) -> p k n", n=P)).then_inc(hT_done, 1)
            act.wait_ge(gd_ready, 1)
            nc.scalar.activation(gexp[:, :, :], gd[:, :, :], ACT.Exp).then_inc(gexp_done, 1)
            act.wait_ge(dm_ready, 1)
            nc.scalar.activation(r8["e2"][:, :], r8["dm"][:, :], ACT.Exp).then_inc(e2_done, 1)

            def tile(i):
                act.wait_ge(chunk_used, 6 * i + 2)
                nc.scalar.activation(gact[:, :], bank(0), ACT.Silu).then_inc(silu_done, 1)
                turn_rows(i + 1)
                act.wait_ge(hid_turned, i + 1)
                copy(actT[:, :, :], bank(4).rearrange("p (k n) -> p k n", n=P)).then_inc(hidT_done, 1)
                act.wait_ge(chunk_used, 6 * i + 6)
                copy(y[:, 0:BANK], bank(6)).then_inc(ya_done, 1)

            def turn_rows(i):
                act.wait_ge(rows_turned, i + 1)
                copy(xT[:, 0:KD // 2, :], bank(2).rearrange("p (k n) -> p k n", n=P)).then_inc(xTa_done, 1)

            turn_rows(0)
            with act.Fori(0, NE) as i:
                tile(i)
            act.wait_ge(eid_ready, 2)
            with act.Fori(0, OVER) as o:
                e = act.value_load(eidi[0:1, 0, bass.ds(o, 1)], min_val=0, max_val=NE)
                with act.If(e < NE):
                    tile(o + NE)

        @block.vector
        def _(dve):
            steps = [0]

            def link(ins):
                steps[0] += 1
                ins.then_inc(dve_step, 1)
                dve.wait_ge(dve_step, steps[0])

            def residual(j):
                dve.wait_ge(hx_in, 16)
                for t in range(T):
                    if t < T - 1:
                        dve.wait_ge(acc_ready, (T - 1) * (NB_IN + j) + t + 1)
                    else:
                        dve.wait_ge(w_used, STEPS_IN + KD * (j + 1))
                    dst = h[:, t, WB * j:WB * j + WB]
                    dve.tensor_tensor(dst, bank(t), dst, ALU.add).then_inc(h_ready, 1)

            def take_logits(t):
                dve.wait_ge(logits, t + 1)
                dve.tensor_tensor(lg[:, t, :], bank(4 + t % 2)[:, 0:NG + NE], rbias[:, :], ALU.add).then_inc(lg_done, 1)

            dve.wait_ge(gmix_in, 16)

            def scale_x(t):
                dve.wait_ge(rs_ready, t + 1)
                if t >= 2:
                    dve.wait_ge(x_turned, t - 1)
                dve.scalar_tensor_tensor(out=xs[:, t % 2, :], in0=xin[:, t % 4, :], scalar=rs[:, t:t + 1],
                                         in1=gmix[:, :], op0=ALU.mult, op1=ALU.mult).then_inc(xs_ready, 1)

            def lower(dst, turned, hi, t):
                return dve.tensor_tensor(dst[:, :, P * t:P * t + P],
                                         turned.rearrange("p (k n) -> p k n", n=P),
                                         hi[:, :, P * t:P * t + P].bitcast(F32), ALU.subtract)

            scale_x(0)
            for t in range(T):
                if t + 1 < T:
                    scale_x(t + 1)
                dve.wait_ge(hn_hi_done, t + 1)
                lower(hn_lo, PS[t % 2][:, :], hn_hi, t).then_inc(hn_lo_done, 1)

            def split_w(s):
                dve.wait_ge(w_hi_done, s + 1)
                dve.tensor_tensor(w_lo[:, s % RING, :], w_raw[:, s % RAW, :], w_hi[:, s % RING, :].bitcast(F32),
                                  ALU.subtract).then_inc(w_lo_done, 1)

            for s in range(RING):
                split_w(s)

            dve.wait_ge(small_in, 16 * len(SMALL))
            link(dve.tensor_copy(posf[:, :], posi[:, :]))
            for i in range(HALF):
                link(dve.tensor_scalar(ang[:, 0, :, i], posf[:, :], float(np.float32(THETA ** (-2.0 * i / ROPE))), None,
                                       ALU.mult))
            a0, turns, a2, a3 = (ang[:, i] for i in range(4))
            ROUND = 1.5 * 2.0 ** 23
            T1, T2 = 6.28125, 0.001934051513671875
            T3 = 2 * np.pi - T1 - T2
            link(dve.tensor_scalar(turns, a0, 1 / (2 * np.pi), None, ALU.mult))
            link(dve.tensor_scalar(turns, turns, ROUND, None, ALU.add))
            link(dve.tensor_scalar(turns, turns, ROUND, None, ALU.subtract))
            for c in (T1, T2, float(np.float32(T3))):
                link(dve.scalar_tensor_tensor(out=a0, in0=turns, scalar=-c, in1=a0, op0=ALU.mult, op1=ALU.add))
            LIM = 3.1415925
            dve.tensor_scalar(a2, a0, LIM, -LIM, ALU.min, ALU.max).then_inc(rope_arg, 1)
            link(dve.tensor_scalar(turns, a0, np.pi / 2, None, ALU.is_gt))
            link(dve.tensor_scalar(a3, a0, np.pi / 2, None, ALU.add))
            link(dve.scalar_tensor_tensor(out=a3, in0=turns, scalar=-2 * np.pi, in1=a3, op0=ALU.mult, op1=ALU.add))
            dve.tensor_scalar(a3, a3, LIM, -LIM, ALU.min, ALU.max).then_inc(rope_arg, 1)
            link(dve.tensor_tensor(lam4[:, 0:2, :], lam4[:, 0:2, :], lam4[:, 2:4, :], ALU.mult))
            dve.reduce_sum(lam[:, 0:2], lam4[:, 0:2, :], AX.X).then_inc(lam_dot, 1)
            dve.wait_ge(lam_exp, 1)
            link(dve.tensor_tensor(lam[:, 4:5], lam[:, 3:4], lam[:, 2:3], ALU.subtract))
            link(dve.tensor_scalar(lam[:, 5:6], lam[:, 4:5], -LAMBDA_INIT, None, ALU.add))
            dve.wait_ge(ws_turned, 1)
            dve.tensor_copy(wsT[:, :, :], bank(7).rearrange("p (g n) -> p g n", n=P)).then_inc(ws_out, 1)

            def layer_norm(t):
                dve.wait_ge(acc_out, T * SV + t + 1)
                if t:
                    dve.wait_ge(mv_ready, t)
                link(dve.bn_stats(stat[:, :], sv[:, t, :]))
                dve.bn_aggr(mv[:, t, :], stat[:, :]).then_inc(mv_ready, 1)

            def sum_squares(n):
                width = DH if n < 2 * T else P
                dve.wait_ge(sq_done, n + 1)
                dve.reduce_sum(sums[:, n % 2, 0:WB // width], sq[:, n % 2, :].rearrange("p (g d) -> p g d", d=width),
                               AX.X).then_inc(sums_done, 1)

            for s in range(STEPS_IN):
                j, t = s // KD, s % KD
                split_w(s + RING)
                if j == SV + 1:
                    layer_norm(t)
                if j == Q + 1:
                    sum_squares(t)
                if j == K + 1:
                    sum_squares(T + t)

            for t in range(T):
                dve.wait_ge(qk_turned, 2 * t + 2)
                dve.tensor_copy(kT[:, :, P * t:P * t + P], bank(7).rearrange("p (h n) -> p h n", n=P))\
                    .then_inc(kT_done, 1)

            for i in range(2 * G):
                c0, g = T // 2 * (i // G), i % G
                dve.wait_ge(sg_ready, i + 1)
                dst = su[:, c0:c0 + T // 2, P * g:P * g + P]
                dve.scalar_tensor_tensor(out=dst, in0=bank(i % 6).rearrange("p (c d) -> p c d", d=P),
                                         scalar=bs[:, g:g + 1], in1=dst, op0=ALU.add, op1=ALU.mult)\
                    .then_inc(sg_gated, 1)

            def maxima(u):
                n = u // H + 1
                for m in range(2):
                    dve.wait_ge(s_ready, 2 * u + m + 1)
                    dve.tensor_reduce(nmax[:, 2 * u + m:2 * u + m + 1], PS[(2 * u + m) % 3][:, 0:P * n], AX.X, ALU.max,
                                      negate=True).then_inc(max_done, 1)

            def combine(u):
                n = u // H + 1
                dve.wait_ge(exp_done, 2 * u + 2)
                link(dve.reciprocal(linv[:, u, :], lsum[:, u, :]))
                link(dve.scalar_tensor_tensor(out=mixc[:, u:u + 1], in0=lsum[:, u, 0:1], scalar=lam[:, 5:6],
                                              in1=linv[:, u, 1:2], op0=ALU.mult, op1=ALU.mult))
                dve.scalar_tensor_tensor(out=prob[:, u % 2, 0, 0:P * n], in0=prob[:, u % 2, 1, 0:P * n],
                                         scalar=mixc[:, u:u + 1], in1=prob[:, u % 2, 0, 0:P * n],
                                         op0=ALU.mult, op1=ALU.add).then_inc(a_ready, 1)

            def head_out(u):
                t, hd = u // H, u % H
                dve.wait_ge(o_ready, u + 1)
                dve.tensor_scalar(att[:, t, P * hd:P * hd + P], bank(7)[:, 0:P], linv[:, u, 0:1], None, ALU.mult)\
                    .then_inc(o_done, 1)

            maxima(0)
            for u in range(H * T):
                if u + 1 < H * T:
                    maxima(u + 1)
                combine(u)
                if u >= 1:
                    head_out(u - 1)
                if u < T:
                    sum_squares(2 * T + u)
                if u % H == 1 and u > 2 * H:
                    sum_squares(3 * T + u // H - 2)
            head_out(H * T - 1)
            sum_squares(4 * T - 2)
            sum_squares(4 * T - 1)

            for t in range(T):
                dve.wait_ge(mix_hi_done, t + 1)
                lower(mix_lo, PS[t % 2][:, :], mix_hi, t).then_inc(mix_lo_done, 1)
            for s in range(STEPS_IN + RING, STEPS):
                if s - RING == STEPS_IN + KD - 1:
                    residual(0)
                split_w(s)
            residual(1)

            for t in range(T):
                dve.wait_ge(rs2_ready, t + 1)
                if t >= 2:
                    dve.wait_ge(hn2_out[t % 2], 16 * (t // 2))
                    dve.wait_ge(h_turned, t - 1)
                dve.scalar_tensor_tensor(out=hn2[:, t % 2, :], in0=h[:, t, :], scalar=rs2[:, t:t + 1],
                                         in1=gffn[:, :], op0=ALU.mult, op1=ALU.mult).then_inc(hn2_ready, 1)
                if t:
                    take_logits(t - 1)
            take_logits(T - 1)
            dve.wait_ge(lg_done, T)

            dve.wait_ge(rtab, 8)
            R8 = {n: m[:, :] for n, m in r8.items()}

            def over(m, shape):
                return m.unsqueeze(2).broadcast_to(shape)

            gs, es = [P, T, NG], [P, T, NE]
            link(dve.tensor_reduce(R8["gmax"], lg[:, :, 0:NG], AX.X, ALU.max))
            dve.tensor_tensor(gd[:, :, :], lg[:, :, 0:NG], over(R8["gmax"], gs), ALU.subtract).then_inc(gd_ready, 1)
            dve.wait_ge(gd_ready, 1)
            link(dve.scalar_tensor_tensor(out=grk[:, :, :], in0=gd[:, :, :], scalar=0.0,
                                          in1=revg[:, :].unsqueeze(1).broadcast_to(gs),
                                          op0=ALU.is_equal, op1=ALU.mult))
            link(dve.tensor_reduce(R8["grank"], grk[:, :, :], AX.X, ALU.max))
            link(dve.tensor_tensor(pen[:, :, :], grk[:, :, :], over(R8["grank"], gs), ALU.is_equal))
            link(dve.tensor_scalar(pen[:, :, :], pen[:, :, :], -1.0, -NEG, ALU.add, ALU.mult))
            link(dve.tensor_tensor(ev[:, :, :].rearrange("p t (g e) -> p t g e", e=EG),
                                   lg[:, :, NG:].rearrange("p t (g e) -> p t g e", e=EG),
                                   pen[:, :, :].unsqueeze(3).broadcast_to([P, T, NG, EG]), ALU.add))
            for m, r, oh in (("m1", "r1", oh1), ("m2", "r2", oh2)):
                link(dve.tensor_reduce(R8[m], ev[:, :, :], AX.X, ALU.max))
                link(dve.tensor_tensor(rk[:, :, :], ev[:, :, :], over(R8[m], es), ALU.is_equal))
                link(dve.tensor_tensor(rk[:, :, :], rk[:, :, :], reve[:, :].unsqueeze(1).broadcast_to(es), ALU.mult))
                link(dve.tensor_reduce(R8[r], rk[:, :, :], AX.X, ALU.max))
                link(dve.tensor_tensor(oh[:, :, :], rk[:, :, :], over(R8[r], es), ALU.is_equal))
                if m == "m1":
                    link(dve.scalar_tensor_tensor(out=ev[:, :, :], in0=oh[:, :, :], scalar=4 * NEG, in1=ev[:, :, :],
                                                  op0=ALU.mult, op1=ALU.add))
            dve.tensor_tensor(cnt[:, :, :], oh1[:, :, :], oh2[:, :, :], ALU.add).then_inc(cnt_ready, 1)
            dve.tensor_tensor(R8["dm"], R8["m2"], R8["m1"], ALU.subtract).then_inc(dm_ready, 1)

            dve.memset(total[:, 0, :], 0.0).then_inc(dve_step, 1)
            steps[0] += 1
            dve.wait_ge(counted, 1)
            dve.wait_ge(dve_step, steps[0])
            for t in range(T):
                link(dve.tensor_tensor(total[:, t + 1, :], total[:, t, :],
                                       bank(7)[:, NE * t:NE * t + NE], ALU.add))
            link(dve.tensor_tensor(pos[:, :, :], bank(6)[:, 0:T * NE].rearrange("p (t e) -> p t e", e=NE),
                                   total[:, 0:T, :], ALU.add))
            link(dve.tensor_tensor(cmpt[:, :, 0:NTHR], total[:, T, :].unsqueeze(2).broadcast_to([P, NE, NTHR]),
                                   thr[:, :].unsqueeze(1).broadcast_to([P, NE, NTHR]), ALU.is_gt))
            link(dve.reduce_sum(nover[:, :], cmpt[:, :, 0:NTHR], AX.X))
            link(dve.tensor_tensor(cmpt[:, :, :], tri[:, :, :], nover[:, :].unsqueeze(1).broadcast_to([P, NE, NE]),
                                   ALU.mult))
            link(dve.reduce_sum(cum[:, :], cmpt[:, :, :], AX.X))
            link(dve.tensor_tensor(cmpt[:, 0:OVER + 1, :], cum[:, :].unsqueeze(1).broadcast_to([P, OVER + 1, NE]),
                                   ocol[:, :].unsqueeze(2).broadcast_to([P, OVER + 1, NE]), ALU.is_le))
            link(dve.reduce_sum(eid[:, :], cmpt[:, 0:OVER + 1, :], AX.X))
            link(dve.tensor_tensor(offs[:, :], cum[:, :], nover[:, :], ALU.subtract))
            link(dve.tensor_tensor(offs[:, :], offs[:, :], ecol[:, :], ALU.subtract))
            link(dve.tensor_scalar(offs[:, :], offs[:, :], float(NE - 1), None, ALU.add))
            link(dve.tensor_copy(posn[:, :, :], pos[:, :, :]))
            link(dve.tensor_scalar(qti[:, :, :], posn[:, :, :], 7, None, ALU.arith_shift_right))
            link(dve.tensor_copy(qt[:, :, :], qti[:, :, :]))
            link(dve.tensor_tensor(ev[:, :, :], qt[:, :, :], offs[:, :].unsqueeze(1).broadcast_to(es), ALU.add))
            link(dve.tensor_scalar(rk[:, :, :], qt[:, :, :], 0.0, None, ALU.is_gt))
            link(dve.tensor_tensor(ev[:, :, :], ev[:, :, :], rk[:, :, :], ALU.mult))
            link(dve.scalar_tensor_tensor(out=ev[:, :, :], in0=pos[:, :, :], scalar=float(NT), in1=ev[:, :, :],
                                          op0=ALU.mult, op1=ALU.add))
            link(dve.scalar_tensor_tensor(out=ev[:, :, :], in0=qt[:, :, :], scalar=float(-P * NT), in1=ev[:, :, :],
                                          op0=ALU.mult, op1=ALU.add))
            link(dve.tensor_tensor(ev[:, :, :], ev[:, :, :], ecol[:, :].unsqueeze(1).broadcast_to(es), ALU.add))
            for oh, s in ((oh1, "slot1"), (oh2, "slot2")):
                link(dve.tensor_tensor(rk[:, :, :], oh[:, :, :], ev[:, :, :], ALU.mult))
                link(dve.reduce_sum(R8[s], rk[:, :, :], AX.X))
            link(dve.tensor_copy(sloti[:, 0, :], R8["slot1"]))
            dve.tensor_copy(sloti[:, 1, :], R8["slot2"]).then_inc(slots_ready, 1)
            dve.tensor_copy(eidi[:, 0, :], eid[:, :]).then_inc(eid_ready, 1)
            dve.tensor_scalar(eidi[:, 1, :], eid[:, :], float(NE - 1), None, ALU.min).then_inc(eid_ready, 1)
            dve.wait_ge(gexp_done, 1)
            link(dve.reduce_sum(R8["gsum"], gexp[:, :, :], AX.X))
            dve.wait_ge(e2_done, 1)
            link(dve.tensor_scalar(R8["den"], R8["e2"], 1.0, None, ALU.add))
            link(dve.tensor_tensor(R8["den"], R8["den"], R8["gsum"], ALU.mult))
            link(dve.reciprocal(R8["gate1"], R8["den"]))
            link(dve.tensor_tensor(R8["gate2"], R8["gate1"], R8["e2"], ALU.mult))

            def turn_rows(i):
                dve.wait_ge(rows_turned, i + 1)
                dve.tensor_copy(xT[:, KD // 2:, :], bank(3).rearrange("p (k n) -> p k n", n=P)).then_inc(xTb_done, 1)

            def tile(i):
                dve.wait_ge(chunk_used, 6 * i + 4)
                dve.wait_ge(silu_done, i + 1)
                dve.tensor_tensor(hid[:, :], bank(1), gact[:, :], ALU.mult).then_inc(hid_done, 1)
                turn_rows(i + 1)
                dve.wait_ge(chunk_used, 6 * i + 6)
                dve.tensor_copy(y[:, BANK:], bank(7)).then_inc(yb_done, 1)

            turn_rows(0)
            with dve.Fori(0, NE) as i:
                tile(i)
            with dve.Fori(0, OVER) as o:
                e = dve.value_load(eidi[0:1, 0, bass.ds(o, 1)], min_val=0, max_val=NE)
                with dve.If(e < NE):
                    tile(o + NE)

            for t in range(T):
                dve.wait_ge(yin_sem[t], 16)
                dve.scalar_tensor_tensor(out=h[:, t, :], in0=yin[:, t, 0, :], scalar=r8["gate1"][:, t:t + 1],
                                         in1=h[:, t, :], op0=ALU.mult, op1=ALU.add).then_inc(h1_done, 1)
                dve.wait_ge(h1_done, t + 1)
                dve.scalar_tensor_tensor(out=h[:, t, :], in0=yin[:, t, 1, :], scalar=r8["gate2"][:, t:t + 1],
                                         in1=h[:, t, :], op0=ALU.mult, op1=ALU.add).then_inc(h2_done, 1)

        @block.tensor
        def _(pe):
            pe.wait_ge(made, 5)

            def turn(dst, src, n=KD):
                for b in range(n):
                    ins = pe.transpose(dst[:, P * b:P * b + P], src[:, P * b:P * b + P], ident[:, :])
                return ins

            for t in range(T):
                pe.wait_ge(xs_ready, t + 1)
                if t >= 2:
                    pe.wait_ge(hn_lo_done, t - 1)
                turn(PS[t % 2][:, :], xs[:, t % 2, :]).then_inc(x_turned, 1)
            pe.wait_ge(ws_masked, 1)
            for g in range(G):
                ins = pe.transpose(bank(7)[:, P * g:P * g + P], wsm[:, g, :], ident[:, :])
            ins.then_inc(ws_turned, 1)
            pe.wait_ge(hn_lo_done, T)

            def project(s, hi, lo):
                j, kk = s // KD, s % KD
                pe.wait_ge(w_lo_done, s + 1)
                for t in range(T):
                    if kk == 0 and j and j != NB_IN:
                        if j < NB_IN:
                            pe.wait_ge(acc_out, T * (j - 1) + t + 1)
                        else:
                            pe.wait_ge(h_ready, t + 1)
                    if s == 0 and t == 7:
                        pe.wait_ge(ws_out, 1)
                    rows = slice(P * t, P * t + P)
                    w = w_hi[:, s % RING, :]
                    pe.matmul(bank(t), lo[:, kk, rows], w, start=(kk == 0), stop=False)
                    pe.matmul(bank(t), hi[:, kk, rows], w_lo[:, s % RING, :], start=False, stop=False)
                    ins = pe.matmul(bank(t), hi[:, kk, rows], w, start=False, stop=(kk == KD - 1))
                    if kk == KD - 1 and t < T - 1:
                        ins.then_inc(acc_ready, 1)
                ins.then_inc(w_used, 1)

            for s in range(STEPS_IN):
                project(s, hn_hi, hn_lo)

            for t in range(T):
                pe.wait_ge(acc_out, NB_IN * T)
                pe.wait_ge(qk_done, 2 * (T + t + 1))
                if t:
                    pe.wait_ge(qT_done, t)
                turn(bank(6), q[:, t, :], H).then_inc(qk_turned, 1)
                if t:
                    pe.wait_ge(kT_done, t)
                turn(bank(7), k[:, t, :], H).then_inc(qk_turned, 1)
            pe.wait_ge(sv_done, T)
            for i in range(2 * G):
                c0, g = T // 2 * (i // G), i % G
                if i >= 6:
                    pe.wait_ge(sg_gated, i - 5)
                pe.matmul(bank(i % 6).rearrange("p (c d) -> p c d", d=P), wsT[:, g, :],
                          sv[:, c0:c0 + T // 2, P * g:P * g + P], start=True, stop=True).then_inc(sg_ready, 1)
            pe.wait_ge(qT_done, T)
            pe.wait_ge(kT_done, T)
            pe.wait_ge(sg_gated, 2 * G)

            def scores(u):
                t, hd = u // H, u % H
                n = P * (t + 1)
                for m in range(2):
                    w = 2 * u + m
                    if w >= 3:
                        pe.wait_ge(exp_done, w - 2)
                    half = slice(DH * m, DH * m + DH)
                    for c0 in range(0, n, BANK):
                        c1 = min(n, c0 + BANK)
                        pe.matmul(PS[w % 3][:, c0:c1], qT[half, hd, P * t:P * t + P], kT[half, hd, c0:c1],
                                  start=True, stop=(c1 < n))
                    ins = pe.matmul(PS[w % 3][:, n - P:n], identb[:, :], causal[:, :], start=False, stop=True)
                    ins.then_inc(s_ready, 1)

            groups = [0]

            def turn_weights(u):
                n = u // H + 1
                pe.wait_ge(a_ready, u + 1)
                for g0 in range(0, n, 4):
                    if groups[0]:
                        pe.wait_ge(aT_done, groups[0])
                    ins = turn(bank(6), prob[:, u % 2, 0, P * g0:], min(4, n - g0))
                    ins.then_inc(a_turned, 1)
                    groups[0] += 1

            def values(u):
                n, hd = u // H + 1, u % H
                if u:
                    pe.wait_ge(o_done, u)
                pe.wait_ge(aT_done, done_groups(u))
                for b in range(n):
                    ins = pe.matmul(bank(7)[:, 0:P], probT[:, u % 2, b, :], v[:, b, P * hd:P * hd + P],
                                    start=(b == 0), stop=(b == n - 1))
                ins.then_inc(o_ready, 1)

            scores(0)
            for u in range(H * T):
                if u + 1 < H * T:
                    scores(u + 1)
                turn_weights(u)
                values(u)

            for t in range(T):
                pe.wait_ge(att_done, t + 1)
                pe.wait_ge(sg_done, t + 1)
                pe.wait_ge(exp_done, 2 * H * T)
                if t >= 2:
                    pe.wait_ge(mix_lo_done, t - 1)
                turn(PS[t % 2][:, 0:BANK], att[:, t, :], H)
                turn(PS[t % 2][:, BANK:], su[:, t, :], G).then_inc(mix_turned, 1)
            pe.wait_ge(mix_lo_done, T)
            pe.wait_ge(o_done, H * T)
            for s in range(STEPS_IN, STEPS):
                project(s, mix_hi, mix_lo)

            pe.wait_ge(h_ready, 2 * T)
            for t in range(T):
                pe.wait_ge(hn2_ready, t + 1)
                if t >= 2:
                    pe.wait_ge(hT_done, t - 1)
                turn(PS[t % 2][:, :], hn2[:, t % 2, :]).then_inc(h_turned, 1)
                pe.wait_ge(hT_done, t + 1)
                if t >= 2:
                    pe.wait_ge(lg_done, t - 1)
                for b in range(KD):
                    ins = pe.matmul(bank(4 + t % 2)[:, 0:NG + NE], hnT2[:, b, :], router[:, b, :],
                                    start=(b == 0), stop=(b == KD - 1))
                ins.then_inc(logits, 1)
            pe.wait_ge(cnt_ready, 1)
            flat = cnt[:, :, :].rearrange("p t e -> p (t e)")
            pe.matmul(bank(6)[:, 0:T * NE], earlier[:, :], flat, start=True, stop=True)
            pe.matmul(bank(7)[:, 0:T * NE], onesb[:, :], flat, start=True, stop=True).then_inc(counted, 1)

            def turn_rows(i):
                pe.wait_ge(rows_in, 16 * i + 16)
                turn(PS[1][:, :], xg[:, :]).then_inc(rows_turned, 1)

            def tile(i, half, use):
                pe.wait_ge(xTa_done, i + 1)
                pe.wait_ge(xTb_done, i + 1)
                for side in range(2):
                    for kk in range(KD):
                        c = 2 * side + kk // (KD // 2)
                        if kk % (KD // 2) == 0:
                            pe.wait_ge(ew_in[half][c], 16 * use)
                        ins = pe.matmul(bank(side), xT[:, kk, :], ew_chunk(half, c)[:, kk % (KD // 2), :],
                                        start=(kk == 0), stop=(kk == KD - 1))
                        if kk % (KD // 2) == KD // 2 - 1:
                            ins.then_inc(chunk_used, 1)
                turn_rows(i + 1)
                pe.wait_ge(hid_done, i + 1)
                turn(bank(4), hid[:, :], F // P).then_inc(hid_turned, 1)
                pe.wait_ge(hidT_done, i + 1)
                for kk in range(F // P):
                    c = 4 + kk // 2
                    if kk % 2 == 0:
                        pe.wait_ge(ew_in[half][c], 16 * use)
                    for b in range(2):
                        ins = pe.matmul(bank(6 + b), actT[:, kk, :],
                                        ew_chunk(half, c)[:, kk % 2, BANK * b:BANK * b + BANK],
                                        start=(kk == 0), stop=(kk == F // P - 1))
                    if kk % 2:
                        ins.then_inc(chunk_used, 1)

            pe.wait_ge(lg_done, T)
            pe.wait_ge(slots_ready, 1)
            turn_rows(0)
            with pe.Fori(0, NE // 2) as e2:
                tile(2 * e2, 0, e2 + 1)
                tile(2 * e2 + 1, 1, e2 + 1)
            pe.wait_ge(eid_ready, 2)
            with pe.Fori(0, OVER) as o:
                e = pe.value_load(eidi[0:1, 0, bass.ds(o, 1)], min_val=0, max_val=NE)
                with pe.If(e < NE):
                    tile(o + NE, 0, o + NE // 2 + 1)


_INS = ["x", "positions", "norm_mix_g", "w_in", "q_norm_g", "k_norm_g", "lambda_q1", "lambda_k1", "lambda_q2",
        "lambda_k2", "diff_out_norm_g", "sgu_ln_g", "sgu_ln_b", "sgu_w", "sgu_b", "sgu_out_norm_g", "w_out",
        "norm_ffn_g", "router_group_w", "router_group_b", "router_expert_w", "router_expert_b",
        "expert_w_gate", "expert_w_up", "expert_w_down"]


def kernel(**inputs):
    import numpy as _np
    import concourse.bacc as _bacc
    from concourse import mybir as _mybir
    from concourse.bass_utils import run_bass_kernel_spmd as _run

    nc = _bacc.Bacc("TRN2", target_bir_lowering=False, num_devices=1)
    arrays, args = {}, []
    for name in _INS:
        a = _np.ascontiguousarray(inputs[name])
        arrays[f"in_{name}"] = a
        args.append(nc.dram_tensor(f"in_{name}", a.shape, _mybir.dt.from_np(a.dtype), kind="ExternalInput").ap())
    args.append(nc.dram_tensor("out_0", (1, SEQ, D), F32, kind="ExternalOutput").ap())
    build(nc, *args)
    r = _run(nc, [arrays], core_ids=[0])
    return r.results[0]["out_0"]
```

```python
from contextlib import ExitStack

import numpy as np

import concourse.bass as bass
from concourse import mybir

ALU = mybir.AluOpType
ACT = mybir.ActivationFunctionType
AX = mybir.AxisListType
F32 = mybir.dt.float32
F32R = mybir.dt.float32r
BF16 = mybir.dt.bfloat16
I32 = mybir.dt.int32

P = 128
BANK = 512
KB = 1024

D = 1024
SEQ = 1024
T = SEQ // P
KD = D // P
H = 4
DH = 64
QK = 2 * H
ROPE = DH // 4
HALF = ROPE // 2
THETA = 500000.0
G = 4
WB = 512
NB_IN, NB_OUT = 5, 2
EPS = 1e-6
LAMBDA_INIT = 0.2
NEG = -1e30

NG, EG = 4, 8
NE = NG * EG
F = 512
OVER = 2 * SEQ // P - 1
NT = NE + OVER + 2
NTHR = SEQ // P - 1
EMPTY = 1 << 20

SV, SU, Q, K, V = range(5)
COLUMN = {Q: 0, K: 1, V: 2, SU: 3, SV: 4}
STEPS_IN = NB_IN * KD
STEPS = STEPS_IN + NB_OUT * KD
CHUNKS = 6
AHEAD = 5
CHUNK = 3 * D * F // CHUNKS // P
PROBS = 4
RAW, RING = 8, 4


def build(nc, x, positions, norm_mix_g, w_in, q_norm_g, k_norm_g, lambda_q1, lambda_k1, lambda_q2,
          lambda_k2, diff_out_norm_g, sgu_ln_g, sgu_ln_b, sgu_w, sgu_b, sgu_out_norm_g, w_out,
          norm_ffn_g, router_group_w, router_group_b, router_expert_w, router_expert_b,
          expert_w_gate, expert_w_up, expert_w_down, out):
    ctx = ExitStack()
    with ctx:
        hn2_dram = nc.dram_tensor("hn2_rows", [SEQ, D], F32).ap()
        y_dram = nc.dram_tensor("expert_rows", [2 * SEQ, D], F32).ap()
        table_dram = nc.dram_tensor("slot_table", [P * NT, 2], I32).ap()

        base = -(-nc.sbuf_base // 64) * 64
        A = base + 31 * KB
        B = A + 64 * KB
        C = B + 80 * KB
        at_const = [base]

        def place(name, shape, dt, offset):
            return nc.alloc_sbuf_tensor_at(name, shape, dt, offset=offset)

        def const(name, shape, dt):
            size = int(np.prod(shape[1:])) * (2 if dt == BF16 else 4)
            t = place(name, shape, dt, at_const[0])
            at_const[0] += -(-size // 32) * 32
            assert at_const[0] <= A, name
            return t

        ident = const("ident", [P, P], F32)
        identb = const("identb", [P, P], BF16)
        causal = const("causal", [P, P], BF16)
        earlier = const("earlier", [P, P], BF16)
        onesb = const("onesb", [P, P], BF16)
        gmix = const("gmix", [P, D], F32)
        gffn = const("gffn", [P, D], F32)
        lng = const("lng", [P, WB], F32)
        lnb = const("lnb", [P, WB], F32)
        gsgu = const("gsgu", [P, WB], F32)
        gatt = const("gatt", [P, P], F32)
        gq = const("gq", [P, DH], F32)
        gk = const("gk", [P, DH], F32)
        lam4 = const("lam4", [P, 4, DH], F32)
        lam = const("lam", [P, 8], F32)
        wsT = const("wsT", [P, G, P], F32)
        bs = const("bs", [P, G], F32)
        router = const("router", [P, KD, NG + NE], F32)
        rbias = const("rbias", [P, NG + NE], F32)
        posi = const("posi", [P, T], I32)
        posf = const("posf", [P, T], F32)
        ang = const("ang", [P, 4, T, HALF], F32)
        cs = const("cs", [P, T, HALF], F32)
        sn = const("sn", [P, T, HALF], F32)
        ss = const("ss", [P, T], F32)
        rs = const("rs", [P, T], F32)
        ss2 = const("ss2", [P, T], F32)
        rs2 = const("rs2", [P, T], F32)
        stat = const("stat", [P, 6], F32)
        mv = const("mv", [P, T, 2], F32)
        lnr = const("lnr", [P, 2], F32)
        half = const("half", [P, QK], F32)
        sums = const("sums", [P, 2, QK], F32)
        inv = const("inv", [P, 2, QK], F32)
        sq = const("sq", [P, 2, WB], F32)
        rp = const("rp", [P, 4, QK, HALF], F32)
        nmax = const("nmax", [P, 2 * H * T], F32)
        lsum = const("lsum", [P, H * T, 2], F32)
        linv = const("linv", [P, H * T, 2], F32)
        mixc = const("mixc", [P, H * T], F32)

        hn_hi = place("hn_hi", [P, KD, SEQ], F32R, A)
        hn_lo = place("hn_lo", [P, KD, SEQ], F32R, A + 32 * KB)
        qT = place("qT", [P, H, SEQ], F32, A)
        kT = place("kT", [P, H, SEQ], F32, A + 16 * KB)
        att = place("att", [P, T, WB], F32, A + 32 * KB)
        h = place("h", [P, T, D], F32, A)
        hn2 = place("hn2", [P, 2, D], F32, A + 48 * KB)
        sq2 = place("sq2", [P, D], F32, A + 56 * KB)
        hnT2 = place("hnT2", [P, KD, P], F32, A + 32 * KB)
        actT_hi = place("actT_hi", [P, F // P, P], F32R, A + 36 * KB)
        actT_lo = place("actT_lo", [P, F // P, P], F32R, A + 52 * KB)

        q = place("q", [P, T, WB], F32, B)
        k = place("k", [P, T, WB], F32, B + 16 * KB)
        v = place("v", [P, T, WB], F32, B + 32 * KB)
        sv = place("sv", [P, T, WB], F32, B + 48 * KB)
        su = place("su", [P, T, WB], F32, B + 64 * KB)
        xin = place("xin", [P, 4, D], F32, B)
        xs = place("xs", [P, 2, D], F32, B + 16 * KB)
        sq1 = place("sq1", [P, D], F32, B + 24 * KB)
        wsm = place("wsm", [P, G, P], F32, B + 32 * KB)
        prob = place("prob", [P, PROBS, 2, SEQ], F32, B)
        probT = place("probT", [P, 2, T, P], F32, B + 48 * KB)
        mix_hi = place("mix_hi", [P, KD, SEQ], F32R, B)
        mix_lo = place("mix_lo", [P, KD, SEQ], F32R, B + 32 * KB)

        w_raw = place("w_raw", [P, RAW, WB], F32, C)
        w_hi = place("w_hi", [P, RING, WB], F32R, C + 16 * KB)
        w_lo = place("w_lo", [P, RING, WB], F32R, C + 24 * KB)

        ew_raw = place("ew_raw", [P, CHUNKS, CHUNK], F32, B)
        ew_lo = place("ew_lo", [P, CHUNKS, CHUNK], F32R, B)
        ew_hi = place("ew_hi", [P, CHUNKS, CHUNK], F32R, B + CHUNKS * CHUNK * 4)
        xg = place("xg", [P, D], F32, C + 16 * KB)
        xT_hi = place("xT_hi", [P, KD, P], F32R, C + 20 * KB)
        xT_lo = place("xT_lo", [P, KD, P], F32R, A + 48 * KB)
        y = place("y", [P, D], F32, C + 24 * KB)
        gact = place("gact", [P, F], F32, C + 28 * KB)
        hid = place("hid", [P, F], F32, C + 30 * KB)
        yin = place("yin", [P, T, 2, D], F32, B)

        R = A + 38 * KB
        at_r = [R]

        def scratch(name, shape, dt=F32):
            size = int(np.prod(shape[1:])) * (2 if dt == BF16 else 4)
            t = place(name, shape, dt, at_r[0])
            at_r[0] += -(-size // 32) * 32
            assert at_r[0] <= A + 48 * KB, name
            return t

        lg = scratch("lg", [P, T, NG + NE])
        r8 = {n: scratch(n, [P, T]) for n in ("gmax", "gsum", "pgrp", "grank", "m1", "r1", "m2", "r2", "dm", "e2",
                                                "den", "gate1", "gate2", "slot1", "slot2")}
        gd = scratch("gd", [P, T, NG])
        grk = scratch("grk", [P, T, NG])
        gexp = scratch("gexp", [P, T, NG])
        pen = scratch("pen", [P, T, NG])
        revg = scratch("revg", [P, NG])
        reve = scratch("reve", [P, NE])
        ecol = scratch("ecol", [P, NE])
        thr = scratch("thr", [P, NTHR])
        ocol = scratch("ocol", [P, OVER + 1])
        eid = scratch("eid", [P, OVER + 1])
        total = scratch("total", [P, T + 1, NE])
        nover = scratch("nover", [P, NE])
        cum = scratch("cum", [P, NE])
        offs = scratch("offs", [P, NE])
        sloti = scratch("sloti", [P, 2, T], I32)
        pairs = scratch("pairs", [P, 2, T, 2], I32)
        idx1 = scratch("idx1", [P, 1], I32)
        idx2 = scratch("idx2", [P, 1], I32)
        oh1 = scratch("oh1", [P, T, NE])
        oh2 = scratch("oh2", [P, T, NE])
        W0 = C + 16 * KB
        ev = place("ev", [P, T, NE], F32, W0 + 4 * KB)
        rk = place("rk", [P, T, NE], F32, W0 + 5 * KB)
        pos = place("pos", [P, T, NE], F32, W0 + 6 * KB)
        posn = place("posn", [P, T, NE], I32, W0 + 7 * KB)
        qti = place("qti", [P, T, NE], I32, W0 + 8 * KB)
        qt = place("qt", [P, T, NE], F32, W0 + 9 * KB)
        tri = place("tri", [P, NE, NE], F32, W0 + 10 * KB)
        cnt = place("cnt", [P, T, NE], BF16, W0 + 14 * KB)
        cmpt = place("cmpt", [P, NE, NE], F32, A + 60 * KB)
        init = place("init", [P, 2 * NT], I32, W0 + 15 * KB)
        slots = place("slots", [P, NT, 2], I32, A + 56 * KB)
        eidi = place("eidi", [P, 2, OVER + 1], I32, A + 57 * KB)

        PS = [ctx.enter_context(nc.psum_tensor(f"ps{i}", [P, 2 * BANK], F32)) for i in range(4)]

        def bank(i):
            return PS[i // 2][:, BANK * (i % 2):BANK * (i % 2) + BANK]

        def sem(name):
            return ctx.enter_context(nc.semaphore(name))

        gmix_in, small_in, hx_in = sem("gmix_in"), sem("small_in"), sem("hx_in")
        x_in = [sem(f"x_in{i}") for i in range(4)]
        w_in_sem = [sem(f"w_in{i}") for i in range(RAW)]
        dve_step, pool_step = sem("dve_step"), sem("pool_step")
        ws_out = sem("ws_out")
        made, sin_done, lam_exp, ws_masked, ws_turned, rope_arg, lam_dot = (
            sem(n) for n in ("made", "sin_done", "lam_exp", "ws_masked", "ws_turned", "rope_arg", "lam_dot"))
        ss_ready, xs_ready, x_turned, hn_hi_done, hn_lo_done = (
            sem(n) for n in ("ss_ready", "xs_ready", "x_turned", "hn_hi_done", "hn_lo_done"))
        w_hi_done, w_lo_done, w_used, acc_ready, acc_out = (
            sem(n) for n in ("w_hi_done", "w_lo_done", "w_used", "acc_ready", "acc_out"))
        mv_ready, sv_done, sq_done, sums_done, qk_done, consts_done, rs_ready, rs2_ready, inv_done, scaled = (
            sem(n) for n in ("mv_ready", "sv_done", "sq_done", "sums_done", "qk_done", "consts_done", "rs_ready",
                             "rs2_ready", "inv_done", "scaled"))
        qk_turned, qT_done, kT_done, sg_ready, sg_gated, sg_done = (
            sem(n) for n in ("qk_turned", "qT_done", "kT_done", "sg_ready", "sg_gated", "sg_done"))
        s_ready, max_done, exp_done, a_ready, a_turned, aT_done, o_ready, o_done = (
            sem(n) for n in ("s_ready", "max_done", "exp_done", "a_ready", "a_turned", "aT_done", "o_ready", "o_done"))
        att_done = sem("att_done")
        mix_turned, mix_hi_done, mix_lo_done = sem("mix_turned"), sem("mix_hi_done"), sem("mix_lo_done")
        h_ready, ss2_ready, hn2_ready = sem("h_ready"), sem("ss2_ready"), sem("hn2_ready")
        hn2_out = [sem("hn2_out0"), sem("hn2_out1")]
        h_turned, hT_done, logits, lg_done = sem("h_turned"), sem("hT_done"), sem("logits"), sem("lg_done")
        gd_ready, gexp_done, dm_ready, e2_done, cnt_ready, counted, slots_ready = (
            sem(n) for n in ("gd_ready", "gexp_done", "dm_ready", "e2_done", "cnt_ready", "counted", "slots_ready"))
        table_init, table_out, slots_in = sem("table_init"), sem("table_out"), sem("slots_in")
        eid_ready, rtab, init_ready, zeroed = sem("eid_ready"), sem("rtab"), sem("init_ready"), sem("zeroed")
        ew_in = [sem(f"ew_in{c}") for c in range(CHUNKS)]
        ew_hi_done, ew_lo_done = sem("ew_hi_done"), sem("ew_lo_done")
        rows_in, rows_turned, xT_hi_done, xT_lo_done = sem("rows_in"), sem("rows_turned"), sem("xT_hi_done"), sem("xT_lo_done")
        chunk_used, silu_done, hid_done, hid_turned, actT_hi_done, actT_lo_done = (
            sem(n) for n in ("chunk_used", "silu_done", "hid_done", "hid_turned", "actT_hi_done", "actT_lo_done"))
        ya_done, yb_done, y_out, idx_first, idx1_set, idx2_set, moe_done = (
            sem(n) for n in ("ya_done", "yb_done", "y_out", "idx_first", "idx1_set", "idx2_set", "moe_done"))
        yin_sem = [sem(f"yin{t}") for t in range(T)]
        h1_done, h2_done, out_done = sem("h1_done"), sem("h2_done"), sem("out_done")

        x_t = x[0].rearrange("(t p) d -> t p d", p=P)
        out_t = out[0].rearrange("(t p) d -> t p d", p=P)
        y_t = y_dram.rearrange("(c t p) d -> t p c d", p=P, t=T)
        w_cols = [COLUMN[j] for j in range(NB_IN)]

        def w_slice(s):
            if s < STEPS_IN:
                c = w_cols[s // KD]
                return w_in[0, (s % KD) * P:(s % KD + 1) * P, c * WB:(c + 1) * WB]
            s -= STEPS_IN
            return w_out[0, (s % KD) * P:(s % KD + 1) * P, s // KD * WB:(s // KD + 1) * WB]

        def expert_chunk(e, c):
            w = (expert_w_gate, expert_w_up, expert_w_down)[c // 2]
            rows = w.shape[2] // 2
            return w[0, bass.ds(e, 1), (c % 2) * rows:(c % 2 + 1) * rows, :].rearrange("o (k p) n -> p (o k) n", p=P)

        def by_row(ew, c):
            return ew[:, c, :].rearrange("p (k n) -> p k n", n=F if c < 4 else D)

        SMALL = [(lng[:, :], sgu_ln_g.broadcast_to([P, WB])), (lnb[:, :], sgu_ln_b.broadcast_to([P, WB])),
                 (gsgu[:, :], sgu_out_norm_g.rearrange("l g d -> l (g d)").broadcast_to([P, WB])),
                 (gatt[:, :], diff_out_norm_g.broadcast_to([P, P])),
                 (gq[:, :], q_norm_g.broadcast_to([P, DH])), (gk[:, :], k_norm_g.broadcast_to([P, DH])),
                 (lam4[:, 0, :], lambda_q1.broadcast_to([P, DH])), (lam4[:, 1, :], lambda_q2.broadcast_to([P, DH])),
                 (lam4[:, 2, :], lambda_k1.broadcast_to([P, DH])), (lam4[:, 3, :], lambda_k2.broadcast_to([P, DH])),
                 (gffn[:, :], norm_ffn_g.broadcast_to([P, D])),
                 (rbias[:, 0:NG], router_group_b.broadcast_to([P, NG])),
                 (rbias[:, NG:], router_expert_b.broadcast_to([P, NE])),
                 (router[:, :, 0:NG], router_group_w[0].rearrange("(k p) n -> p k n", p=P)),
                 (router[:, :, NG:], router_expert_w[0].rearrange("(k p) n -> p k n", p=P)),
                 (wsm[:, :, :], sgu_w[0].rearrange("g t s -> t g s")),
                 (bs[:, :], sgu_b[0].rearrange("g t -> t g")),
                 (posi[:, :], positions[0].rearrange("(t p) -> p t", p=P))]

        def done_groups(u):
            return sum(-(-(w // H + 1) // 4) for w in range(u + 1))

        block = ctx.enter_context(nc.Block())

        @block.sync
        def _(sp):
            sp.dma_start(gmix[:, :], norm_mix_g.broadcast_to([P, D])).then_inc(gmix_in, 16)
            for t in range(T):
                if t >= 4:
                    sp.wait_ge(xs_ready, t - 3)
                sp.dma_start(xin[:, t % 4, :], x_t[t]).then_inc(x_in[t % 4], 16)
            for s in range(STEPS):
                if s == RAW:
                    for dst, src in SMALL:
                        sp.dma_start(dst, src, allow_slow_non_contiguous=True).then_inc(small_in, 16)
                if s >= RAW:
                    sp.wait_ge(w_lo_done, s - RAW + 1)
                sp.dma_start(w_raw[:, s % RAW, :], w_slice(s)).then_inc(w_in_sem[s % RAW], 16)
                if s == STEPS - 1 - RING:
                    sp.wait_ge(mix_turned, 1)
                    sp.dma_start(h[:, :, :], x[0].rearrange("(t p) d -> p t d", p=P)).then_inc(hx_in, 16)
            sp.wait_ge(w_used, STEPS)
            for c in range(CHUNKS):
                sp.dma_start(by_row(ew_raw, c), expert_chunk(0, c)).then_inc(ew_in[c], 16)
            with sp.Fori(0, NE - 1) as i:
                for c in range(CHUNKS):
                    sp.wait_ge(chunk_used, CHUNKS * i + c + 1)
                    sp.dma_start(by_row(ew_raw, c), expert_chunk(i + 1, c)).then_inc(ew_in[c], 16)
            sp.wait_ge(eid_ready, 2)
            with sp.Fori(0, OVER) as o:
                e = sp.value_load(eidi[0:1, 0, bass.ds(o, 1)], min_val=0, max_val=NE)
                with sp.If(e < NE):
                    weights = sp.value_load(eidi[0:1, 1, bass.ds(o, 1)], min_val=0, max_val=NE - 1)
                    for c in range(CHUNKS):
                        sp.wait_ge(chunk_used, CHUNKS * (NE - 1) + CHUNKS * o + c + 1)
                        sp.dma_start(by_row(ew_raw, c), expert_chunk(weights, c)).then_inc(ew_in[c], 16)
            sp.wait_ge(moe_done, 1)
            for t in range(T):
                sp.dma_start(yin[:, t, :, :], y_t[t]).then_inc(yin_sem[t], 16)
            for t in range(T):
                sp.wait_ge(h2_done, t + 1)
                sp.dma_start(out_t[t], h[:, t, :]).then_inc(out_done, 16)
            sp.wait_ge(out_done, 16 * T)

        @block.gpsimd
        def _(pool):
            steps = [0]

            def link(ins):
                steps[0] += 1
                ins.then_inc(pool_step, 1)
                pool.wait_ge(pool_step, steps[0])

            pool.memset(onesb[:, :], 1.0).then_inc(made, 1)
            link(pool.memset(ident[:, :], 0.0))
            pool.affine_select(out=ident[:, :], in_=ident[:, :], compare_op=ALU.not_equal, fill=1.0, base=0,
                               pattern=[[-1, P]], channel_multiplier=1).then_inc(made, 1)
            link(pool.memset(identb[:, :], 0.0))
            pool.affine_select(out=identb[:, :], in_=identb[:, :], compare_op=ALU.not_equal, fill=1.0, base=0,
                               pattern=[[-1, P]], channel_multiplier=1).then_inc(made, 1)
            link(pool.memset(causal[:, :], 0.0))
            pool.affine_select(out=causal[:, :], in_=causal[:, :], compare_op=ALU.is_ge, fill=NEG, base=0,
                               pattern=[[-1, P]], channel_multiplier=1).then_inc(made, 1)
            link(pool.memset(earlier[:, :], 1.0))
            pool.affine_select(out=earlier[:, :], in_=earlier[:, :], compare_op=ALU.is_gt, fill=0.0, base=0,
                               pattern=[[1, P]], channel_multiplier=-1).then_inc(made, 1)
            link(pool.memset(half[:, :], -0.5))

            def rstd(dst, src, n):
                link(pool.tensor_scalar(dst, src, 1.0 / n, EPS, ALU.mult, ALU.add))
                return pool.tensor_tensor(dst, dst, half[:, 0:dst.shape[1]], ALU.pow)

            for t in range(T):
                pool.wait_ge(ss_ready, t + 1)
                rstd(rs[:, t:t + 1], ss[:, t:t + 1], D).then_inc(rs_ready, 1)
            pool.wait_ge(small_in, 16 * len(SMALL))
            pool.affine_select(out=wsm[:, :, :], in_=wsm[:, :, :], compare_op=ALU.is_ge, fill=0.0, base=0,
                               pattern=[[0, G], [-1, P]], channel_multiplier=1).then_inc(ws_masked, 1)
            pool.tensor_scalar(gq[:, :], gq[:, :], DH ** -0.5, None, ALU.mult).then_inc(consts_done, 1)
            pool.tensor_scalar(gatt[:, :], gatt[:, :], 1.0 - LAMBDA_INIT, None, ALU.mult).then_inc(consts_done, 1)
            pool.wait_ge(consts_done, 2)

            for t in range(T):
                pool.wait_ge(mv_ready, t + 1)
                link(rstd(lnr[:, 0:1], mv[:, t, 1:2], 1))
                link(pool.tensor_tensor(lnr[:, 1:2], mv[:, t, 0:1], lnr[:, 0:1], ALU.mult))
                link(pool.tensor_scalar(lnr[:, 1:2], lnr[:, 1:2], -1.0, None, ALU.mult))
                link(pool.tensor_scalar(sv[:, t, :], sv[:, t, :], lnr[:, 0:1], lnr[:, 1:2], ALU.mult, ALU.add))
                link(pool.tensor_tensor(sv[:, t, :], sv[:, t, :], lng[:, :], ALU.mult))
                pool.tensor_tensor(sv[:, t, :], sv[:, t, :], lnb[:, :], ALU.add).then_inc(sv_done, 1)

            rotated = [0]

            def rotate(n):
                t = n % T
                mt = (q, k)[n // T][:, t, :].rearrange("p (g d) -> p g d", d=DH)
                x1, x2 = mt[:, :, 0:HALF], mt[:, :, HALF:ROPE]
                c = cs[:, t, :].unsqueeze(1).broadcast_to([P, QK, HALF])
                s = sn[:, t, :].unsqueeze(1).broadcast_to([P, QK, HALF])
                pool.wait_ge(scaled, n + 1)
                if n:
                    pool.wait_ge(qk_done, 2 * n)
                for i, (a, b) in enumerate(((x1, c), (x2, s), (x1, s), (x2, c))):
                    steps[0] += 1
                    pool.tensor_tensor(rp[:, i], a, b, ALU.mult).then_inc(pool_step, 1)
                pool.wait_ge(pool_step, steps[0])
                pool.tensor_tensor(x1, rp[:, 0], rp[:, 1], ALU.subtract).then_inc(qk_done, 1)
                pool.tensor_tensor(x2, rp[:, 2], rp[:, 3], ALU.add).then_inc(qk_done, 1)

            pool.wait_ge(sin_done, 2)
            for n in range(2 * T):
                pool.wait_ge(sums_done, n + 1)
                if n >= 2:
                    pool.wait_ge(scaled, n - 1)
                rstd(inv[:, n % 2, :], sums[:, n % 2, :], DH).then_inc(inv_done, 1)
                if n:
                    rotate(n - 1)
            rotate(2 * T - 1)

            normed = [(m, t) for m in (su, att) for t in range(T)]

            def squares(i):
                m, t = normed[i]
                if m is su:
                    pool.wait_ge(sg_gated, 2 * G if t >= T // 2 else G)
                else:
                    pool.wait_ge(o_done, H * (t + 1))
                pool.tensor_tensor(sq[:, i % 2, :], m[:, t, :], m[:, t, :], ALU.mult).then_inc(sq_done, 1)

            for i, (m, t) in enumerate(normed):
                if t == 0 or m is att:
                    squares(i)
                if t + 1 < T and m is su:
                    squares(i + 1)
                mt = m[:, t, :].rearrange("p (g d) -> p g d", d=P)
                r = inv[:, i % 2, 0:H]
                pool.wait_ge(sums_done, 2 * T + i + 1)
                link(rstd(r, sums[:, i % 2, 0:H], P))
                link(pool.tensor_tensor(mt, mt, r.unsqueeze(2).broadcast_to([P, H, P]), ALU.mult))
                if m is su:
                    pool.tensor_tensor(su[:, t, :], su[:, t, :], gsgu[:, :], ALU.mult).then_inc(sg_done, 1)
                else:
                    pool.tensor_tensor(mt, mt, gatt[:, :].unsqueeze(1).broadcast_to([P, H, P]), ALU.mult)\
                        .then_inc(att_done, 1)

            for t in range(T):
                pool.wait_ge(ss2_ready, t + 1)
                rstd(rs2[:, t:t + 1], ss2[:, t:t + 1], D).then_inc(rs2_ready, 1)
            pool.wait_ge(w_used, STEPS)
            pool.memset(init[:, :], EMPTY).then_inc(init_ready, 1)
            pool.wait_ge(init_ready, 1)
            pool.dma_start(table_dram.rearrange("(p a) c -> p (a c)", p=P), init[:, :]).then_inc(table_init, 16)
            pool.iota(revg[:, :], pattern=[[-1, NG]], base=NG, channel_multiplier=0,
                      allow_small_or_imprecise_dtypes=True).then_inc(rtab, 1)
            pool.iota(reve[:, :], pattern=[[-1, NE]], base=NE, channel_multiplier=0,
                      allow_small_or_imprecise_dtypes=True).then_inc(rtab, 1)
            pool.iota(ecol[:, :], pattern=[[1, NE]], base=0, channel_multiplier=0,
                      allow_small_or_imprecise_dtypes=True).then_inc(rtab, 1)
            pool.iota(thr[:, :], pattern=[[P, NTHR]], base=P, channel_multiplier=0,
                      allow_small_or_imprecise_dtypes=True).then_inc(rtab, 1)
            pool.iota(ocol[:, :], pattern=[[1, OVER + 1]], base=0, channel_multiplier=0,
                      allow_small_or_imprecise_dtypes=True).then_inc(rtab, 1)
            pool.iota(pairs[:, :, :, 0], pattern=[[0, 2], [P, T]], base=0, channel_multiplier=1).then_inc(rtab, 1)
            pool.iota(pairs[:, :, :, 1], pattern=[[SEQ, 2], [P, T]], base=0, channel_multiplier=1).then_inc(rtab, 1)
            link(pool.memset(tri[:, :, :], 1.0))
            pool.affine_select(out=tri[:, :, :], in_=tri[:, :, :], compare_op=ALU.is_ge, fill=0.0, base=0,
                               pattern=[[1, NE], [-1, NE]], channel_multiplier=0).then_inc(rtab, 1)
            pool.memset(xg[:, :], 0.0).then_inc(zeroed, 1)
            pool.wait_ge(zeroed, 1)
            pool.wait_ge(table_init, 16)
            pool.wait_ge(slots_ready, 1)
            pool.wait_ge(rtab, 8)
            for c in range(2):
                for t in range(T):
                    pool.indirect_dma_start(
                        out=table_dram, out_offset=bass.IndirectOffsetOnAxis(ap=sloti[:, c, t:t + 1], axis=0),
                        in_=pairs[:, c, t, :], in_offset=None).then_inc(table_out, 16)
            pool.wait_ge(table_out, 16 * 2 * T)
            pool.dma_start(slots[:, :, :], table_dram.rearrange("(p a) c -> p a c", p=P)).then_inc(slots_in, 16)
            pool.wait_ge(slots_in, 16)
            last_token, last_row = pool.to_reg(SEQ - 1), pool.to_reg(2 * SEQ - 1)

            def fetch_rows(i, is_set, times):
                pool.tensor_copy(idx1[:, :], slots[:, bass.ds(i, 1), 0]).then_inc(is_set, 1)
                for b in range(2):
                    pool.wait_ge(hn2_out[b], 16 * T // 2)
                pool.wait_ge(is_set, times)
                pool.indirect_dma_start(
                    out=xg[:, :], out_offset=None, in_=hn2_dram,
                    in_offset=bass.IndirectOffsetOnAxis(ap=idx1[:, 0:1], axis=0),
                    bounds_check=last_token, oob_is_err=False).then_inc(rows_in, 16)

            def tile(n):
                pool.wait_ge(rows_turned, n + 1)
                pool.tensor_copy(idx2[:, :], slots[:, bass.ds(n - 1, 1), 1]).then_inc(idx2_set, 1)
                fetch_rows(n + 1, idx1_set, n)
                pool.wait_ge(slots_in, 16)
                pool.wait_ge(ya_done, n)
                pool.wait_ge(yb_done, n)
                pool.wait_ge(idx2_set, n)
                pool.indirect_dma_start(
                    out=y_dram, out_offset=bass.IndirectOffsetOnAxis(ap=idx2[:, 0:1], axis=0),
                    in_=y[:, :], in_offset=None,
                    bounds_check=last_row, oob_is_err=False).then_inc(y_out, 16)
                pool.wait_ge(rows_in, 16 * n + 32)
                pool.wait_ge(y_out, 16 * n)

            fetch_rows(0, idx_first, 1)
            pool.wait_ge(rows_turned, 1)
            pool.wait_ge(rows_in, 16)
            fetch_rows(1, idx_first, 2)
            pool.wait_ge(rows_in, 32)
            with pool.Fori(1, NE + 1) as n:
                tile(n)
            pool.wait_ge(eid_ready, 2)
            with pool.Fori(NE + 1, NE + 1 + OVER) as n:
                e = pool.value_load(eidi[0:1, 0, bass.ds(n - (NE + 1), 1)], min_val=0, max_val=NE)
                with pool.If(e < NE):
                    tile(n)
            pool.memset(idx2[:, :], 0).then_inc(moe_done, 1)

        @block.scalar
        def _(act):
            def copy(dst, src):
                return nc.scalar.activation(dst, src, ACT.Copy)

            def square_x(t):
                act.wait_ge(x_in[t % 4], 16 * (t // 4 + 1))
                if t:
                    act.wait_ge(ss_ready, t)
                nc.scalar.activation(sq1[:, :], xin[:, t % 4, :], ACT.Square,
                                     accum_out=ss[:, t:t + 1]).then_inc(ss_ready, 1)

            def split_w(s):
                act.wait_ge(w_in_sem[s % RAW], 16 * (s // RAW + 1))
                if s >= RING:
                    act.wait_ge(w_used, s - RING + 1)
                copy(w_hi[:, s % RING, :], w_raw[:, s % RAW, :]).then_inc(w_hi_done, 1)

            square_x(0)
            for t in range(T):
                if t + 1 < T:
                    square_x(t + 1)
                act.wait_ge(x_turned, t + 1)
                copy(hn_hi[:, :, P * t:P * t + P], PS[t % 2][:, :].rearrange("p (k n) -> p k n", n=P))\
                    .then_inc(hn_hi_done, 1)
            for s in range(RING):
                split_w(s)
            act.wait_ge(rope_arg, 2)
            nc.scalar.activation(sn[:, :, :], ang[:, 2], ACT.Sin).then_inc(sin_done, 1)
            nc.scalar.activation(cs[:, :, :], ang[:, 3], ACT.Sin).then_inc(sin_done, 1)
            act.wait_ge(lam_dot, 1)
            nc.scalar.activation(lam[:, 2:4], lam[:, 0:2], ACT.Exp).then_inc(lam_exp, 1)

            def evacuate(j):
                for t in range(T):
                    if t < T - 1:
                        act.wait_ge(acc_ready, (T - 1) * j + t + 1)
                    else:
                        act.wait_ge(w_used, KD * (j + 1))
                    dst = {SV: sv, SU: su, Q: q, K: k, V: v}[j]
                    nc.scalar.activation(dst[:, t, :], bank(t), ACT.Gelu if j in (SV, SU) else ACT.Copy)\
                        .then_inc(acc_out, 1)

            for s in range(STEPS_IN):
                if s % KD == KD - 1:
                    evacuate(s // KD)
                split_w(s + RING)
            for t in range(T):
                act.wait_ge(qk_turned, 2 * t + 1)
                copy(qT[:, :, P * t:P * t + P], bank(6).rearrange("p (h n) -> p h n", n=P)).then_inc(qT_done, 1)

            def exponentials(u, m):
                n = u // H + 1
                act.wait_ge(max_done, 2 * u + m + 1)
                if u >= PROBS:
                    act.wait_ge(a_turned, done_groups(u - PROBS))
                nc.scalar.activation(prob[:, u % PROBS, m, 0:P * n], PS[(2 * u + m) % 3][:, 0:P * n], ACT.Exp,
                                     bias=nmax[:, 2 * u + m:2 * u + m + 1],
                                     accum_out=lsum[:, u, m:m + 1]).then_inc(exp_done, 1)

            def turned_out(u, group):
                w = min(4, u // H + 1 - 4 * group)
                act.wait_ge(a_turned, done_groups(u - 1) + group + 1)
                if u >= 2:
                    act.wait_ge(o_ready, u - 1)
                copy(probT[:, u % 2, 4 * group:4 * group + w, :],
                     bank(6)[:, 0:P * w].rearrange("p (k n) -> p k n", n=P)).then_inc(aT_done, 1)

            exponentials(0, 0)
            exponentials(0, 1)
            for u in range(H * T):
                if u + 1 < H * T:
                    exponentials(u + 1, 0)
                turned_out(u, 0)
                if u + 1 < H * T:
                    exponentials(u + 1, 1)
                if u >= H * T // 2:
                    turned_out(u, 1)

            for t in range(T):
                act.wait_ge(mix_turned, t + 1)
                copy(mix_hi[:, :, P * t:P * t + P], PS[t % 2][:, :].rearrange("p (k n) -> p k n", n=P))\
                    .then_inc(mix_hi_done, 1)
            for s in range(STEPS_IN + RING, STEPS):
                split_w(s)

            for t in range(T):
                act.wait_ge(h_ready, T + t + 1)
                if t:
                    act.wait_ge(ss2_ready, t)
                nc.scalar.activation(sq2[:, :], h[:, t, :], ACT.Square,
                                     accum_out=ss2[:, t:t + 1]).then_inc(ss2_ready, 1)
            for t in range(T):
                act.wait_ge(hn2_ready, t + 1)
                act.dma_start(hn2_dram[P * t:P * t + P, :], hn2[:, t % 2, :]).then_inc(hn2_out[t % 2], 16)
                act.wait_ge(h_turned, t + 1)
                if t:
                    act.wait_ge(logits, t)
                copy(hnT2[:, :, :], PS[t % 2][:, :].rearrange("p (k n) -> p k n", n=P)).then_inc(hT_done, 1)
            act.wait_ge(gd_ready, 1)
            nc.scalar.activation(gexp[:, :, :], gd[:, :, :], ACT.Exp).then_inc(gexp_done, 1)
            act.wait_ge(dm_ready, 1)
            nc.scalar.activation(r8["e2"][:, :], r8["dm"][:, :], ACT.Exp).then_inc(e2_done, 1)

            def split_chunks(i, chunks):
                for c in chunks:
                    act.wait_ge(ew_in[c], 16 * i + 16)
                    copy(ew_hi[:, c, :], ew_raw[:, c, :]).then_inc(ew_hi_done, 1)

            def turn_rows(i):
                act.wait_ge(rows_turned, i + 1)
                copy(xT_hi[:, :, :], PS[1][:, :].rearrange("p (k n) -> p k n", n=P)).then_inc(xT_hi_done, 1)

            def tile(i, ahead):
                act.wait_ge(chunk_used, CHUNKS * i + 2)
                nc.scalar.activation(gact[:, :], bank(0), ACT.Silu).then_inc(silu_done, 1)
                split_chunks(i, range(AHEAD, CHUNKS))
                act.wait_ge(hid_turned, i + 1)
                copy(actT_hi[:, :, :], bank(4).rearrange("p (k n) -> p k n", n=P)).then_inc(actT_hi_done, 1)
                turn_rows(i + 1)
                if ahead:
                    split_chunks(i + 1, range(AHEAD - 1))
                act.wait_ge(chunk_used, CHUNKS * i + CHUNKS)
                act.wait_ge(idx2_set, i + 1)
                copy(y[:, 0:BANK], bank(6)).then_inc(ya_done, 1)
                if ahead:
                    split_chunks(i + 1, range(AHEAD - 1, AHEAD))

            act.wait_ge(w_used, STEPS)
            split_chunks(0, range(AHEAD))
            turn_rows(0)
            with act.Fori(0, NE - 1) as i:
                tile(i, True)
            tile(NE - 1, False)
            act.wait_ge(eid_ready, 2)
            with act.Fori(0, OVER) as o:
                e = act.value_load(eidi[0:1, 0, bass.ds(o, 1)], min_val=0, max_val=NE)
                with act.If(e < NE):
                    split_chunks(o + NE, range(AHEAD))
                    tile(o + NE, False)

        @block.vector
        def _(dve):
            steps = [0]

            def link(ins):
                steps[0] += 1
                ins.then_inc(dve_step, 1)
                dve.wait_ge(dve_step, steps[0])

            def residual(j):
                dve.wait_ge(hx_in, 16)
                for t in range(T):
                    if t < T - 1:
                        dve.wait_ge(acc_ready, (T - 1) * (NB_IN + j) + t + 1)
                    else:
                        dve.wait_ge(w_used, STEPS_IN + KD * (j + 1))
                    dst = h[:, t, WB * j:WB * j + WB]
                    dve.tensor_tensor(dst, bank(t), dst, ALU.add).then_inc(h_ready, 1)

            def take_logits(t):
                dve.wait_ge(logits, t + 1)
                dve.tensor_tensor(lg[:, t, :], bank(4 + t % 2)[:, 0:NG + NE], rbias[:, :], ALU.add).then_inc(lg_done, 1)

            dve.wait_ge(gmix_in, 16)

            def scale_x(t):
                dve.wait_ge(rs_ready, t + 1)
                if t >= 2:
                    dve.wait_ge(x_turned, t - 1)
                dve.scalar_tensor_tensor(out=xs[:, t % 2, :], in0=xin[:, t % 4, :], scalar=rs[:, t:t + 1],
                                         in1=gmix[:, :], op0=ALU.mult, op1=ALU.mult).then_inc(xs_ready, 1)

            def lower(dst, turned, hi, t):
                return dve.tensor_tensor(dst[:, :, P * t:P * t + P],
                                         turned.rearrange("p (k n) -> p k n", n=P),
                                         hi[:, :, P * t:P * t + P].bitcast(F32), ALU.subtract)

            scale_x(0)
            for t in range(T):
                if t + 1 < T:
                    scale_x(t + 1)
                dve.wait_ge(hn_hi_done, t + 1)
                lower(hn_lo, PS[t % 2][:, :], hn_hi, t).then_inc(hn_lo_done, 1)

            def split_w(s):
                dve.wait_ge(w_hi_done, s + 1)
                dve.tensor_tensor(w_lo[:, s % RING, :], w_raw[:, s % RAW, :], w_hi[:, s % RING, :].bitcast(F32),
                                  ALU.subtract).then_inc(w_lo_done, 1)

            for s in range(RING):
                split_w(s)

            dve.wait_ge(small_in, 16 * len(SMALL))
            link(dve.tensor_copy(posf[:, :], posi[:, :]))
            for i in range(HALF):
                link(dve.tensor_scalar(ang[:, 0, :, i], posf[:, :], float(np.float32(THETA ** (-2.0 * i / ROPE))), None,
                                       ALU.mult))
            a0, turns, a2, a3 = (ang[:, i] for i in range(4))
            ROUND = 1.5 * 2.0 ** 23
            T1, T2 = 6.28125, 0.001934051513671875
            T3 = 2 * np.pi - T1 - T2
            link(dve.tensor_scalar(turns, a0, 1 / (2 * np.pi), None, ALU.mult))
            link(dve.tensor_scalar(turns, turns, ROUND, None, ALU.add))
            link(dve.tensor_scalar(turns, turns, ROUND, None, ALU.subtract))
            for c in (T1, T2, float(np.float32(T3))):
                link(dve.scalar_tensor_tensor(out=a0, in0=turns, scalar=-c, in1=a0, op0=ALU.mult, op1=ALU.add))
            LIM = 3.1415925
            dve.tensor_scalar(a2, a0, LIM, -LIM, ALU.min, ALU.max).then_inc(rope_arg, 1)
            link(dve.tensor_scalar(turns, a0, np.pi / 2, None, ALU.is_gt))
            link(dve.tensor_scalar(a3, a0, np.pi / 2, None, ALU.add))
            link(dve.scalar_tensor_tensor(out=a3, in0=turns, scalar=-2 * np.pi, in1=a3, op0=ALU.mult, op1=ALU.add))
            dve.tensor_scalar(a3, a3, LIM, -LIM, ALU.min, ALU.max).then_inc(rope_arg, 1)
            link(dve.tensor_tensor(lam4[:, 0:2, :], lam4[:, 0:2, :], lam4[:, 2:4, :], ALU.mult))
            dve.reduce_sum(lam[:, 0:2], lam4[:, 0:2, :], AX.X).then_inc(lam_dot, 1)
            dve.wait_ge(lam_exp, 1)
            link(dve.tensor_tensor(lam[:, 4:5], lam[:, 3:4], lam[:, 2:3], ALU.subtract))
            link(dve.tensor_scalar(lam[:, 5:6], lam[:, 4:5], -LAMBDA_INIT, None, ALU.add))
            dve.wait_ge(ws_turned, 1)
            dve.tensor_copy(wsT[:, :, :], bank(7).rearrange("p (g n) -> p g n", n=P)).then_inc(ws_out, 1)

            def layer_norm(t):
                dve.wait_ge(acc_out, T * SV + t + 1)
                if t:
                    dve.wait_ge(mv_ready, t)
                link(dve.bn_stats(stat[:, :], sv[:, t, :]))
                dve.bn_aggr(mv[:, t, :], stat[:, :]).then_inc(mv_ready, 1)

            def sum_squares(i):
                dve.wait_ge(sq_done, i + 1)
                dve.reduce_sum(sums[:, i % 2, 0:H], sq[:, i % 2, :].rearrange("p (g d) -> p g d", d=P),
                               AX.X).then_inc(sums_done, 1)

            def item(n):
                return (q, k)[n // T][:, n % T, :].rearrange("p (g d) -> p g d", d=DH)

            def norm_sums(n):
                dve.wait_ge(acc_out, T * Q + n + 1)
                if n >= 2:
                    dve.wait_ge(inv_done, n - 1)
                if n:
                    dve.wait_ge(sums_done, n)
                link(dve.tensor_tensor(sq[:, 0, :], item(n), item(n), ALU.mult))
                dve.reduce_sum(sums[:, n % 2, :], sq[:, 0, :].rearrange("p (g d) -> p g d", d=DH), AX.X)\
                    .then_inc(sums_done, 1)

            def scale(n):
                dve.wait_ge(inv_done, n + 1)
                link(dve.tensor_tensor(item(n), item(n), inv[:, n % 2, :].unsqueeze(2).broadcast_to([P, QK, DH]),
                                       ALU.mult))
                dve.tensor_tensor(item(n), item(n), (gq, gk)[n // T][:, :].unsqueeze(1).broadcast_to([P, QK, DH]),
                                  ALU.mult).then_inc(scaled, 1)

            dve.wait_ge(consts_done, 2)
            for s in range(STEPS_IN):
                j, t = s // KD, s % KD
                split_w(s + RING)
                if j == SV + 1:
                    layer_norm(t)
                if j > Q:
                    n = s - KD * (Q + 1)
                    norm_sums(n)
                    if n:
                        scale(n - 1)
            scale(2 * T - 1)

            for i in range(2 * G):
                c0, g = T // 2 * (i // G), i % G
                dve.wait_ge(sg_ready, i + 1)
                dst = su[:, c0:c0 + T // 2, P * g:P * g + P]
                dve.scalar_tensor_tensor(out=dst, in0=bank(i % 6).rearrange("p (c d) -> p c d", d=P),
                                         scalar=bs[:, g:g + 1], in1=dst, op0=ALU.add, op1=ALU.mult)\
                    .then_inc(sg_gated, 1)

            for t in range(T):
                dve.wait_ge(qk_turned, 2 * t + 2)
                dve.tensor_copy(kT[:, :, P * t:P * t + P], bank(7).rearrange("p (h n) -> p h n", n=P))\
                    .then_inc(kT_done, 1)

            def maximum(u, m):
                n = u // H + 1
                dve.wait_ge(s_ready, 2 * u + m + 1)
                dve.tensor_reduce(nmax[:, 2 * u + m:2 * u + m + 1], PS[(2 * u + m) % 3][:, 0:P * n], AX.X, ALU.max,
                                  negate=True).then_inc(max_done, 1)

            def combine(u):
                n = u // H + 1
                dve.wait_ge(exp_done, 2 * u + 2)
                link(dve.reciprocal(linv[:, u, :], lsum[:, u, :]))
                link(dve.scalar_tensor_tensor(out=mixc[:, u:u + 1], in0=lsum[:, u, 0:1], scalar=lam[:, 5:6],
                                              in1=linv[:, u, 1:2], op0=ALU.mult, op1=ALU.mult))
                dve.scalar_tensor_tensor(out=prob[:, u % PROBS, 0, 0:P * n], in0=prob[:, u % PROBS, 1, 0:P * n],
                                         scalar=mixc[:, u:u + 1], in1=prob[:, u % PROBS, 0, 0:P * n],
                                         op0=ALU.mult, op1=ALU.add).then_inc(a_ready, 1)

            def head_out(u):
                t, hd = u // H, u % H
                dve.wait_ge(o_ready, u + 1)
                dve.tensor_scalar(att[:, t, P * hd:P * hd + P], bank(7)[:, 0:P], linv[:, u, 0:1], None, ALU.mult)\
                    .then_inc(o_done, 1)

            maximum(0, 0)
            maximum(0, 1)
            maximum(1, 0)
            for u in range(H * T):
                if u + 1 < H * T:
                    maximum(u + 1, 1)
                combine(u)
                if u + 2 < H * T:
                    maximum(u + 2, 0)
                if u >= 2:
                    head_out(u - 2)
                if H <= u < H + T:
                    sum_squares(u - H)
                if u % H == 3 and u > 3 * H:
                    sum_squares(T + u // H - 3)
            head_out(H * T - 2)
            head_out(H * T - 1)
            for i in range(3, 0, -1):
                sum_squares(2 * T - i)

            for t in range(T):
                dve.wait_ge(mix_hi_done, t + 1)
                lower(mix_lo, PS[t % 2][:, :], mix_hi, t).then_inc(mix_lo_done, 1)
            for s in range(STEPS_IN + RING, STEPS):
                if s - RING == STEPS_IN + KD - 1:
                    residual(0)
                split_w(s)
            residual(1)

            for t in range(T):
                dve.wait_ge(rs2_ready, t + 1)
                if t >= 2:
                    dve.wait_ge(hn2_out[t % 2], 16 * (t // 2))
                    dve.wait_ge(h_turned, t - 1)
                dve.scalar_tensor_tensor(out=hn2[:, t % 2, :], in0=h[:, t, :], scalar=rs2[:, t:t + 1],
                                         in1=gffn[:, :], op0=ALU.mult, op1=ALU.mult).then_inc(hn2_ready, 1)
                if t:
                    take_logits(t - 1)
            take_logits(T - 1)
            dve.wait_ge(lg_done, T)

            dve.wait_ge(rtab, 8)
            R8 = {n: m[:, :] for n, m in r8.items()}

            def over(m, shape):
                return m.unsqueeze(2).broadcast_to(shape)

            gs, es = [P, T, NG], [P, T, NE]
            link(dve.tensor_reduce(R8["gmax"], lg[:, :, 0:NG], AX.X, ALU.max))
            dve.tensor_tensor(gd[:, :, :], lg[:, :, 0:NG], over(R8["gmax"], gs), ALU.subtract).then_inc(gd_ready, 1)
            dve.wait_ge(gd_ready, 1)
            link(dve.scalar_tensor_tensor(out=grk[:, :, :], in0=gd[:, :, :], scalar=0.0,
                                          in1=revg[:, :].unsqueeze(1).broadcast_to(gs),
                                          op0=ALU.is_equal, op1=ALU.mult))
            link(dve.tensor_reduce(R8["grank"], grk[:, :, :], AX.X, ALU.max))
            link(dve.tensor_tensor(pen[:, :, :], grk[:, :, :], over(R8["grank"], gs), ALU.is_equal))
            link(dve.tensor_scalar(pen[:, :, :], pen[:, :, :], -1.0, -NEG, ALU.add, ALU.mult))
            link(dve.tensor_tensor(ev[:, :, :].rearrange("p t (g e) -> p t g e", e=EG),
                                   lg[:, :, NG:].rearrange("p t (g e) -> p t g e", e=EG),
                                   pen[:, :, :].unsqueeze(3).broadcast_to([P, T, NG, EG]), ALU.add))
            for m, r, oh in (("m1", "r1", oh1), ("m2", "r2", oh2)):
                link(dve.tensor_reduce(R8[m], ev[:, :, :], AX.X, ALU.max))
                link(dve.tensor_tensor(rk[:, :, :], ev[:, :, :], over(R8[m], es), ALU.is_equal))
                link(dve.tensor_tensor(rk[:, :, :], rk[:, :, :], reve[:, :].unsqueeze(1).broadcast_to(es), ALU.mult))
                link(dve.tensor_reduce(R8[r], rk[:, :, :], AX.X, ALU.max))
                link(dve.tensor_tensor(oh[:, :, :], rk[:, :, :], over(R8[r], es), ALU.is_equal))
                if m == "m1":
                    link(dve.scalar_tensor_tensor(out=ev[:, :, :], in0=oh[:, :, :], scalar=4 * NEG, in1=ev[:, :, :],
                                                  op0=ALU.mult, op1=ALU.add))
            dve.tensor_tensor(cnt[:, :, :], oh1[:, :, :], oh2[:, :, :], ALU.add).then_inc(cnt_ready, 1)
            dve.tensor_tensor(R8["dm"], R8["m2"], R8["m1"], ALU.subtract).then_inc(dm_ready, 1)

            dve.memset(total[:, 0, :], 0.0).then_inc(dve_step, 1)
            steps[0] += 1
            dve.wait_ge(counted, 1)
            dve.wait_ge(dve_step, steps[0])
            for t in range(T):
                link(dve.tensor_tensor(total[:, t + 1, :], total[:, t, :],
                                       bank(7)[:, NE * t:NE * t + NE], ALU.add))
            link(dve.tensor_tensor(pos[:, :, :], bank(6)[:, 0:T * NE].rearrange("p (t e) -> p t e", e=NE),
                                   total[:, 0:T, :], ALU.add))
            link(dve.tensor_tensor(cmpt[:, :, 0:NTHR], total[:, T, :].unsqueeze(2).broadcast_to([P, NE, NTHR]),
                                   thr[:, :].unsqueeze(1).broadcast_to([P, NE, NTHR]), ALU.is_gt))
            link(dve.reduce_sum(nover[:, :], cmpt[:, :, 0:NTHR], AX.X))
            link(dve.tensor_tensor(cmpt[:, :, :], tri[:, :, :], nover[:, :].unsqueeze(1).broadcast_to([P, NE, NE]),
                                   ALU.mult))
            link(dve.reduce_sum(cum[:, :], cmpt[:, :, :], AX.X))
            link(dve.tensor_tensor(cmpt[:, 0:OVER + 1, :], cum[:, :].unsqueeze(1).broadcast_to([P, OVER + 1, NE]),
                                   ocol[:, :].unsqueeze(2).broadcast_to([P, OVER + 1, NE]), ALU.is_le))
            link(dve.reduce_sum(eid[:, :], cmpt[:, 0:OVER + 1, :], AX.X))
            link(dve.tensor_tensor(offs[:, :], cum[:, :], nover[:, :], ALU.subtract))
            link(dve.tensor_tensor(offs[:, :], offs[:, :], ecol[:, :], ALU.subtract))
            link(dve.tensor_scalar(offs[:, :], offs[:, :], float(NE - 1), None, ALU.add))
            link(dve.tensor_copy(posn[:, :, :], pos[:, :, :]))
            link(dve.tensor_scalar(qti[:, :, :], posn[:, :, :], 7, None, ALU.arith_shift_right))
            link(dve.tensor_copy(qt[:, :, :], qti[:, :, :]))
            link(dve.tensor_tensor(ev[:, :, :], qt[:, :, :], offs[:, :].unsqueeze(1).broadcast_to(es), ALU.add))
            link(dve.tensor_scalar(rk[:, :, :], qt[:, :, :], 0.0, None, ALU.is_gt))
            link(dve.tensor_tensor(ev[:, :, :], ev[:, :, :], rk[:, :, :], ALU.mult))
            link(dve.scalar_tensor_tensor(out=ev[:, :, :], in0=pos[:, :, :], scalar=float(NT), in1=ev[:, :, :],
                                          op0=ALU.mult, op1=ALU.add))
            link(dve.scalar_tensor_tensor(out=ev[:, :, :], in0=qt[:, :, :], scalar=float(-P * NT), in1=ev[:, :, :],
                                          op0=ALU.mult, op1=ALU.add))
            link(dve.tensor_tensor(ev[:, :, :], ev[:, :, :], ecol[:, :].unsqueeze(1).broadcast_to(es), ALU.add))
            for oh, s in ((oh1, "slot1"), (oh2, "slot2")):
                link(dve.tensor_tensor(rk[:, :, :], oh[:, :, :], ev[:, :, :], ALU.mult))
                link(dve.reduce_sum(R8[s], rk[:, :, :], AX.X))
            link(dve.tensor_copy(sloti[:, 0, :], R8["slot1"]))
            dve.tensor_copy(sloti[:, 1, :], R8["slot2"]).then_inc(slots_ready, 1)
            dve.tensor_copy(eidi[:, 0, :], eid[:, :]).then_inc(eid_ready, 1)
            dve.tensor_scalar(eidi[:, 1, :], eid[:, :], float(NE - 1), None, ALU.min).then_inc(eid_ready, 1)
            dve.wait_ge(gexp_done, 1)
            link(dve.reduce_sum(R8["gsum"], gexp[:, :, :], AX.X))
            dve.wait_ge(e2_done, 1)
            link(dve.tensor_scalar(R8["den"], R8["e2"], 1.0, None, ALU.add))
            link(dve.tensor_tensor(R8["den"], R8["den"], R8["gsum"], ALU.mult))
            link(dve.reciprocal(R8["gate1"], R8["den"]))
            link(dve.tensor_tensor(R8["gate2"], R8["gate1"], R8["e2"], ALU.mult))

            def split_chunks(i, chunks):
                for c in chunks:
                    dve.wait_ge(ew_hi_done, CHUNKS * i + c + 1)
                    dve.tensor_tensor(ew_lo[:, c, :], ew_raw[:, c, :], ew_hi[:, c, :].bitcast(F32), ALU.subtract)\
                        .then_inc(ew_lo_done, 1)

            def turn_rows(i):
                dve.wait_ge(xT_hi_done, i + 1)
                dve.tensor_tensor(xT_lo[:, :, :], PS[1][:, :].rearrange("p (k n) -> p k n", n=P),
                                  xT_hi[:, :, :].bitcast(F32), ALU.subtract).then_inc(xT_lo_done, 1)

            def tile(i, ahead):
                split_chunks(i, range(AHEAD, CHUNKS))
                dve.wait_ge(chunk_used, CHUNKS * i + 4)
                dve.wait_ge(silu_done, i + 1)
                dve.tensor_tensor(hid[:, :], bank(1), gact[:, :], ALU.mult).then_inc(hid_done, 1)
                dve.wait_ge(actT_hi_done, i + 1)
                dve.tensor_tensor(actT_lo[:, :, :], bank(4).rearrange("p (k n) -> p k n", n=P),
                                  actT_hi[:, :, :].bitcast(F32), ALU.subtract).then_inc(actT_lo_done, 1)
                turn_rows(i + 1)
                if ahead:
                    split_chunks(i + 1, range(AHEAD - 1))
                dve.wait_ge(chunk_used, CHUNKS * i + CHUNKS)
                dve.wait_ge(idx2_set, i + 1)
                dve.tensor_copy(y[:, BANK:], bank(7)).then_inc(yb_done, 1)
                if ahead:
                    split_chunks(i + 1, range(AHEAD - 1, AHEAD))

            split_chunks(0, range(AHEAD))
            turn_rows(0)
            with dve.Fori(0, NE - 1) as i:
                tile(i, True)
            tile(NE - 1, False)
            with dve.Fori(0, OVER) as o:
                e = dve.value_load(eidi[0:1, 0, bass.ds(o, 1)], min_val=0, max_val=NE)
                with dve.If(e < NE):
                    split_chunks(o + NE, range(AHEAD))
                    tile(o + NE, False)

            for t in range(T):
                dve.wait_ge(yin_sem[t], 16)
                dve.scalar_tensor_tensor(out=h[:, t, :], in0=yin[:, t, 0, :], scalar=r8["gate1"][:, t:t + 1],
                                         in1=h[:, t, :], op0=ALU.mult, op1=ALU.add).then_inc(h1_done, 1)
                dve.wait_ge(h1_done, t + 1)
                dve.scalar_tensor_tensor(out=h[:, t, :], in0=yin[:, t, 1, :], scalar=r8["gate2"][:, t:t + 1],
                                         in1=h[:, t, :], op0=ALU.mult, op1=ALU.add).then_inc(h2_done, 1)

        @block.tensor
        def _(pe):
            pe.wait_ge(made, 5)

            def turn(dst, src, n=KD):
                for b in range(n):
                    ins = pe.transpose(dst[:, P * b:P * b + P], src[:, P * b:P * b + P], ident[:, :])
                return ins

            for t in range(T):
                pe.wait_ge(xs_ready, t + 1)
                if t >= 2:
                    pe.wait_ge(hn_lo_done, t - 1)
                turn(PS[t % 2][:, :], xs[:, t % 2, :]).then_inc(x_turned, 1)
            pe.wait_ge(ws_masked, 1)
            for g in range(G):
                ins = pe.transpose(bank(7)[:, P * g:P * g + P], wsm[:, g, :], ident[:, :])
            ins.then_inc(ws_turned, 1)
            pe.wait_ge(hn_lo_done, T)

            def project(s, hi, lo):
                j, kk = s // KD, s % KD
                pe.wait_ge(w_lo_done, s + 1)
                for t in range(T):
                    if kk == 0 and j and j != NB_IN:
                        if j < NB_IN:
                            pe.wait_ge(acc_out, T * (j - 1) + t + 1)
                        else:
                            pe.wait_ge(h_ready, t + 1)
                    if s == 0 and t == 7:
                        pe.wait_ge(ws_out, 1)
                    rows = slice(P * t, P * t + P)
                    w = w_hi[:, s % RING, :]
                    pe.matmul(bank(t), lo[:, kk, rows], w, start=(kk == 0), stop=False)
                    pe.matmul(bank(t), hi[:, kk, rows], w_lo[:, s % RING, :], start=False, stop=False)
                    ins = pe.matmul(bank(t), hi[:, kk, rows], w, start=False, stop=(kk == KD - 1))
                    if kk == KD - 1 and t < T - 1:
                        ins.then_inc(acc_ready, 1)
                ins.then_inc(w_used, 1)

            for s in range(STEPS_IN):
                project(s, hn_hi, hn_lo)

            pe.wait_ge(sv_done, T)
            for i in range(2 * G):
                c0, g = T // 2 * (i // G), i % G
                if i < 6:
                    pe.wait_ge(acc_out, T * (NB_IN - 1) + i + 1)
                else:
                    pe.wait_ge(sg_gated, i - 5)
                pe.matmul(bank(i % 6).rearrange("p (c d) -> p c d", d=P), wsT[:, g, :],
                          sv[:, c0:c0 + T // 2, P * g:P * g + P], start=True, stop=True).then_inc(sg_ready, 1)
            pe.wait_ge(acc_out, NB_IN * T)
            for t in range(T):
                pe.wait_ge(qk_done, 2 * (T + t + 1))
                if t:
                    pe.wait_ge(qT_done, t)
                turn(bank(6), q[:, t, :], H).then_inc(qk_turned, 1)
                if t:
                    pe.wait_ge(kT_done, t)
                turn(bank(7), k[:, t, :], H).then_inc(qk_turned, 1)
            pe.wait_ge(qT_done, T)
            pe.wait_ge(kT_done, T)
            pe.wait_ge(sg_gated, 2 * G)

            def scores(u, m):
                t, hd, w = u // H, u % H, 2 * u + m
                n = P * (t + 1)
                if w >= 3:
                    pe.wait_ge(exp_done, w - 2)
                half = slice(DH * m, DH * m + DH)
                for c0 in range(0, n, BANK):
                    c1 = min(n, c0 + BANK)
                    pe.matmul(PS[w % 3][:, c0:c1], qT[half, hd, P * t:P * t + P], kT[half, hd, c0:c1],
                              start=True, stop=(c1 < n))
                pe.matmul(PS[w % 3][:, n - P:n], identb[:, :], causal[:, :], start=False, stop=True)\
                    .then_inc(s_ready, 1)

            def turn_weights(u, group):
                pe.wait_ge(a_ready, u + 1)
                before = done_groups(u - 1) + group
                if before:
                    pe.wait_ge(aT_done, before)
                turn(bank(6), prob[:, u % PROBS, 0, BANK * group:], min(4, u // H + 1 - 4 * group))\
                    .then_inc(a_turned, 1)

            def values(u):
                n, hd = u // H + 1, u % H
                if u:
                    pe.wait_ge(o_done, u)
                pe.wait_ge(aT_done, done_groups(u))
                for b in range(n):
                    ins = pe.matmul(bank(7)[:, 0:P], probT[:, u % 2, b, :], v[:, b, P * hd:P * hd + P],
                                    start=(b == 0), stop=(b == n - 1))
                ins.then_inc(o_ready, 1)

            for u in range(2):
                for m in range(2):
                    scores(u, m)
            for u in range(H * T):
                for group in range(2):
                    if u + 2 < H * T:
                        scores(u + 2, group)
                    if group <= u // H // 4:
                        turn_weights(u, group)
                if u:
                    values(u - 1)
            values(H * T - 1)

            for t in range(T):
                pe.wait_ge(att_done, t + 1)
                pe.wait_ge(sg_done, t + 1)
                pe.wait_ge(exp_done, 2 * H * T)
                if t >= 2:
                    pe.wait_ge(mix_lo_done, t - 1)
                turn(PS[t % 2][:, 0:BANK], att[:, t, :], H)
                turn(PS[t % 2][:, BANK:], su[:, t, :], G).then_inc(mix_turned, 1)
            pe.wait_ge(mix_lo_done, T)
            pe.wait_ge(o_done, H * T)
            for s in range(STEPS_IN, STEPS):
                project(s, mix_hi, mix_lo)

            pe.wait_ge(h_ready, 2 * T)
            for t in range(T):
                pe.wait_ge(hn2_ready, t + 1)
                if t >= 2:
                    pe.wait_ge(hT_done, t - 1)
                turn(PS[t % 2][:, :], hn2[:, t % 2, :]).then_inc(h_turned, 1)
                pe.wait_ge(hT_done, t + 1)
                if t >= 2:
                    pe.wait_ge(lg_done, t - 1)
                for b in range(KD):
                    ins = pe.matmul(bank(4 + t % 2)[:, 0:NG + NE], hnT2[:, b, :], router[:, b, :],
                                    start=(b == 0), stop=(b == KD - 1))
                ins.then_inc(logits, 1)
            pe.wait_ge(cnt_ready, 1)
            flat = cnt[:, :, :].rearrange("p t e -> p (t e)")
            pe.matmul(bank(6)[:, 0:T * NE], earlier[:, :], flat, start=True, stop=True)
            pe.matmul(bank(7)[:, 0:T * NE], onesb[:, :], flat, start=True, stop=True).then_inc(counted, 1)

            def turn_rows(i, part):
                if part == 0:
                    pe.wait_ge(rows_in, 16 * i + 16)
                cols = slice(BANK * part, BANK * part + BANK)
                ins = turn(PS[1][:, cols], xg[:, cols], KD // 2)
                if part:
                    ins.then_inc(rows_turned, 1)

            def product(dst, hi, lo, w_hi, w_lo, first, last):
                pe.matmul(dst, hi, w_hi, start=first, stop=False)
                pe.matmul(dst, hi, w_lo, start=False, stop=False)
                return pe.matmul(dst, lo, w_hi, start=False, stop=last)

            def tile(i):
                pe.wait_ge(xT_lo_done, i + 1)
                for side in range(2):
                    for kk in range(KD):
                        c, row = 2 * side + kk // (KD // 2), kk % (KD // 2)
                        if row == 0:
                            pe.wait_ge(ew_lo_done, CHUNKS * i + c + 1)
                        ins = product(bank(side), xT_hi[:, kk, :], xT_lo[:, kk, :], by_row(ew_hi, c)[:, row, :],
                                      by_row(ew_lo, c)[:, row, :], kk == 0, kk == KD - 1)
                        if row == KD // 2 - 1:
                            ins.then_inc(chunk_used, 1)
                turn_rows(i + 1, 0)
                pe.wait_ge(hid_done, i + 1)
                turn(bank(4), hid[:, :], F // P).then_inc(hid_turned, 1)
                turn_rows(i + 1, 1)
                pe.wait_ge(actT_hi_done, i + 1)
                for kk in range(F // P):
                    c, row = 4 + kk // 2, kk % 2
                    if row == 0:
                        pe.wait_ge(ew_lo_done, CHUNKS * i + c + 1)
                    for b in range(2):
                        cols = slice(BANK * b, BANK * b + BANK)
                        for w in (ew_hi, ew_lo):
                            pe.matmul(bank(6 + b), actT_hi[:, kk, :], by_row(w, c)[:, row, cols],
                                      start=(kk == 0 and w is ew_hi), stop=False)
                pe.wait_ge(actT_lo_done, i + 1)
                for kk in range(F // P):
                    for b in range(2):
                        ins = pe.matmul(bank(6 + b), actT_lo[:, kk, :],
                                        by_row(ew_hi, 4 + kk // 2)[:, kk % 2, BANK * b:BANK * b + BANK],
                                        start=False, stop=(kk == F // P - 1))
                    if kk % 2:
                        ins.then_inc(chunk_used, 1)

            pe.wait_ge(lg_done, T)
            pe.wait_ge(slots_ready, 1)
            turn_rows(0, 0)
            turn_rows(0, 1)
            with pe.Fori(0, NE) as i:
                tile(i)
            pe.wait_ge(eid_ready, 2)
            with pe.Fori(0, OVER) as o:
                e = pe.value_load(eidi[0:1, 0, bass.ds(o, 1)], min_val=0, max_val=NE)
                with pe.If(e < NE):
                    tile(o + NE)


_INS = ["x", "positions", "norm_mix_g", "w_in", "q_norm_g", "k_norm_g", "lambda_q1", "lambda_k1", "lambda_q2",
        "lambda_k2", "diff_out_norm_g", "sgu_ln_g", "sgu_ln_b", "sgu_w", "sgu_b", "sgu_out_norm_g", "w_out",
        "norm_ffn_g", "router_group_w", "router_group_b", "router_expert_w", "router_expert_b",
        "expert_w_gate", "expert_w_up", "expert_w_down"]


def kernel(**inputs):
    import numpy as _np
    import concourse.bacc as _bacc
    from concourse import mybir as _mybir
    from concourse.bass_utils import run_bass_kernel_spmd as _run

    nc = _bacc.Bacc("TRN2", target_bir_lowering=False, num_devices=1)
    arrays, args = {}, []
    for name in _INS:
        a = _np.ascontiguousarray(inputs[name])
        arrays[f"in_{name}"] = a
        args.append(nc.dram_tensor(f"in_{name}", a.shape, _mybir.dt.from_np(a.dtype), kind="ExternalInput").ap())
    args.append(nc.dram_tensor("out_0", (1, SEQ, D), F32, kind="ExternalOutput").ap())
    build(nc, *args)
    r = _run(nc, [arrays], core_ids=[0])
    return r.results[0]["out_0"]
```

```python
from contextlib import ExitStack

import numpy as np

import concourse.bass as bass
from concourse import mybir

ALU = mybir.AluOpType
ACT = mybir.ActivationFunctionType
AX = mybir.AxisListType
F32 = mybir.dt.float32
F32R = mybir.dt.float32r
BF16 = mybir.dt.bfloat16
I32 = mybir.dt.int32

P = 128
BANK = 512
KB = 1024

D = 1024
SEQ = 1024
T = SEQ // P
KD = D // P
H = 4
DH = 64
QK = 2 * H
ROPE = DH // 4
HALF = ROPE // 2
THETA = 500000.0
G = 4
WB = 512
NB_IN = 5
EPS = 1e-6
LAMBDA_INIT = 0.2
NEG = -1e30

NG, EG = 4, 8
NE = NG * EG
F = 512
OVER = 2 * SEQ // P - 1
NT = NE + OVER + 2
NTHR = SEQ // P - 1
ROUNDS = ((0, 2), (2, 6), (6, OVER))
EMPTY = 1 << 20

SV, SU, Q, K, V = range(5)
COLUMN = {Q: 0, K: 1, V: 2, SU: 3, SV: 4}
STEPS = NB_IN * KD
CHUNKS = 6
AHEAD = 5
CHUNK = 3 * D * F // CHUNKS // P
EARLY = 4
PROBS = 3
RAW, RING = 8, 4


def build(nc, x, positions, norm_mix_g, w_in, q_norm_g, k_norm_g, lambda_q1, lambda_k1, lambda_q2,
          lambda_k2, diff_out_norm_g, sgu_ln_g, sgu_ln_b, sgu_w, sgu_b, sgu_out_norm_g, w_out,
          norm_ffn_g, router_group_w, router_group_b, router_expert_w, router_expert_b,
          expert_w_gate, expert_w_up, expert_w_down, out):
    ctx = ExitStack()
    with ctx:
        hn2_dram = nc.dram_tensor("hn2_rows", [SEQ, D], F32).ap()
        y_dram = nc.dram_tensor("expert_rows", [2 * SEQ, D], F32).ap()

        base = -(-nc.sbuf_base // 64) * 64
        A = base + 31 * KB
        B = A + 64 * KB
        C = B + 80 * KB
        at_const = [base]

        def place(name, shape, dt, offset):
            return nc.alloc_sbuf_tensor_at(name, shape, dt, offset=offset)

        def const(name, shape, dt):
            size = int(np.prod(shape[1:])) * (2 if dt == BF16 else 4)
            t = place(name, shape, dt, at_const[0])
            at_const[0] += -(-size // 32) * 32
            assert at_const[0] <= A, name
            return t

        ident = const("ident", [P, P], F32)
        identb = const("identb", [P, P], BF16)
        causal = const("causal", [P, P], BF16)
        earlier = const("earlier", [P, P], BF16)
        onesb = const("onesb", [P, P], BF16)
        at_gmix = at_const[0]
        gmix = const("gmix", [P, D], F32)
        gffn = const("gffn", [P, D], F32)
        at_ln = at_const[0]
        lng = const("lng", [P, WB], F32)
        lnb = const("lnb", [P, WB], F32)
        gsgu = const("gsgu", [P, WB], F32)
        gatt = const("gatt", [P, P], F32)
        gq = const("gq", [P, DH], F32)
        gk = const("gk", [P, DH], F32)
        lam4 = const("lam4", [P, 4, DH], F32)
        lam = const("lam", [P, 8], F32)
        wsT = const("wsT", [P, G, P], F32)
        bs = const("bs", [P, G], F32)
        router = const("router", [P, KD, NG + NE], F32)
        rbias = const("rbias", [P, NG + NE], F32)
        posi = const("posi", [P, T], I32)
        posf = const("posf", [P, T], F32)
        ang = const("ang", [P, 4, T, HALF], F32)
        cs = const("cs", [P, T, HALF], F32)
        sn = const("sn", [P, T, HALF], F32)
        ss = const("ss", [P, T], F32)
        rs = const("rs", [P, T], F32)
        ss2 = const("ss2", [P, T], F32)
        rs2 = const("rs2", [P, T], F32)
        stat = const("stat", [P, 6], F32)
        mv = const("mv", [P, T, 2], F32)
        lnr = const("lnr", [P, 2], F32)
        half = const("half", [P, QK], F32)
        sums = const("sums", [P, 2, QK], F32)
        inv = const("inv", [P, 2, QK], F32)
        at_sq = at_const[0]
        sq = const("sq", [P, 2, WB], F32)
        rp = const("rp", [P, 4, QK, HALF], F32)
        nmax = const("nmax", [P, 2 * H * T], F32)
        lsum = const("lsum", [P, H * T, 2], F32)
        linv = const("linv", [P, H * T, 2], F32)
        mixc = const("mixc", [P, H * T], F32)

        hn_hi = place("hn_hi", [P, KD, SEQ], F32R, A)
        hn_lo = place("hn_lo", [P, KD, SEQ], F32R, A + 32 * KB)
        qT = place("qT", [P, H, SEQ], F32, A)
        kT = place("kT", [P, H, SEQ], F32, A + 16 * KB)
        att = place("att", [P, T, WB], F32, A + 32 * KB)
        h = place("h", [P, T, D], F32, A)
        hn2 = place("hn2", [P, 2, D], F32, B + 40 * KB)
        sq2 = place("sq2", [P, D], F32, at_gmix)
        hnT2 = place("hnT2", [P, KD, P], F32, at_ln)
        lg = place("lg", [P, T, NG + NE], F32, at_sq)
        actT_hi = place("actT_hi", [P, F // P, P], F32R, A + 36 * KB)
        actT_lo = place("actT_lo", [P, F // P, P], F32R, A + 52 * KB)

        q = place("q", [P, T, WB], F32, B)
        k = place("k", [P, T, WB], F32, B + 16 * KB)
        v = place("v", [P, T, WB], F32, B + 32 * KB)
        sv = place("sv", [P, T, WB], F32, B + 48 * KB)
        su = place("su", [P, T, WB], F32, B + 64 * KB)
        xin = place("xin", [P, T, D], F32, B + 40 * KB)
        xs = place("xs", [P, 2, D], F32, B + 16 * KB)
        sq1 = place("sq1", [P, D], F32, B + 24 * KB)
        wsm = place("wsm", [P, G, P], F32, B + 32 * KB)
        prob = place("prob", [P, PROBS, 2, SEQ], F32, B)
        probT = place("probT", [P, 2, T, P], F32, B + 48 * KB)
        mix_hi = [place(f"mix_hi{i}", [P, KD, P], F32R, B + 16 * (1 - i) * KB) for i in range(2)]
        mix_lo = [place(f"mix_lo{i}", [P, KD, P], F32R, B + (16 * (1 - i) + 4) * KB) for i in range(2)]

        w_raw = place("w_raw", [P, RAW, WB], F32, C)
        w_hi = place("w_hi", [P, RING, WB], F32R, C + 16 * KB)
        w_lo = place("w_lo", [P, RING, WB], F32R, C + 24 * KB)

        wo_raw = place("wo_raw", [P, KD, D], F32, C)
        wo_lo = place("wo_lo", [P, KD, D], F32R, C)
        wo_hi = [place(f"wo_hi{kk}", [P, D], F32R, at + 4 * KB * (kk % n)) for kk, (at, n) in
                 enumerate(4 * [(A + 48 * KB, 4)] + 2 * [(B + 24 * KB, 2)] + 2 * [(B + 56 * KB, 2)])]

        ew_raw = place("ew_raw", [P, CHUNKS, CHUNK], F32, B)
        ew_lo = place("ew_lo", [P, CHUNKS, CHUNK], F32R, B)
        ew_hi = place("ew_hi", [P, CHUNKS, CHUNK], F32R, B + CHUNKS * CHUNK * 4)
        xg = place("xg", [P, D], F32, C + 16 * KB)
        xT_hi = place("xT_hi", [P, KD, P], F32R, C + 20 * KB)
        xT_lo = place("xT_lo", [P, KD, P], F32R, A + 48 * KB)
        y = place("y", [P, D], F32, C + 24 * KB)
        gact = place("gact", [P, F], F32, C + 28 * KB)
        hid = place("hid", [P, F], F32, C + 30 * KB)
        yin = place("yin", [P, T, 2, D], F32, B)

        R = A + 38 * KB
        at_r = [R]

        def scratch(name, shape, dt=F32):
            size = int(np.prod(shape[1:])) * (2 if dt == BF16 else 4)
            t = place(name, shape, dt, at_r[0])
            at_r[0] += -(-size // 32) * 32
            assert at_r[0] <= A + 48 * KB, name
            return t

        r8 = {n: scratch(n, [P, T]) for n in ("gmax", "gsum", "pgrp", "grank", "m1", "r1", "m2", "r2", "dm", "e2",
                                                "den", "gate1", "gate2")}
        gd = scratch("gd", [P, T, NG])
        grk = scratch("grk", [P, T, NG])
        gexp = scratch("gexp", [P, T, NG])
        pen = scratch("pen", [P, T, NG])
        revg = scratch("revg", [P, NG])
        reve = scratch("reve", [P, NE])
        count = scratch("count", [P, P])
        ecol, ocol = count[:, 0:NE], count[:, 0:OVER + 1]
        partition = scratch("partition", [P, 1])
        thr = scratch("thr", [P, NTHR])
        eid = scratch("eid", [P, OVER + 1])
        total = scratch("total", [P, NE])
        nover = scratch("nover", [P, NE])
        cum = scratch("cum", [P, 5, NE])
        offs = scratch("offs", [P, NE])
        place_of = scratch("place_of", [P, 2 * T])
        placei = scratch("placei", [P, 2 * T], I32)
        column = scratch("column", [P, 2 * T])
        row = scratch("row", [P, 2 * T])
        empty = scratch("empty", [P, NT])
        idx1 = scratch("idx1", [P, 1], I32)
        idx2 = scratch("idx2", [P, 1], I32)
        oh1 = scratch("oh1", [P, T, NE])
        oh2 = scratch("oh2", [P, T, NE])
        W0 = C + 16 * KB
        ev = place("ev", [P, T, NE], F32, W0 + 4 * KB)
        rk = place("rk", [P, T, NE], F32, W0 + 5 * KB)
        hot_column = place("hot_column", [P, 2 * T, NT], BF16, W0 + 6 * KB)
        entry = place("entry", [P, NT], F32, W0 + 8 * KB)
        second = place("second", [P, NT], F32, W0 + 9 * KB)
        hot_row = place("hot_row", [P, 2 * T, P], BF16, W0 + 10 * KB)
        cnt = place("cnt", [P, T, NE], BF16, W0 + 14 * KB)
        cmpt = place("cmpt", [P, OVER + 1, NE], F32, A + 58 * KB)
        entries = place("entries", [P, 2 * T, 2, NT], BF16, A + 60 * KB)
        slots = place("slots", [P, NT, 2], I32, A + 56 * KB)
        eidi = place("eidi", [P, 2, OVER + 1], I32, A + 57 * KB)

        PS = [ctx.enter_context(nc.psum_tensor(f"ps{i}", [P, 2 * BANK], F32)) for i in range(4)]

        def bank(i):
            return PS[i // 2][:, BANK * (i % 2):BANK * (i % 2) + BANK]

        def q_bank(t):
            return bank(6 - 2 * (t % 2))

        def k_bank(t):
            return bank(7 - 2 * (t % 2))

        def sem(name):
            return ctx.enter_context(nc.semaphore(name))

        gmix_in, small_in, wo_in = sem("gmix_in"), sem("small_in"), sem("wo_in")
        hx_in = [sem(f"hx_in{t}") for t in range(T)]
        x_in = [sem(f"x_in{t}") for t in range(T)]
        w_in_sem = [sem(f"w_in{i}") for i in range(RAW)]
        dve_step, pool_step = sem("dve_step"), sem("pool_step")
        ws_out = sem("ws_out")
        made, sin_done, lam_exp, ws_masked, ws_turned, rope_arg, lam_dot = (
            sem(n) for n in ("made", "sin_done", "lam_exp", "ws_masked", "ws_turned", "rope_arg", "lam_dot"))
        ss_ready, xs_ready, x_turned, hn_hi_done, hn_lo_done = (
            sem(n) for n in ("ss_ready", "xs_ready", "x_turned", "hn_hi_done", "hn_lo_done"))
        w_hi_done, w_lo_done, w_used, acc_ready, acc_out = (
            sem(n) for n in ("w_hi_done", "w_lo_done", "w_used", "acc_ready", "acc_out"))
        mv_ready, sv_done, sums_done, qk_done, consts_done, rs_ready, rs2_ready, inv_done, scaled = (
            sem(n) for n in ("mv_ready", "sv_done", "sums_done", "qk_done", "consts_done", "rs_ready",
                             "rs2_ready", "inv_done", "scaled"))
        qk_turned, qT_done, kT_done, sg_ready, sg_gated, sg_done = (
            sem(n) for n in ("qk_turned", "qT_done", "kT_done", "sg_ready", "sg_gated", "sg_done"))
        s_ready, max_done, exp_done, a_ready, a_turned, aT_done, o_ready, o_done = (
            sem(n) for n in ("s_ready", "max_done", "exp_done", "a_ready", "a_turned", "aT_done", "o_ready", "o_done"))
        att_done = sem("att_done")
        mix_turned, mix_hi_done, mix_lo_done = sem("mix_turned"), sem("mix_hi_done"), sem("mix_lo_done")
        wo_hi_done, wo_lo_done, mixed = sem("wo_hi_done"), sem("wo_lo_done"), sem("mixed")
        h_ready, ss2_ready, hn2_ready = sem("h_ready"), sem("ss2_ready"), sem("hn2_ready")
        hn2_out = [sem("hn2_out0"), sem("hn2_out1")]
        h_turned, hT_done, logits, lg_done = sem("h_turned"), sem("hT_done"), sem("logits"), sem("lg_done")
        gd_ready, gexp_done, dm_ready, e2_done, cnt_ready, counted, hot_ready, table_ready, slots_ready = (
            sem(n) for n in ("gd_ready", "gexp_done", "dm_ready", "e2_done", "cnt_ready", "counted", "hot_ready",
                             "table_ready", "slots_ready"))
        eid_ready, rtab, zeroed = sem("eid_ready"), sem("rtab"), sem("zeroed")
        ew_in = [sem(f"ew_in{c}") for c in range(CHUNKS)]
        ew_hi_done, ew_lo_done = sem("ew_hi_done"), sem("ew_lo_done")
        rows_in, rows_turned, xT_hi_done, xT_lo_done = sem("rows_in"), sem("rows_turned"), sem("xT_hi_done"), sem("xT_lo_done")
        chunk_used, silu_done, hid_done, hid_turned, actT_hi_done, actT_lo_done = (
            sem(n) for n in ("chunk_used", "silu_done", "hid_done", "hid_turned", "actT_hi_done", "actT_lo_done"))
        ya_done, yb_done, y_out, idx_first, idx1_set, idx2_set, moe_done = (
            sem(n) for n in ("ya_done", "yb_done", "y_out", "idx_first", "idx1_set", "idx2_set", "moe_done"))
        yin_sem = [sem(f"yin{t}") for t in range(T)]
        h1_done, h2_done, out_done = sem("h1_done"), sem("h2_done"), sem("out_done")

        x_t = x[0].rearrange("(t p) d -> t p d", p=P)
        out_t = out[0].rearrange("(t p) d -> t p d", p=P)
        y_t = y_dram.rearrange("(c t p) d -> t p c d", p=P, t=T)
        w_cols = [COLUMN[j] for j in range(NB_IN)]

        def w_slice(s):
            c = w_cols[s // KD]
            return w_in[0, (s % KD) * P:(s % KD + 1) * P, c * WB:(c + 1) * WB]

        def expert_chunk(e, c):
            w = (expert_w_gate, expert_w_up, expert_w_down)[c // 2]
            rows = w.shape[2] // 2
            return w[0, bass.ds(e, 1), (c % 2) * rows:(c % 2 + 1) * rows, :].rearrange("o (k p) n -> p (o k) n", p=P)

        def by_row(ew, c):
            return ew[:, c, :].rearrange("p (k n) -> p k n", n=F if c < 4 else D)

        SMALL = [(lng[:, :], sgu_ln_g.broadcast_to([P, WB])), (lnb[:, :], sgu_ln_b.broadcast_to([P, WB])),
                 (gsgu[:, :], sgu_out_norm_g.rearrange("l g d -> l (g d)").broadcast_to([P, WB])),
                 (gatt[:, :], diff_out_norm_g.broadcast_to([P, P])),
                 (gq[:, :], q_norm_g.broadcast_to([P, DH])), (gk[:, :], k_norm_g.broadcast_to([P, DH])),
                 (lam4[:, 0, :], lambda_q1.broadcast_to([P, DH])), (lam4[:, 1, :], lambda_q2.broadcast_to([P, DH])),
                 (lam4[:, 2, :], lambda_k1.broadcast_to([P, DH])), (lam4[:, 3, :], lambda_k2.broadcast_to([P, DH])),
                 (gffn[:, :], norm_ffn_g.broadcast_to([P, D])),
                 (rbias[:, 0:NG], router_group_b.broadcast_to([P, NG])),
                 (rbias[:, NG:], router_expert_b.broadcast_to([P, NE])),
                 (router[:, :, 0:NG], router_group_w[0].rearrange("(k p) n -> p k n", p=P)),
                 (router[:, :, NG:], router_expert_w[0].rearrange("(k p) n -> p k n", p=P)),
                 (wsm[:, :, :], sgu_w[0].rearrange("g t s -> t g s")),
                 (bs[:, :], sgu_b[0].rearrange("g t -> t g")),
                 (posi[:, :], positions[0].rearrange("(t p) -> p t", p=P))]

        def done_groups(u):
            return sum(-(-(w // H + 1) // 4) for w in range(u + 1))

        def more_tiles(engine, tile, first=0):
            for start, end in ROUNDS:
                e = engine.value_load(eidi[0:1, 0, start:start + 1], min_val=0, max_val=NE)
                with engine.If(e < NE):
                    with engine.Fori(first + start, first + end) as o:
                        e = engine.value_load(eidi[0:1, 0, bass.ds(o - first if first else o, 1)], min_val=0,
                                              max_val=NE)
                        with engine.If(e < NE):
                            tile(o)

        norm_at = {12: (su, 0), 13: (att, 0), 14: (su, 1), 16: (att, 1), 17: (su, 2), 18: (att, 2), 19: (su, 3),
                   20: (su, 4), 21: (att, 3), 22: (su, 5), 23: (su, 6), 24: (su, 7), 25: (att, 4), 27: (att, 5),
                   31: (att, 6), 32: (att, 7)}
        normed = list(norm_at.values())

        block = ctx.enter_context(nc.Block())

        @block.sync
        def _(sp):
            sp.dma_start(gmix[:, :], norm_mix_g.broadcast_to([P, D])).then_inc(gmix_in, 16)
            for t in range(T):
                sp.dma_start(xin[:, t, :], x_t[t]).then_inc(x_in[t], 16)
            for s in range(STEPS):
                if s == RAW:
                    for dst, src in SMALL:
                        sp.dma_start(dst, src, allow_slow_non_contiguous=True).then_inc(small_in, 16)
                if s >= RAW:
                    sp.wait_ge(w_lo_done, s - RAW + 1)
                sp.dma_start(w_raw[:, s % RAW, :], w_slice(s)).then_inc(w_in_sem[s % RAW], 16)
            sp.wait_ge(w_used, STEPS)
            sp.dma_start(wo_raw[:, :, :], w_out[0].rearrange("(k p) n -> p k n", p=P)).then_inc(wo_in, 16)
            sp.wait_ge(s_ready, 2 * H * T)
            for t in range(T):
                sp.dma_start(h[:, t, :], x_t[t]).then_inc(hx_in[t], 16)
            sp.wait_ge(mixed, 2 * T)
            for c in range(CHUNKS):
                if c == CHUNKS - 1:
                    sp.wait_ge(h_turned, T)
                    for b in range(2):
                        sp.wait_ge(hn2_out[b], 16 * T // 2)
                sp.dma_start(by_row(ew_raw, c), expert_chunk(0, c)).then_inc(ew_in[c], 16)
            with sp.Fori(0, NE - 1) as i:
                for c in range(CHUNKS):
                    sp.wait_ge(chunk_used, CHUNKS * i + c + 1)
                    sp.dma_start(by_row(ew_raw, c), expert_chunk(i + 1, c)).then_inc(ew_in[c], 16)
            sp.wait_ge(eid_ready, 2)

            def load_more(o):
                weights = sp.value_load(eidi[0:1, 1, bass.ds(o, 1)], min_val=0, max_val=NE - 1)
                for c in range(CHUNKS):
                    sp.wait_ge(chunk_used, CHUNKS * (NE - 1) + CHUNKS * o + c + 1)
                    sp.dma_start(by_row(ew_raw, c), expert_chunk(weights, c)).then_inc(ew_in[c], 16)

            more_tiles(sp, load_more)
            sp.wait_ge(moe_done, 1)
            for t in range(T):
                sp.dma_start(yin[:, t, :, :], y_t[t]).then_inc(yin_sem[t], 16)
            for t in range(T):
                sp.wait_ge(h2_done, t + 1)
                sp.dma_start(out_t[t], h[:, t, :]).then_inc(out_done, 16)
            sp.wait_ge(out_done, 16 * T)

        @block.gpsimd
        def _(pool):
            steps = [0]

            def link(ins):
                steps[0] += 1
                ins.then_inc(pool_step, 1)
                pool.wait_ge(pool_step, steps[0])

            pool.memset(onesb[:, :], 1.0).then_inc(made, 1)
            link(pool.memset(ident[:, :], 0.0))
            pool.affine_select(out=ident[:, :], in_=ident[:, :], compare_op=ALU.not_equal, fill=1.0, base=0,
                               pattern=[[-1, P]], channel_multiplier=1).then_inc(made, 1)
            link(pool.memset(identb[:, :], 0.0))
            pool.affine_select(out=identb[:, :], in_=identb[:, :], compare_op=ALU.not_equal, fill=1.0, base=0,
                               pattern=[[-1, P]], channel_multiplier=1).then_inc(made, 1)
            link(pool.memset(causal[:, :], 0.0))
            pool.affine_select(out=causal[:, :], in_=causal[:, :], compare_op=ALU.is_ge, fill=NEG, base=0,
                               pattern=[[-1, P]], channel_multiplier=1).then_inc(made, 1)
            link(pool.memset(earlier[:, :], 1.0))
            pool.affine_select(out=earlier[:, :], in_=earlier[:, :], compare_op=ALU.is_gt, fill=0.0, base=0,
                               pattern=[[1, P]], channel_multiplier=-1).then_inc(made, 1)
            link(pool.memset(half[:, :], -0.5))

            def rstd(dst, src, n):
                link(pool.tensor_scalar(dst, src, 1.0 / n, EPS, ALU.mult, ALU.add))
                return pool.tensor_tensor(dst, dst, half[:, 0:dst.shape[1]], ALU.pow)

            for t in range(T):
                pool.wait_ge(ss_ready, t + 1)
                rstd(rs[:, t:t + 1], ss[:, t:t + 1], D).then_inc(rs_ready, 1)
            pool.wait_ge(small_in, 16 * len(SMALL))
            pool.affine_select(out=wsm[:, :, :], in_=wsm[:, :, :], compare_op=ALU.is_ge, fill=0.0, base=0,
                               pattern=[[0, G], [-1, P]], channel_multiplier=1).then_inc(ws_masked, 1)
            pool.tensor_scalar(gq[:, :], gq[:, :], DH ** -0.5, None, ALU.mult).then_inc(consts_done, 1)
            pool.tensor_scalar(gatt[:, :], gatt[:, :], 1.0 - LAMBDA_INIT, None, ALU.mult).then_inc(consts_done, 1)
            pool.wait_ge(consts_done, 2)

            for t in range(T):
                pool.wait_ge(mv_ready, t + 1)
                link(rstd(lnr[:, 0:1], mv[:, t, 1:2], 1))
                link(pool.tensor_tensor(lnr[:, 1:2], mv[:, t, 0:1], lnr[:, 0:1], ALU.mult))
                link(pool.tensor_scalar(lnr[:, 1:2], lnr[:, 1:2], -1.0, None, ALU.mult))
                link(pool.tensor_scalar(sv[:, t, :], sv[:, t, :], lnr[:, 0:1], lnr[:, 1:2], ALU.mult, ALU.add))
                link(pool.tensor_tensor(sv[:, t, :], sv[:, t, :], lng[:, :], ALU.mult))
                pool.tensor_tensor(sv[:, t, :], sv[:, t, :], lnb[:, :], ALU.add).then_inc(sv_done, 1)

            rotated = [0]

            def rotate(n):
                t = n % T
                mt = (q, k)[n // T][:, t, :].rearrange("p (g d) -> p g d", d=DH)
                x1, x2 = mt[:, :, 0:HALF], mt[:, :, HALF:ROPE]
                c = cs[:, t, :].unsqueeze(1).broadcast_to([P, QK, HALF])
                s = sn[:, t, :].unsqueeze(1).broadcast_to([P, QK, HALF])
                pool.wait_ge(scaled, n + 1)
                if n:
                    pool.wait_ge(qk_done, 2 * n)
                for i, (a, b) in enumerate(((x1, c), (x2, s), (x1, s), (x2, c))):
                    steps[0] += 1
                    pool.tensor_tensor(rp[:, i], a, b, ALU.mult).then_inc(pool_step, 1)
                pool.wait_ge(pool_step, steps[0])
                pool.tensor_tensor(x1, rp[:, 0], rp[:, 1], ALU.subtract).then_inc(qk_done, 1)
                pool.tensor_tensor(x2, rp[:, 2], rp[:, 3], ALU.add).then_inc(qk_done, 1)

            pool.wait_ge(sin_done, 2)
            for n in range(2 * T):
                pool.wait_ge(sums_done, n + 1)
                if n >= 2:
                    pool.wait_ge(scaled, n - 1)
                rstd(inv[:, n % 2, :], sums[:, n % 2, :], DH).then_inc(inv_done, 1)
                if n:
                    rotate(n - 1)
            rotate(2 * T - 1)

            for kk in range(KD):
                pool.wait_ge(wo_hi_done, kk + 1)
                pool.tensor_tensor(wo_lo[:, kk, :], wo_raw[:, kk, :], wo_hi[kk][:, :].bitcast(F32), ALU.subtract)\
                    .then_inc(wo_lo_done, 1)

            for i, (m, t) in enumerate(normed):
                mt = m[:, t, :].rearrange("p (g d) -> p g d", d=P)
                r = inv[:, i % 2, 0:H]
                pool.wait_ge(sums_done, 2 * T + H * (i + 1))
                rstd(r, sums[:, i % 2, 0:H], P).then_inc(inv_done, 1)
                pool.wait_ge(inv_done, 2 * T + i + 1)
                link(pool.tensor_tensor(mt, mt, r.unsqueeze(2).broadcast_to([P, H, P]), ALU.mult))
                if m is su:
                    pool.tensor_tensor(su[:, t, :], su[:, t, :], gsgu[:, :], ALU.mult).then_inc(sg_done, 1)
                else:
                    pool.tensor_tensor(mt, mt, gatt[:, :].unsqueeze(1).broadcast_to([P, H, P]), ALU.mult)\
                        .then_inc(att_done, 1)

            for t in range(T):
                pool.wait_ge(ss2_ready, t + 1)
                rstd(rs2[:, t:t + 1], ss2[:, t:t + 1], D).then_inc(rs2_ready, 1)
            pool.wait_ge(mixed, 2 * T)
            pool.iota(revg[:, :], pattern=[[-1, NG]], base=NG, channel_multiplier=0,
                      allow_small_or_imprecise_dtypes=True).then_inc(rtab, 1)
            pool.iota(reve[:, :], pattern=[[-1, NE]], base=NE, channel_multiplier=0,
                      allow_small_or_imprecise_dtypes=True).then_inc(rtab, 1)
            pool.iota(count[:, :], pattern=[[1, P]], base=0, channel_multiplier=0,
                      allow_small_or_imprecise_dtypes=True).then_inc(rtab, 1)
            pool.iota(partition[:, :], pattern=[[0, 1]], base=0, channel_multiplier=1,
                      allow_small_or_imprecise_dtypes=True).then_inc(rtab, 1)
            pool.iota(thr[:, :], pattern=[[P, NTHR]], base=P, channel_multiplier=0,
                      allow_small_or_imprecise_dtypes=True).then_inc(rtab, 1)
            pool.memset(xg[:, :], 0.0).then_inc(zeroed, 1)
            pool.wait_ge(zeroed, 1)
            for c in range(AHEAD):
                pool.wait_ge(ew_hi_done, c + 1)
                pool.tensor_tensor(ew_lo[:, c, :], ew_raw[:, c, :], ew_hi[:, c, :].bitcast(F32), ALU.subtract)\
                    .then_inc(ew_lo_done, 1)
            pool.wait_ge(slots_ready, 1)
            last_token, last_row = pool.to_reg(SEQ - 1), pool.to_reg(2 * SEQ - 1)

            def fetch_rows(i, is_set, times):
                pool.tensor_copy(idx1[:, :], slots[:, bass.ds(i, 1), 0]).then_inc(is_set, 1)
                for b in range(2):
                    pool.wait_ge(hn2_out[b], 16 * T // 2)
                pool.wait_ge(is_set, times)
                pool.indirect_dma_start(
                    out=xg[:, :], out_offset=None, in_=hn2_dram,
                    in_offset=bass.IndirectOffsetOnAxis(ap=idx1[:, 0:1], axis=0),
                    bounds_check=last_token, oob_is_err=False).then_inc(rows_in, 16)

            def tile(n):
                pool.wait_ge(rows_turned, n + 1)
                pool.tensor_copy(idx2[:, :], slots[:, bass.ds(n - 1, 1), 1]).then_inc(idx2_set, 1)
                fetch_rows(n + 1, idx1_set, n)
                pool.wait_ge(slots_ready, 1)
                pool.wait_ge(ya_done, n)
                pool.wait_ge(yb_done, n)
                pool.wait_ge(idx2_set, n)
                pool.indirect_dma_start(
                    out=y_dram, out_offset=bass.IndirectOffsetOnAxis(ap=idx2[:, 0:1], axis=0),
                    in_=y[:, :], in_offset=None,
                    bounds_check=last_row, oob_is_err=False).then_inc(y_out, 16)
                pool.wait_ge(rows_in, 16 * n + 32)
                pool.wait_ge(y_out, 16 * n)

            fetch_rows(0, idx_first, 1)
            pool.wait_ge(rows_turned, 1)
            pool.wait_ge(rows_in, 16)
            fetch_rows(1, idx_first, 2)
            pool.wait_ge(rows_in, 32)
            with pool.Fori(1, NE + 1) as n:
                tile(n)
            pool.wait_ge(eid_ready, 2)
            more_tiles(pool, tile, NE + 1)
            pool.memset(idx2[:, :], 0).then_inc(moe_done, 1)

        @block.scalar
        def _(act):
            def copy(dst, src):
                return nc.scalar.activation(dst, src, ACT.Copy)

            def square_x(t):
                act.wait_ge(x_in[t], 16)
                if t:
                    act.wait_ge(ss_ready, t)
                nc.scalar.activation(sq1[:, :], xin[:, t, :], ACT.Square,
                                     accum_out=ss[:, t:t + 1]).then_inc(ss_ready, 1)

            def split_w(s):
                act.wait_ge(w_in_sem[s % RAW], 16 * (s // RAW + 1))
                if s >= RING:
                    act.wait_ge(w_used, s - RING + 1)
                copy(w_hi[:, s % RING, :], w_raw[:, s % RAW, :]).then_inc(w_hi_done, 1)

            for t in range(3):
                square_x(t)
            for t in range(T):
                if t + 3 < T:
                    square_x(t + 3)
                act.wait_ge(x_turned, t + 1)
                copy(hn_hi[:, :, P * t:P * t + P], PS[2 + t % 2][:, :].rearrange("p (k n) -> p k n", n=P))\
                    .then_inc(hn_hi_done, 1)
                if EARLY - 1 <= t <= EARLY:
                    for s in range(RING // 2):
                        split_w(RING // 2 * (t - EARLY + 1) + s)
            act.wait_ge(rope_arg, 2)
            nc.scalar.activation(sn[:, :, :], ang[:, 2], ACT.Sin).then_inc(sin_done, 1)
            nc.scalar.activation(cs[:, :, :], ang[:, 3], ACT.Sin).then_inc(sin_done, 1)
            act.wait_ge(lam_dot, 1)
            nc.scalar.activation(lam[:, 2:4], lam[:, 0:2], ACT.Exp).then_inc(lam_exp, 1)

            def evacuate(j):
                for t in range(T):
                    if t < T - 1:
                        act.wait_ge(acc_ready, (T - 1) * j + t + 1)
                    else:
                        act.wait_ge(w_used, KD * (j + 1))
                    dst = {SV: sv, SU: su, Q: q, K: k, V: v}[j]
                    nc.scalar.activation(dst[:, t, :], bank(t), ACT.Gelu if j in (SV, SU) else ACT.Copy)\
                        .then_inc(acc_out, 1)

            for s in range(STEPS):
                if s % KD == KD - 1:
                    evacuate(s // KD)
                if s + RING < STEPS:
                    split_w(s + RING)
            for t in range(T):
                act.wait_ge(qk_turned, 2 * t + 1)
                copy(qT[:, :, P * t:P * t + P], q_bank(t).rearrange("p (h n) -> p h n", n=P)).then_inc(qT_done, 1)

            def exponentials(u, m):
                n = u // H + 1
                act.wait_ge(max_done, 2 * u + m + 1)
                if u >= PROBS:
                    act.wait_ge(a_turned, done_groups(u - PROBS))
                nc.scalar.activation(prob[:, u % PROBS, m, 0:P * n], PS[(2 * u + m) % 3][:, 0:P * n], ACT.Exp,
                                     bias=nmax[:, 2 * u + m:2 * u + m + 1],
                                     accum_out=lsum[:, u, m:m + 1]).then_inc(exp_done, 1)

            def turned_out(u, group):
                w = min(4, u // H + 1 - 4 * group)
                act.wait_ge(a_turned, done_groups(u - 1) + group + 1)
                if u >= 2:
                    act.wait_ge(o_ready, u - 1)
                copy(probT[:, u % 2, 4 * group:4 * group + w, :],
                     bank(6)[:, 0:P * w].rearrange("p (k n) -> p k n", n=P)).then_inc(aT_done, 1)

            def sum_squares(i):
                m, t = normed[i]
                if m is su:
                    act.wait_ge(sg_gated, 2 * G if t >= T // 2 else G)
                else:
                    act.wait_ge(o_done, H * (t + 1))
                act.wait_ge(inv_done, max(2 * T, 2 * T + i - 1))
                for g in range(H):
                    nc.scalar.activation(sq[:, i % 2, P * g:P * g + P], m[:, t, P * g:P * g + P], ACT.Square,
                                         accum_out=sums[:, i % 2, g:g + 1]).then_inc(sums_done, 1)

            def upper_mixed(t):
                act.wait_ge(mix_turned, t + 1)
                copy(mix_hi[t % 2][:, :, :], PS[0][:, :].rearrange("p (k n) -> p k n", n=P))\
                    .then_inc(mix_hi_done, 1)

            act.wait_ge(wo_in, 16)
            exponentials(0, 0)
            exponentials(0, 1)
            for u in range(H * T):
                if u + 1 < H * T:
                    exponentials(u + 1, 0)
                else:
                    upper_mixed(0)
                turned_out(u, 0)
                if u + 1 < H * T:
                    exponentials(u + 1, 1)
                if u >= H * T // 2:
                    turned_out(u, 1)
                if u < KD:
                    copy(wo_hi[u][:, :], wo_raw[:, u, :]).then_inc(wo_hi_done, 1)
                if u in norm_at:
                    sum_squares(list(norm_at).index(u))
            sum_squares(2 * T - 1)

            def second_norm(t):
                act.wait_ge(h_ready, 2 * t + 2)
                if t:
                    act.wait_ge(ss2_ready, t)
                nc.scalar.activation(sq2[:, :], h[:, t, :], ACT.Square,
                                     accum_out=ss2[:, t:t + 1]).then_inc(ss2_ready, 1)

            def norm_out(t):
                act.wait_ge(hn2_ready, t + 1)
                act.dma_start(hn2_dram[P * t:P * t + P, :], hn2[:, t % 2, :]).then_inc(hn2_out[t % 2], 16)
                act.wait_ge(h_turned, t + 1)
                if t:
                    act.wait_ge(logits, t)
                copy(hnT2[:, :, :], PS[1][:, :].rearrange("p (k n) -> p k n", n=P)).then_inc(hT_done, 1)

            for t in range(T + 1):
                if t:
                    second_norm(t - 1)
                if t + 1 < T:
                    upper_mixed(t + 1)
                if t:
                    norm_out(t - 1)

            def split_chunks(i, chunks):
                for c in chunks:
                    act.wait_ge(ew_in[c], 16 * i + 16)
                    copy(ew_hi[:, c, :], ew_raw[:, c, :]).then_inc(ew_hi_done, 1)

            def turn_rows(i):
                act.wait_ge(rows_turned, i + 1)
                copy(xT_hi[:, :, :], PS[1][:, :].rearrange("p (k n) -> p k n", n=P)).then_inc(xT_hi_done, 1)

            def tile(i, ahead):
                act.wait_ge(chunk_used, CHUNKS * i + 2)
                nc.scalar.activation(gact[:, :], bank(0), ACT.Silu).then_inc(silu_done, 1)
                split_chunks(i, range(AHEAD, CHUNKS))
                act.wait_ge(hid_turned, i + 1)
                copy(actT_hi[:, :, :], bank(4).rearrange("p (k n) -> p k n", n=P)).then_inc(actT_hi_done, 1)
                turn_rows(i + 1)
                if ahead:
                    split_chunks(i + 1, range(AHEAD - 1))
                act.wait_ge(chunk_used, CHUNKS * i + CHUNKS)
                act.wait_ge(idx2_set, i + 1)
                copy(y[:, 0:BANK], bank(6)).then_inc(ya_done, 1)
                if ahead:
                    split_chunks(i + 1, range(AHEAD - 1, AHEAD))

            act.wait_ge(mixed, 2 * T)
            split_chunks(0, range(AHEAD))
            act.wait_ge(gd_ready, 1)
            nc.scalar.activation(gexp[:, :, :], gd[:, :, :], ACT.Exp).then_inc(gexp_done, 1)
            act.wait_ge(dm_ready, 1)
            nc.scalar.activation(r8["e2"][:, :], r8["dm"][:, :], ACT.Exp).then_inc(e2_done, 1)
            turn_rows(0)
            with act.Fori(0, NE - 1) as i:
                tile(i, True)
            tile(NE - 1, False)
            act.wait_ge(eid_ready, 2)

            def one_more(o):
                split_chunks(o + NE, range(AHEAD))
                tile(o + NE, False)

            more_tiles(act, one_more)

        @block.vector
        def _(dve):
            steps = [0]

            def link(ins):
                steps[0] += 1
                ins.then_inc(dve_step, 1)
                dve.wait_ge(dve_step, steps[0])

            def residual(t, b):
                if b == 0:
                    dve.wait_ge(hx_in[t], 16)
                dve.wait_ge(mixed, 2 * t + b + 1)
                dst = h[:, t, BANK * b:BANK * b + BANK]
                dve.tensor_tensor(dst, bank(4 + b), dst, ALU.add).then_inc(h_ready, 1)

            def take_logits(t):
                dve.wait_ge(logits, t + 1)
                dve.tensor_tensor(lg[:, t, :], bank(6 + t % 2)[:, 0:NG + NE], rbias[:, :], ALU.add).then_inc(lg_done, 1)

            dve.wait_ge(gmix_in, 16)

            def scale_x(t):
                dve.wait_ge(rs_ready, t + 1)
                if t >= 2:
                    dve.wait_ge(x_turned, t - 1)
                dve.scalar_tensor_tensor(out=xs[:, t % 2, :], in0=xin[:, t, :], scalar=rs[:, t:t + 1],
                                         in1=gmix[:, :], op0=ALU.mult, op1=ALU.mult).then_inc(xs_ready, 1)

            def lower(dst, turned, hi, t):
                return dve.tensor_tensor(dst[:, :, P * t:P * t + P],
                                         turned.rearrange("p (k n) -> p k n", n=P),
                                         hi[:, :, P * t:P * t + P].bitcast(F32), ALU.subtract)

            def split_w(s):
                dve.wait_ge(w_hi_done, s + 1)
                dve.tensor_tensor(w_lo[:, s % RING, :], w_raw[:, s % RAW, :], w_hi[:, s % RING, :].bitcast(F32),
                                  ALU.subtract).then_inc(w_lo_done, 1)

            scale_x(0)
            for t in range(T):
                if t + 1 < T:
                    scale_x(t + 1)
                dve.wait_ge(hn_hi_done, t + 1)
                lower(hn_lo, PS[2 + t % 2][:, :], hn_hi, t).then_inc(hn_lo_done, 1)
                if EARLY - 1 <= t <= EARLY:
                    for s in range(RING // 2):
                        split_w(RING // 2 * (t - EARLY + 1) + s)

            dve.wait_ge(small_in, 16 * len(SMALL))
            link(dve.tensor_copy(posf[:, :], posi[:, :]))
            for i in range(HALF):
                link(dve.tensor_scalar(ang[:, 0, :, i], posf[:, :], float(np.float32(THETA ** (-2.0 * i / ROPE))), None,
                                       ALU.mult))
            a0, turns, a2, a3 = (ang[:, i] for i in range(4))
            ROUND = 1.5 * 2.0 ** 23
            T1, T2 = 6.28125, 0.001934051513671875
            T3 = 2 * np.pi - T1 - T2
            link(dve.tensor_scalar(turns, a0, 1 / (2 * np.pi), None, ALU.mult))
            link(dve.tensor_scalar(turns, turns, ROUND, None, ALU.add))
            link(dve.tensor_scalar(turns, turns, ROUND, None, ALU.subtract))
            for c in (T1, T2, float(np.float32(T3))):
                link(dve.scalar_tensor_tensor(out=a0, in0=turns, scalar=-c, in1=a0, op0=ALU.mult, op1=ALU.add))
            LIM = 3.1415925
            dve.tensor_scalar(a2, a0, LIM, -LIM, ALU.min, ALU.max).then_inc(rope_arg, 1)
            link(dve.tensor_scalar(turns, a0, np.pi / 2, None, ALU.is_gt))
            link(dve.tensor_scalar(a3, a0, np.pi / 2, None, ALU.add))
            link(dve.scalar_tensor_tensor(out=a3, in0=turns, scalar=-2 * np.pi, in1=a3, op0=ALU.mult, op1=ALU.add))
            dve.tensor_scalar(a3, a3, LIM, -LIM, ALU.min, ALU.max).then_inc(rope_arg, 1)
            link(dve.tensor_tensor(lam4[:, 0:2, :], lam4[:, 0:2, :], lam4[:, 2:4, :], ALU.mult))
            dve.reduce_sum(lam[:, 0:2], lam4[:, 0:2, :], AX.X).then_inc(lam_dot, 1)
            dve.wait_ge(lam_exp, 1)
            link(dve.tensor_tensor(lam[:, 4:5], lam[:, 3:4], lam[:, 2:3], ALU.subtract))
            link(dve.tensor_scalar(lam[:, 5:6], lam[:, 4:5], -LAMBDA_INIT, None, ALU.add))
            dve.wait_ge(ws_turned, 1)
            dve.tensor_copy(wsT[:, :, :], bank(7).rearrange("p (g n) -> p g n", n=P)).then_inc(ws_out, 1)

            def layer_norm(t):
                dve.wait_ge(acc_out, T * SV + t + 1)
                if t:
                    dve.wait_ge(mv_ready, t)
                link(dve.bn_stats(stat[:, :], sv[:, t, :]))
                dve.bn_aggr(mv[:, t, :], stat[:, :]).then_inc(mv_ready, 1)

            def item(n):
                return (q, k)[n // T][:, n % T, :].rearrange("p (g d) -> p g d", d=DH)

            def norm_sums(n):
                dve.wait_ge(acc_out, T * Q + n + 1)
                if n >= 2:
                    dve.wait_ge(inv_done, n - 1)
                if n:
                    dve.wait_ge(sums_done, n)
                link(dve.tensor_tensor(sq[:, 0, :], item(n), item(n), ALU.mult))
                dve.reduce_sum(sums[:, n % 2, :], sq[:, 0, :].rearrange("p (g d) -> p g d", d=DH), AX.X)\
                    .then_inc(sums_done, 1)

            def scale(n):
                dve.wait_ge(inv_done, n + 1)
                link(dve.tensor_tensor(item(n), item(n), inv[:, n % 2, :].unsqueeze(2).broadcast_to([P, QK, DH]),
                                       ALU.mult))
                dve.tensor_tensor(item(n), item(n), (gq, gk)[n // T][:, :].unsqueeze(1).broadcast_to([P, QK, DH]),
                                  ALU.mult).then_inc(scaled, 1)

            dve.wait_ge(consts_done, 2)
            for s in range(STEPS):
                j, t = s // KD, s % KD
                if s + RING < STEPS:
                    split_w(s + RING)
                if j == SV + 1:
                    layer_norm(t)
                if j > Q:
                    n = s - KD * (Q + 1)
                    norm_sums(n)
                    if n:
                        scale(n - 1)
            scale(2 * T - 1)

            for i in range(2 * G):
                c0, g = T // 2 * (i // G), i % G
                dve.wait_ge(sg_ready, i + 1)
                dst = su[:, c0:c0 + T // 2, P * g:P * g + P]
                dve.scalar_tensor_tensor(out=dst, in0=bank(i % 6).rearrange("p (c d) -> p c d", d=P),
                                         scalar=bs[:, g:g + 1], in1=dst, op0=ALU.add, op1=ALU.mult)\
                    .then_inc(sg_gated, 1)

            for t in range(T):
                dve.wait_ge(qk_turned, 2 * t + 2)
                dve.tensor_copy(kT[:, :, P * t:P * t + P], k_bank(t).rearrange("p (h n) -> p h n", n=P))\
                    .then_inc(kT_done, 1)

            def maximum(u, m):
                n = u // H + 1
                dve.wait_ge(s_ready, 2 * u + m + 1)
                dve.tensor_reduce(nmax[:, 2 * u + m:2 * u + m + 1], PS[(2 * u + m) % 3][:, 0:P * n], AX.X, ALU.max,
                                  negate=True).then_inc(max_done, 1)

            def combine(u):
                n = u // H + 1
                dve.wait_ge(exp_done, 2 * u + 2)
                link(dve.reciprocal(linv[:, u, :], lsum[:, u, :]))
                link(dve.scalar_tensor_tensor(out=mixc[:, u:u + 1], in0=lsum[:, u, 0:1], scalar=lam[:, 5:6],
                                              in1=linv[:, u, 1:2], op0=ALU.mult, op1=ALU.mult))
                dve.scalar_tensor_tensor(out=prob[:, u % PROBS, 0, 0:P * n], in0=prob[:, u % PROBS, 1, 0:P * n],
                                         scalar=mixc[:, u:u + 1], in1=prob[:, u % PROBS, 0, 0:P * n],
                                         op0=ALU.mult, op1=ALU.add).then_inc(a_ready, 1)

            def head_out(u):
                t, hd = u // H, u % H
                dve.wait_ge(o_ready, u + 1)
                dve.tensor_scalar(att[:, t, P * hd:P * hd + P], bank(7)[:, 0:P], linv[:, u, 0:1], None, ALU.mult)\
                    .then_inc(o_done, 1)

            def lower_mixed(t):
                dve.wait_ge(mix_hi_done, t + 1)
                dve.tensor_tensor(mix_lo[t % 2][:, :, :], PS[0][:, :].rearrange("p (k n) -> p k n", n=P),
                                  mix_hi[t % 2][:, :, :].bitcast(F32), ALU.subtract).then_inc(mix_lo_done, 1)

            maximum(0, 0)
            maximum(0, 1)
            maximum(1, 0)
            for u in range(H * T):
                if u + 1 < H * T:
                    maximum(u + 1, 1)
                combine(u)
                if u + 2 < H * T:
                    maximum(u + 2, 0)
                if u == H * T - 1:
                    lower_mixed(0)
                if u >= 2:
                    head_out(u - 2)
            head_out(H * T - 2)
            head_out(H * T - 1)

            def second_norm(t):
                dve.wait_ge(rs2_ready, t + 1)
                if t >= 2:
                    dve.wait_ge(hn2_out[t % 2], 16 * (t // 2))
                    dve.wait_ge(h_turned, t - 1)
                dve.scalar_tensor_tensor(out=hn2[:, t % 2, :], in0=h[:, t, :], scalar=rs2[:, t:t + 1],
                                         in1=gffn[:, :], op0=ALU.mult, op1=ALU.mult).then_inc(hn2_ready, 1)

            for t in range(T + 1):
                if t:
                    residual(t - 1, 1)
                if t + 1 < T:
                    lower_mixed(t + 1)
                if t:
                    second_norm(t - 1)
                if t < T:
                    residual(t, 0)
                if t >= 2:
                    take_logits(t - 2)
            take_logits(T - 1)
            dve.wait_ge(lg_done, T)

            dve.wait_ge(rtab, 5)
            R8 = {n: m[:, :] for n, m in r8.items()}

            def over(m, shape):
                return m.unsqueeze(2).broadcast_to(shape)

            gs, es = [P, T, NG], [P, T, NE]
            link(dve.tensor_reduce(R8["gmax"], lg[:, :, 0:NG], AX.X, ALU.max))
            dve.tensor_tensor(gd[:, :, :], lg[:, :, 0:NG], over(R8["gmax"], gs), ALU.subtract).then_inc(gd_ready, 1)
            dve.wait_ge(gd_ready, 1)
            link(dve.scalar_tensor_tensor(out=grk[:, :, :], in0=gd[:, :, :], scalar=0.0,
                                          in1=revg[:, :].unsqueeze(1).broadcast_to(gs),
                                          op0=ALU.is_equal, op1=ALU.mult))
            link(dve.tensor_reduce(R8["grank"], grk[:, :, :], AX.X, ALU.max))
            link(dve.tensor_tensor(pen[:, :, :], grk[:, :, :], over(R8["grank"], gs), ALU.is_equal))
            link(dve.tensor_scalar(pen[:, :, :], pen[:, :, :], -1.0, -NEG, ALU.add, ALU.mult))
            link(dve.tensor_tensor(ev[:, :, :].rearrange("p t (g e) -> p t g e", e=EG),
                                   lg[:, :, NG:].rearrange("p t (g e) -> p t g e", e=EG),
                                   pen[:, :, :].unsqueeze(3).broadcast_to([P, T, NG, EG]), ALU.add))
            for m, r, oh in (("m1", "r1", oh1), ("m2", "r2", oh2)):
                link(dve.tensor_reduce(R8[m], ev[:, :, :], AX.X, ALU.max))
                link(dve.tensor_tensor(rk[:, :, :], ev[:, :, :], over(R8[m], es), ALU.is_equal))
                link(dve.tensor_tensor(rk[:, :, :], rk[:, :, :], reve[:, :].unsqueeze(1).broadcast_to(es), ALU.mult))
                link(dve.tensor_reduce(R8[r], rk[:, :, :], AX.X, ALU.max))
                link(dve.tensor_tensor(oh[:, :, :], rk[:, :, :], over(R8[r], es), ALU.is_equal))
                if m == "m1":
                    link(dve.scalar_tensor_tensor(out=ev[:, :, :], in0=oh[:, :, :], scalar=4 * NEG, in1=ev[:, :, :],
                                                  op0=ALU.mult, op1=ALU.add))
            dve.tensor_tensor(cnt[:, :, :], oh1[:, :, :], oh2[:, :, :], ALU.add).then_inc(cnt_ready, 1)
            dve.tensor_tensor(R8["dm"], R8["m2"], R8["m1"], ALU.subtract).then_inc(dm_ready, 1)

            dve.wait_ge(counted, 1)
            link(dve.tensor_copy(total[:, :], bank(7)[:, 0:NE]))
            above = cmpt[:, :, :].rearrange("p o e -> p (o e)")[:, 0:NE * NTHR].rearrange("p (e n) -> p e n", n=NTHR)
            link(dve.tensor_tensor(above, total[:, :].unsqueeze(2).broadcast_to([P, NE, NTHR]),
                                   thr[:, :].unsqueeze(1).broadcast_to([P, NE, NTHR]), ALU.is_gt))
            link(dve.reduce_sum(nover[:, :], above, AX.X))
            before, width = nover, 1
            for n in range(int(np.log2(NE))):
                dve.tensor_copy(cum[:, n, 0:width], before[:, 0:width]).then_inc(dve_step, 1)
                steps[0] += 1
                link(dve.tensor_tensor(cum[:, n, width:], before[:, width:], before[:, 0:NE - width], ALU.add))
                before, width = cum[:, n, :], 2 * width
            all_over = before
            link(dve.tensor_tensor(offs[:, :], all_over, nover[:, :], ALU.subtract))
            link(dve.tensor_tensor(offs[:, :], offs[:, :], ecol, ALU.subtract))
            link(dve.tensor_scalar(offs[:, :], offs[:, :], float(NE - 1), float(P), ALU.add, ALU.mult))
            pos = bank(6)[:, 0:T * NE].rearrange("p (t e) -> p t e", e=NE)
            link(dve.scalar_tensor_tensor(out=ev[:, :, :], in0=pos, scalar=float(P),
                                          in1=offs[:, :].unsqueeze(1).broadcast_to(es), op0=ALU.is_ge, op1=ALU.mult))
            link(dve.tensor_tensor(ev[:, :, :], pos, ev[:, :, :], ALU.add))
            link(dve.scalar_tensor_tensor(out=ev[:, :, :], in0=ecol.unsqueeze(1).broadcast_to(es), scalar=float(P),
                                          in1=ev[:, :, :], op0=ALU.mult, op1=ALU.add))
            for c, oh in enumerate((oh1, oh2)):
                link(dve.tensor_tensor(rk[:, :, :], oh[:, :, :], ev[:, :, :], ALU.mult))
                link(dve.reduce_sum(place_of[:, T * c:T * c + T], rk[:, :, :], AX.X))
            link(dve.tensor_copy(placei[:, :], place_of[:, :]))
            link(dve.tensor_scalar(placei[:, :], placei[:, :], 7, None, ALU.arith_shift_right))
            link(dve.tensor_copy(column[:, :], placei[:, :]))
            link(dve.scalar_tensor_tensor(out=row[:, :], in0=column[:, :], scalar=float(-P), in1=place_of[:, :],
                                          op0=ALU.mult, op1=ALU.add))
            all_rows, all_columns = [P, 2 * T, P], [P, 2 * T, NT]
            dve.tensor_tensor(hot_row[:, :, :], row[:, :].unsqueeze(2).broadcast_to(all_rows),
                              count[:, :].unsqueeze(1).broadcast_to(all_rows), ALU.is_equal).then_inc(hot_ready, 1)
            link(dve.tensor_tensor(hot_column[:, :, :], column[:, :].unsqueeze(2).broadcast_to(all_columns),
                                   count[:, 0:NT].unsqueeze(1).broadcast_to(all_columns), ALU.is_equal))
            dve.tensor_tensor(entries[:, :, 0, :], hot_column[:, :, :],
                              count[:, 1:2 * T + 1].unsqueeze(2).broadcast_to(all_columns), ALU.mult)\
                .then_inc(hot_ready, 1)
            dve.tensor_scalar(entries[:, :, 1, :], hot_column[:, :, :], partition[:, 0:1], None, ALU.mult)\
                .then_inc(hot_ready, 1)
            link(dve.tensor_tensor(cmpt[:, :, :], all_over.unsqueeze(1).broadcast_to([P, OVER + 1, NE]),
                                   ocol.unsqueeze(2).broadcast_to([P, OVER + 1, NE]), ALU.is_le))
            link(dve.reduce_sum(eid[:, :], cmpt[:, :, :], AX.X))
            dve.tensor_copy(eidi[:, 0, :], eid[:, :]).then_inc(eid_ready, 1)
            dve.tensor_scalar(eidi[:, 1, :], eid[:, :], float(NE - 1), None, ALU.min).then_inc(eid_ready, 1)
            dve.wait_ge(table_ready, 1)
            link(dve.tensor_scalar(empty[:, :], bank(5)[:, 0:NT], 0.0, float(EMPTY), ALU.is_equal, ALU.mult))
            link(dve.scalar_tensor_tensor(out=entry[:, :], in0=bank(5)[:, 0:NT], scalar=float(P), in1=empty[:, :],
                                          op0=ALU.mult, op1=ALU.add))
            link(dve.scalar_tensor_tensor(out=entry[:, :], in0=entry[:, :], scalar=float(-P),
                                          in1=bank(5)[:, NT:2 * NT], op0=ALU.add, op1=ALU.add))
            link(dve.tensor_scalar(second[:, :], entry[:, :], float(SEQ), float(-SEQ), ALU.is_ge, ALU.mult))
            dve.tensor_copy(slots[:, :, 1], entry[:, :]).then_inc(dve_step, 1)
            steps[0] += 1
            link(dve.tensor_tensor(second[:, :], entry[:, :], second[:, :], ALU.add))
            dve.tensor_copy(slots[:, :, 0], second[:, :]).then_inc(slots_ready, 1)
            dve.wait_ge(gexp_done, 1)
            link(dve.reduce_sum(R8["gsum"], gexp[:, :, :], AX.X))
            dve.wait_ge(e2_done, 1)
            link(dve.tensor_scalar(R8["den"], R8["e2"], 1.0, None, ALU.add))
            link(dve.tensor_tensor(R8["den"], R8["den"], R8["gsum"], ALU.mult))
            link(dve.reciprocal(R8["gate1"], R8["den"]))
            link(dve.tensor_tensor(R8["gate2"], R8["gate1"], R8["e2"], ALU.mult))

            def split_chunks(i, chunks):
                for c in chunks:
                    dve.wait_ge(ew_hi_done, CHUNKS * i + c + 1)
                    dve.tensor_tensor(ew_lo[:, c, :], ew_raw[:, c, :], ew_hi[:, c, :].bitcast(F32), ALU.subtract)\
                        .then_inc(ew_lo_done, 1)

            def turn_rows(i):
                dve.wait_ge(xT_hi_done, i + 1)
                dve.tensor_tensor(xT_lo[:, :, :], PS[1][:, :].rearrange("p (k n) -> p k n", n=P),
                                  xT_hi[:, :, :].bitcast(F32), ALU.subtract).then_inc(xT_lo_done, 1)

            def tile(i, ahead):
                split_chunks(i, range(AHEAD, CHUNKS))
                dve.wait_ge(chunk_used, CHUNKS * i + 4)
                dve.wait_ge(silu_done, i + 1)
                dve.tensor_tensor(hid[:, :], bank(1), gact[:, :], ALU.mult).then_inc(hid_done, 1)
                dve.wait_ge(actT_hi_done, i + 1)
                dve.tensor_tensor(actT_lo[:, :, :], bank(4).rearrange("p (k n) -> p k n", n=P),
                                  actT_hi[:, :, :].bitcast(F32), ALU.subtract).then_inc(actT_lo_done, 1)
                turn_rows(i + 1)
                if ahead:
                    split_chunks(i + 1, range(AHEAD - 1))
                dve.wait_ge(chunk_used, CHUNKS * i + CHUNKS)
                dve.wait_ge(idx2_set, i + 1)
                dve.tensor_copy(y[:, BANK:], bank(7)).then_inc(yb_done, 1)
                if ahead:
                    split_chunks(i + 1, range(AHEAD - 1, AHEAD))

            turn_rows(0)
            with dve.Fori(0, NE - 1) as i:
                tile(i, True)
            tile(NE - 1, False)

            def one_more(o):
                split_chunks(o + NE, range(AHEAD))
                tile(o + NE, False)

            more_tiles(dve, one_more)

            for t in range(T):
                dve.wait_ge(yin_sem[t], 16)
                dve.scalar_tensor_tensor(out=h[:, t, :], in0=yin[:, t, 0, :], scalar=r8["gate1"][:, t:t + 1],
                                         in1=h[:, t, :], op0=ALU.mult, op1=ALU.add).then_inc(h1_done, 1)
                dve.wait_ge(h1_done, t + 1)
                dve.scalar_tensor_tensor(out=h[:, t, :], in0=yin[:, t, 1, :], scalar=r8["gate2"][:, t:t + 1],
                                         in1=h[:, t, :], op0=ALU.mult, op1=ALU.add).then_inc(h2_done, 1)

        @block.tensor
        def _(pe):
            pe.wait_ge(made, 5)

            def turn(dst, src, n=KD):
                for b in range(n):
                    ins = pe.transpose(dst[:, P * b:P * b + P], src[:, P * b:P * b + P], ident[:, :])
                return ins

            def project(s, t):
                j, kk = s // KD, s % KD
                if kk == 0 and j:
                    pe.wait_ge(acc_out, T * (j - 1) + t + 1)
                rows = slice(P * t, P * t + P)
                w = w_hi[:, s % RING, :]
                pe.matmul(bank(t), hn_lo[:, kk, rows], w, start=(kk == 0), stop=False)
                pe.matmul(bank(t), hn_hi[:, kk, rows], w_lo[:, s % RING, :], start=False, stop=False)
                return pe.matmul(bank(t), hn_hi[:, kk, rows], w, start=False, stop=(kk == KD - 1))

            for t in range(T):
                pe.wait_ge(xs_ready, t + 1)
                if t >= 2:
                    pe.wait_ge(hn_lo_done, t - 1)
                turn(PS[2 + t % 2][:, :], xs[:, t % 2, :]).then_inc(x_turned, 1)
                if t >= EARLY:
                    for s in range(RING):
                        pe.wait_ge(w_lo_done, s + 1)
                        project(s, t - EARLY)
            pe.wait_ge(ws_masked, 1)
            pe.wait_ge(hn_lo_done, T)
            for g in range(G):
                ins = pe.transpose(bank(7)[:, P * g:P * g + P], wsm[:, g, :], ident[:, :])
            ins.then_inc(ws_turned, 1)

            for s in range(STEPS):
                pe.wait_ge(w_lo_done, s + 1)
                for t in range(EARLY if s < RING else 0, T):
                    if s == 0 and t == 7:
                        pe.wait_ge(ws_out, 1)
                    ins = project(s, t)
                    if s % KD == KD - 1 and t < T - 1:
                        ins.then_inc(acc_ready, 1)
                ins.then_inc(w_used, 1)

            pe.wait_ge(sv_done, T)
            for i in range(2 * G):
                c0, g = T // 2 * (i // G), i % G
                if i < 6:
                    pe.wait_ge(acc_out, T * (NB_IN - 1) + i + 1)
                else:
                    pe.wait_ge(sg_gated, i - 5)
                pe.matmul(bank(i % 6).rearrange("p (c d) -> p c d", d=P), wsT[:, g, :],
                          sv[:, c0:c0 + T // 2, P * g:P * g + P], start=True, stop=True).then_inc(sg_ready, 1)
            pe.wait_ge(acc_out, NB_IN * T)
            for t in range(T):
                pe.wait_ge(qk_done, 2 * (T + t + 1))
                if t == 1:
                    pe.wait_ge(sg_gated, 6)
                if t >= 2:
                    pe.wait_ge(qT_done, t - 1)
                    pe.wait_ge(kT_done, t - 1)
                turn(q_bank(t), q[:, t, :], H).then_inc(qk_turned, 1)
                turn(k_bank(t), k[:, t, :], H).then_inc(qk_turned, 1)
            pe.wait_ge(qT_done, T)
            pe.wait_ge(kT_done, T)
            pe.wait_ge(sg_gated, 2 * G)

            def scores(u, m):
                t, hd, w = u // H, u % H, 2 * u + m
                n = P * (t + 1)
                if w >= 3:
                    pe.wait_ge(exp_done, w - 2)
                half = slice(DH * m, DH * m + DH)
                for c0 in range(0, n, BANK):
                    c1 = min(n, c0 + BANK)
                    pe.matmul(PS[w % 3][:, c0:c1], qT[half, hd, P * t:P * t + P], kT[half, hd, c0:c1],
                              start=True, stop=(c1 < n))
                pe.matmul(PS[w % 3][:, n - P:n], identb[:, :], causal[:, :], start=False, stop=True)\
                    .then_inc(s_ready, 1)

            def turn_weights(u, group):
                pe.wait_ge(a_ready, u + 1)
                before = done_groups(u - 1) + group
                if before:
                    pe.wait_ge(aT_done, before)
                turn(bank(6), prob[:, u % PROBS, 0, BANK * group:], min(4, u // H + 1 - 4 * group))\
                    .then_inc(a_turned, 1)

            def values(u):
                n, hd = u // H + 1, u % H
                if u:
                    pe.wait_ge(o_done, u)
                pe.wait_ge(aT_done, done_groups(u))
                for b in range(n):
                    ins = pe.matmul(bank(7)[:, 0:P], probT[:, u % 2, b, :], v[:, b, P * hd:P * hd + P],
                                    start=(b == 0), stop=(b == n - 1))
                ins.then_inc(o_ready, 1)

            def product(dst, hi, lo, w_hi, w_lo, first, last):
                pe.matmul(dst, hi, w_hi, start=first, stop=False)
                pe.matmul(dst, hi, w_lo, start=False, stop=False)
                return pe.matmul(dst, lo, w_hi, start=False, stop=last)

            def turn_mixed(t):
                pe.wait_ge(att_done, t + 1)
                pe.wait_ge(sg_done, t + 1)
                if t:
                    pe.wait_ge(mix_lo_done, t)
                turn(PS[0][:, 0:BANK], att[:, t, :], H)
                turn(PS[0][:, BANK:], su[:, t, :], G).then_inc(mix_turned, 1)

            def project_out(t, b):
                pe.wait_ge(mix_lo_done, t + 1)
                if t:
                    pe.wait_ge(h_ready, 2 * t - 1 + b)
                cols = slice(BANK * b, BANK * b + BANK)
                for kk in range(KD):
                    ins = product(bank(4 + b), mix_hi[t % 2][:, kk, :], mix_lo[t % 2][:, kk, :], wo_hi[kk][:, cols],
                                  wo_lo[:, kk, cols], kk == 0, kk == KD - 1)
                ins.then_inc(mixed, 1)

            for u in range(2):
                for m in range(2):
                    scores(u, m)
            for u in range(H * T):
                if u == H * T - 1:
                    pe.wait_ge(exp_done, 2 * H * T)
                    turn_mixed(0)
                for group in range(2):
                    if u + 2 < H * T:
                        scores(u + 2, group)
                    if group <= u // H // 4:
                        turn_weights(u, group)
                if u:
                    values(u - 1)
            pe.wait_ge(wo_lo_done, KD)
            project_out(0, 0)
            values(H * T - 1)

            def turn_normed(t):
                pe.wait_ge(hn2_ready, t + 1)
                if t:
                    pe.wait_ge(hT_done, t)
                turn(PS[1][:, :], hn2[:, t % 2, :]).then_inc(h_turned, 1)

            def router_logits(t):
                pe.wait_ge(hT_done, t + 1)
                if t == 0:
                    pe.wait_ge(o_done, H * T)
                if t >= 2:
                    pe.wait_ge(lg_done, t - 1)
                for b in range(KD):
                    ins = pe.matmul(bank(6 + t % 2)[:, 0:NG + NE], hnT2[:, b, :], router[:, b, :],
                                    start=(b == 0), stop=(b == KD - 1))
                ins.then_inc(logits, 1)

            for t in range(T + 1):
                if t + 1 < T:
                    turn_mixed(t + 1)
                if 0 < t < T:
                    project_out(t, 0)
                if t:
                    turn_normed(t - 1)
                if t < T:
                    project_out(t, 1)
                if t:
                    router_logits(t - 1)
            pe.wait_ge(cnt_ready, 1)
            flat = cnt[:, :, :].rearrange("p t e -> p (t e)")
            pe.matmul(bank(6)[:, 0:T * NE], earlier[:, :], flat, start=True, stop=False)
            for t in range(T):
                if t + 1 < T:
                    later = [P, T - 1 - t, NE]
                    pe.matmul(bank(6)[:, NE * (t + 1):NE * T].rearrange("p (t e) -> p t e", e=NE), onesb[:, :],
                              cnt[:, t:t + 1, :].broadcast_to(later), start=False, stop=(t == T - 2))
                ins = pe.matmul(bank(7)[:, 0:NE], onesb[:, :], cnt[:, t, :], start=(t == 0), stop=(t == T - 1))
            ins.then_inc(counted, 1)
            pe.wait_ge(hot_ready, 3)
            for ct in range(2 * T):
                ins = pe.matmul(bank(5)[:, 0:2 * NT], hot_row[:, ct, :],
                                entries[:, ct, :, :].rearrange("p v n -> p (v n)"), start=(ct == 0),
                                stop=(ct == 2 * T - 1))
            ins.then_inc(table_ready, 1)

            def turn_rows(i, part):
                if part == 0:
                    pe.wait_ge(rows_in, 16 * i + 16)
                cols = slice(BANK * part, BANK * part + BANK)
                ins = turn(PS[1][:, cols], xg[:, cols], KD // 2)
                if part:
                    ins.then_inc(rows_turned, 1)

            def tile(i):
                pe.wait_ge(xT_lo_done, i + 1)
                for side in range(2):
                    for kk in range(KD):
                        c, row = 2 * side + kk // (KD // 2), kk % (KD // 2)
                        if row == 0:
                            pe.wait_ge(ew_lo_done, CHUNKS * i + c + 1)
                        ins = product(bank(side), xT_hi[:, kk, :], xT_lo[:, kk, :], by_row(ew_hi, c)[:, row, :],
                                      by_row(ew_lo, c)[:, row, :], kk == 0, kk == KD - 1)
                        if row == KD // 2 - 1:
                            ins.then_inc(chunk_used, 1)
                turn_rows(i + 1, 0)
                pe.wait_ge(hid_done, i + 1)
                turn(bank(4), hid[:, :], F // P).then_inc(hid_turned, 1)
                turn_rows(i + 1, 1)
                pe.wait_ge(actT_hi_done, i + 1)
                for kk in range(F // P):
                    c, row = 4 + kk // 2, kk % 2
                    if row == 0:
                        pe.wait_ge(ew_lo_done, CHUNKS * i + c + 1)
                    for b in range(2):
                        cols = slice(BANK * b, BANK * b + BANK)
                        for w in (ew_hi, ew_lo):
                            pe.matmul(bank(6 + b), actT_hi[:, kk, :], by_row(w, c)[:, row, cols],
                                      start=(kk == 0 and w is ew_hi), stop=False)
                pe.wait_ge(actT_lo_done, i + 1)
                for kk in range(F // P):
                    for b in range(2):
                        ins = pe.matmul(bank(6 + b), actT_lo[:, kk, :],
                                        by_row(ew_hi, 4 + kk // 2)[:, kk % 2, BANK * b:BANK * b + BANK],
                                        start=False, stop=(kk == F // P - 1))
                    if kk % 2:
                        ins.then_inc(chunk_used, 1)

            pe.wait_ge(lg_done, T)
            pe.wait_ge(slots_ready, 1)
            turn_rows(0, 0)
            turn_rows(0, 1)
            with pe.Fori(0, NE) as i:
                tile(i)
            pe.wait_ge(eid_ready, 2)
            more_tiles(pe, lambda o: tile(o + NE))


_INS = ["x", "positions", "norm_mix_g", "w_in", "q_norm_g", "k_norm_g", "lambda_q1", "lambda_k1", "lambda_q2",
        "lambda_k2", "diff_out_norm_g", "sgu_ln_g", "sgu_ln_b", "sgu_w", "sgu_b", "sgu_out_norm_g", "w_out",
        "norm_ffn_g", "router_group_w", "router_group_b", "router_expert_w", "router_expert_b",
        "expert_w_gate", "expert_w_up", "expert_w_down"]


def kernel(**inputs):
    import numpy as _np
    import concourse.bacc as _bacc
    from concourse import mybir as _mybir
    from concourse.bass_utils import run_bass_kernel_spmd as _run

    nc = _bacc.Bacc("TRN2", target_bir_lowering=False, num_devices=1)
    arrays, args = {}, []
    for name in _INS:
        a = _np.ascontiguousarray(inputs[name])
        arrays[f"in_{name}"] = a
        args.append(nc.dram_tensor(f"in_{name}", a.shape, _mybir.dt.from_np(a.dtype), kind="ExternalInput").ap())
    args.append(nc.dram_tensor("out_0", (1, SEQ, D), F32, kind="ExternalOutput").ap())
    build(nc, *args)
    r = _run(nc, [arrays], core_ids=[0])
    return r.results[0]["out_0"]
```
